# Optimizing a Trainium2 kernel written in Bass

```python
import jax, jax.numpy as jnp
from jax import lax
import numpy as np

D_MODEL = 1024
BATCH = 1
SEQ = 256
DEPTH = 2

CHUNK = 64
Q_BLOCK = 128
MEM_LEN = 256
FFN_HIDDEN = 2048
CONV_CH = 512
CONV_WIDTH = 31
SB_HEADS = 4
SB_HEAD_DIM = 128
MLA_HEADS = 4
MLA_NOPE = 128
MLA_ROPE = 64
MLA_V = 128
MLA_Q_LORA = 256
MLA_KV_LORA = 256
MEM_HEADS = 4
MEM_HEAD_DIM = 128
N_BRANCH = 4
BRANCH_WIDTH = 512
ROPE_BASE = 10000.0
EPS = 1e-6
NEG_INF = -1e30
IN_SPLITS = (2 * CONV_CH, 3 * SB_HEADS * SB_HEAD_DIM, MLA_Q_LORA, MLA_KV_LORA, MLA_ROPE, MEM_HEADS * MEM_HEAD_DIM, N_BRANCH * D_MODEL)
IN_WIDTH = 2 * CONV_CH + 3 * SB_HEADS * SB_HEAD_DIM + MLA_Q_LORA + MLA_KV_LORA + MLA_ROPE + MEM_HEADS * MEM_HEAD_DIM + N_BRANCH * D_MODEL

kernel_name = "hybrid_chunk_causal_encoder_trunk"

def rms_norm(x, g):
    xf = x.astype(jnp.float32)
    y = xf * lax.rsqrt(jnp.mean(xf * xf, axis=-1, keepdims=True) + EPS)
    return (y * g.astype(jnp.float32)).astype(x.dtype)

def layer_norm(x, g, b):
    xf = x.astype(jnp.float32)
    mu = jnp.mean(xf, axis=-1, keepdims=True)
    var = jnp.mean(jnp.square(xf - mu), axis=-1, keepdims=True)
    y = (xf - mu) * lax.rsqrt(var + EPS)
    return (y * g.astype(jnp.float32) + b.astype(jnp.float32)).astype(x.dtype)

def swiglu_ffn(h, w_in, w_out):
    gate, up = jnp.split(h @ w_in, 2, axis=-1)
    return (jax.nn.silu(gate) * up) @ w_out

def rope_tables(positions):
    inv_freq = ROPE_BASE ** (-jnp.arange(0, MLA_ROPE, 2, dtype=jnp.float32) / MLA_ROPE)
    ang = positions.astype(jnp.float32)[..., None] * inv_freq
    return jnp.cos(ang)[:, :, None, :], jnp.sin(ang)[:, :, None, :]

def rope_tail(x, cos, sin):
    x_pass, x_rot = x[..., :-MLA_ROPE], x[..., -MLA_ROPE:]
    x1, x2 = jnp.split(x_rot, 2, axis=-1)
    c, s = cos.astype(x.dtype), sin.astype(x.dtype)
    return jnp.concatenate([x_pass, x1 * c - x2 * s, x2 * c + x1 * s], axis=-1)

def causal_block_sweep(block_fn, q, k, v):
    nb = q.shape[1] // Q_BLOCK
    outs = []
    for i in range(nb):
        lo, hi = i * Q_BLOCK, (i + 1) * Q_BLOCK
        outs.append(block_fn(q[:, lo:hi], k[:, :hi], v[:, :hi], i))
    return jnp.concatenate(outs, axis=1)

def stick_breaking_attention(q, k, v):
    scale = SB_HEAD_DIM ** -0.5
    r = jnp.arange(Q_BLOCK, dtype=jnp.int32)
    later_in_block = (r[:, None] > r[None, :]).astype(jnp.float32)

    def block(qb, kk, vv, i):
        B, Q, H, _ = qb.shape
        L = kk.shape[1]
        nk = L // Q_BLOCK
        q_pos = i * Q_BLOCK + r
        strict = jnp.arange(L, dtype=jnp.int32)[None, :] < q_pos[:, None]
        z = jnp.einsum('bqhd,bkhd->bhqk', qb, kk).astype(jnp.float32) * scale
        log_keep = jnp.where(strict, -jax.nn.softplus(z), 0.0)
        lk = log_keep.reshape(B, H, Q, nk, Q_BLOCK)
        within = jnp.einsum('bhqnk,kj->bhqnj', lk, later_in_block)
        blk = jnp.sum(lk, axis=-1)
        later_blocks = lax.cumsum(blk, axis=3, reverse=True) - blk
        later = (within + later_blocks[..., None]).reshape(B, H, Q, L)
        w = jnp.exp(jnp.where(strict, z + log_keep + later, NEG_INF))
        return jnp.einsum('bhqk,bkhd->bqhd', w.astype(vv.dtype), vv)

    return causal_block_sweep(block, q, k, v)

def chunk_causal_softmax_attention(q, k, v, scale):
    r = jnp.arange(Q_BLOCK, dtype=jnp.int32)

    def block(qb, kk, vv, i):
        L = kk.shape[1]
        q_chunk = (i * Q_BLOCK + r) // CHUNK
        allowed = (jnp.arange(L, dtype=jnp.int32) // CHUNK)[None, :] <= q_chunk[:, None]
        s = jnp.einsum('bqhd,bkhd->bhqk', qb, kk).astype(jnp.float32) * scale
        p = jax.nn.softmax(jnp.where(allowed, s, NEG_INF), axis=-1)
        return jnp.einsum('bhqk,bkhd->bqhd', p.astype(vv.dtype), vv)

    return causal_block_sweep(block, q, k, v)

def conformer_conv_branch(u, dw, b, ln_g, ln_b):
    a, g = jnp.split(u, 2, axis=-1)
    y = a * jax.nn.sigmoid(g)
    y = lax.conv_general_dilated(
        y, dw[:, None, :].astype(y.dtype), window_strides=(1,),
        padding=[(CONV_WIDTH - 1, 0)], dimension_numbers=('NWC', 'WIO', 'NWC'),
        feature_group_count=CONV_CH) + b
    return jax.nn.silu(layer_norm(y, ln_g, ln_b))

def stick_breaking_branch(qkv, q_hnorm, k_hnorm):
    B, S = qkv.shape[:2]
    qkv = qkv.reshape(B, S, 3, SB_HEADS, SB_HEAD_DIM)
    q = rms_norm(qkv[:, :, 0], q_hnorm)
    k = rms_norm(qkv[:, :, 1], k_hnorm)
    o = stick_breaking_attention(q, k, qkv[:, :, 2])
    return o.reshape(B, S, SB_HEADS * SB_HEAD_DIM)

def mla_branch(q_lat, kv_lat, k_rope, cos, sin, q_norm, w_uq, kv_norm, w_ukv, q_hnorm, k_hnorm):
    B, S = q_lat.shape[:2]
    q = (rms_norm(q_lat, q_norm) @ w_uq).reshape(B, S, MLA_HEADS, MLA_NOPE + MLA_ROPE)
    kv = (rms_norm(kv_lat, kv_norm) @ w_ukv).reshape(B, S, MLA_HEADS, MLA_NOPE + MLA_V)
    k_nope, v = kv[..., :MLA_NOPE], kv[..., MLA_NOPE:]
    k_r = jnp.broadcast_to(k_rope[:, :, None, :], (B, S, MLA_HEADS, MLA_ROPE))
    k = jnp.concatenate([k_nope, k_r], axis=-1)
    q = rope_tail(rms_norm(q, q_hnorm), cos, sin)
    k = rope_tail(rms_norm(k, k_hnorm), cos, sin)
    o = chunk_causal_softmax_attention(q, k, v, (MLA_NOPE + MLA_ROPE) ** -0.5)
    return o.reshape(B, S, MLA_HEADS * MLA_V)

def memory_branch(q_raw, mem, mem_norm, w_kv, q_hnorm, k_hnorm):
    B, S = q_raw.shape[:2]
    M = mem.shape[1]
    q = rms_norm(q_raw.reshape(B, S, MEM_HEADS, MEM_HEAD_DIM), q_hnorm)
    kv = (rms_norm(mem, mem_norm) @ w_kv).reshape(B, M, 2, MEM_HEADS, MEM_HEAD_DIM)
    k = rms_norm(kv[:, :, 0], k_hnorm)
    v = kv[:, :, 1]
    s = jnp.einsum('bshd,bmhd->bhsm', q, k).astype(jnp.float32) * (MEM_HEAD_DIM ** -0.5)
    p = jax.nn.softmax(s, axis=-1).astype(v.dtype)
    o = jnp.einsum('bhsm,bmhd->bshd', p, v)
    return o.reshape(B, S, MEM_HEADS * MEM_HEAD_DIM)

def setup_inputs(seed: int = 0) -> dict:
    key = jax.random.key(seed)
    ks = jax.random.split(key, 32)
    L, D, F = DEPTH, D_MODEL, FFN_HIDDEN

    def w(k, shape, fan_in):
        return jax.random.normal(k, shape, jnp.float32) * (fan_in ** -0.5)

    def gain(k, shape):
        return 1.0 + 0.02 * jax.random.normal(k, shape, jnp.float32)

    offsets = jax.random.randint(ks[2], (BATCH, 1), 0, 4096, dtype=jnp.int32)
    positions = offsets + jnp.arange(SEQ, dtype=jnp.int32)[None, :]
    return {
        "x": jax.random.normal(ks[0], (BATCH, SEQ, D), jnp.float32),
        "mem": jax.random.normal(ks[1], (BATCH, MEM_LEN, D), jnp.float32),
        "positions": positions,
        "ffn1_norm": gain(ks[3], (L, D)),
        "ffn1_w_in": w(ks[4], (L, D, 2 * F), D),
        "ffn1_w_out": w(ks[5], (L, F, D), F),
        "mix_norm": gain(ks[6], (L, D)),
        "w_in": w(ks[7], (L, D, IN_WIDTH), D),
        "conv_dw": w(ks[8], (L, CONV_WIDTH, CONV_CH), CONV_WIDTH),
        "conv_b": 0.02 * jax.random.normal(ks[9], (L, CONV_CH), jnp.float32),
        "conv_ln_g": gain(ks[10], (L, CONV_CH)),
        "conv_ln_b": 0.02 * jax.random.normal(ks[11], (L, CONV_CH), jnp.float32),
        "sb_q_hnorm": gain(ks[12], (L, SB_HEAD_DIM)),
        "sb_k_hnorm": gain(ks[13], (L, SB_HEAD_DIM)),
        "mla_q_norm": gain(ks[14], (L, MLA_Q_LORA)),
        "mla_w_uq": w(ks[15], (L, MLA_Q_LORA, MLA_HEADS * (MLA_NOPE + MLA_ROPE)), MLA_Q_LORA),
        "mla_kv_norm": gain(ks[16], (L, MLA_KV_LORA)),
        "mla_w_ukv": w(ks[17], (L, MLA_KV_LORA, MLA_HEADS * (MLA_NOPE + MLA_V)), MLA_KV_LORA),
        "mla_q_hnorm": gain(ks[18], (L, MLA_NOPE + MLA_ROPE)),
        "mla_k_hnorm": gain(ks[19], (L, MLA_NOPE + MLA_ROPE)),
        "mem_norm": gain(ks[20], (L, D)),
        "mem_w_kv": w(ks[21], (L, D, 2 * MEM_HEADS * MEM_HEAD_DIM), D),
        "mem_q_hnorm": gain(ks[22], (L, MEM_HEAD_DIM)),
        "mem_k_hnorm": gain(ks[23], (L, MEM_HEAD_DIM)),
        "w_branch": w(ks[24], (L, N_BRANCH, BRANCH_WIDTH, D), BRANCH_WIDTH),
        "w_out": w(ks[25], (L, D, D), D),
        "ffn2_norm": gain(ks[26], (L, D)),
        "ffn2_w_in": w(ks[27], (L, D, 2 * F), D),
        "ffn2_w_out": w(ks[28], (L, F, D), F),
    }

def reference(x, mem, positions, ffn1_norm, ffn1_w_in, ffn1_w_out, mix_norm, w_in,
              conv_dw, conv_b, conv_ln_g, conv_ln_b, sb_q_hnorm, sb_k_hnorm,
              mla_q_norm, mla_w_uq, mla_kv_norm, mla_w_ukv, mla_q_hnorm, mla_k_hnorm,
              mem_norm, mem_w_kv, mem_q_hnorm, mem_k_hnorm, w_branch, w_out,
              ffn2_norm, ffn2_w_in, ffn2_w_out):
    B, S, D = x.shape
    cos, sin = rope_tables(positions)
    split_at = np.cumsum(IN_SPLITS)[:-1].tolist()
    for l in range(DEPTH):
        x = x + 0.5 * swiglu_ffn(rms_norm(x, ffn1_norm[l]), ffn1_w_in[l], ffn1_w_out[l])
        h = rms_norm(x, mix_norm[l])
        u = h @ w_in[l]
        conv_u, sb_qkv, q_lat, kv_lat, k_rope, mem_q, gate_logits = jnp.split(u, split_at, axis=-1)
        branches = (
            conformer_conv_branch(conv_u, conv_dw[l], conv_b[l], conv_ln_g[l], conv_ln_b[l]),
            stick_breaking_branch(sb_qkv, sb_q_hnorm[l], sb_k_hnorm[l]),
            mla_branch(q_lat, kv_lat, k_rope, cos, sin, mla_q_norm[l], mla_w_uq[l],
                       mla_kv_norm[l], mla_w_ukv[l], mla_q_hnorm[l], mla_k_hnorm[l]),
            memory_branch(mem_q, mem, mem_norm[l], mem_w_kv[l], mem_q_hnorm[l], mem_k_hnorm[l]),
        )
        gates = jax.nn.sigmoid(gate_logits).reshape(B, S, N_BRANCH, D)
        merged = gates[:, :, 0, :] * (branches[0] @ w_branch[l, 0])
        for i in range(1, N_BRANCH):
            merged = merged + gates[:, :, i, :] * (branches[i] @ w_branch[l, i])
        x = x + merged @ w_out[l]
        x = x + 0.5 * swiglu_ffn(rms_norm(x, ffn2_norm[l]), ffn2_w_in[l], ffn2_w_out[l])
    return x


_drawn_inputs = setup_inputs


def setup_inputs(seed=0):
    import zlib

    import numpy as np

    out = dict(_drawn_inputs(seed))
    spreads = {}
    factors = {'ffn1_norm': 4.814,
     'mix_norm': 3.664,
     'conv_b': 3.119,
     'conv_ln_g': 5.948,
     'conv_ln_b': 6.533,
     'sb_q_hnorm': 8.0,
     'sb_k_hnorm': 8.0,
     'mla_q_norm': 8.0,
     'mla_kv_norm': 8.0,
     'mla_q_hnorm': 8.0,
     'mla_k_hnorm': 8.0,
     'mem_norm': 8.0,
     'mem_q_hnorm': 8.0,
     'mem_k_hnorm': 8.0,
     'ffn2_norm': 5.727}
    for name, (base, spread) in spreads.items():
        noise = np.random.default_rng([zlib.crc32(name.encode()), seed]).standard_normal(out[name].shape)
        drawn = base * np.exp(spread * noise) if base else spread * noise
        out[name] = __import__('jax').numpy.asarray(drawn.astype(out[name].dtype))
    for name, factor in factors.items():
        out[name] = (out[name] * factor).astype(out[name].dtype)
    return out
```

```python
import numpy as np

import concourse.bass as bass
from concourse import mybir
from contextlib import ExitStack

D_MODEL, SEQ, DEPTH, MEM_LEN = 1024, 256, 2, 256
FFN, CONV_CH, TAPS, HEADS, HEAD_DIM = 2048, 512, 31, 4, 128
LORA, ROPE, CHUNK, N_BRANCH, EPS = 256, 64, 64, 4, 1e-6
ROPE_BASE = 10000.0
P = 128
T = SEQ
KB = D_MODEL // P
PAD = TAPS - 1

BLK = 1024
RING = 4
AHEAD = 3
B_F1 = 0
B_F2 = B_F1 + 32
B_MEM = B_F2 + 16
B_CONV = B_MEM + 8
B_SBQ = B_CONV + 8
B_SBV = B_SBQ + 8
B_LAT = B_SBV + 4
B_MEMQ = B_LAT + 4
B_UP = B_MEMQ + 4
B_GATE = B_UP + 4
B_BRANCH = B_GATE + 32
B_OUT = B_BRANCH + 16
B_G1 = B_OUT + 8
B_G2 = B_G1 + 32
NBLK = B_G2 + 16
assert NBLK % RING == 0 and NBLK == 192

O_F1 = 0
O_F2 = O_F1 + 16
O_MEM = O_F2 + 4
O_CONV = O_MEM + 4
O_SBQ = O_CONV + 4
O_SBV = O_SBQ + 4
O_LAT = O_SBV + 2
O_MEMQ = O_LAT + 2
O_UP = O_MEMQ + 2
O_GATE = O_UP + 4
O_BRANCH = O_GATE + 16
O_OUT = O_BRANCH + 8
O_G1 = O_OUT + 4
O_G2 = O_G1 + 16
NOUT = O_G2 + 4
assert NOUT % 2 == 0

C_FFN1, C_MIX, C_FFN2, C_MEM = 0, KB, 2 * KB, 3 * KB
C_CONV = 4 * KB
CONVW = TAPS + 1
C_LNG = C_CONV + 4 * CONVW
C_LNB = C_LNG + 4
C_SBQ = C_LNB + 4
C_SBK = C_SBQ + 1
C_QLAT = C_SBK + 1
C_KVLAT = C_QLAT + 2
C_MQN, C_MQR, C_MKN, C_MKR = C_KVLAT + 2, C_KVLAT + 3, C_KVLAT + 4, C_KVLAT + 5
C_EQ, C_EK = C_KVLAT + 6, C_KVLAT + 7
NPAR = C_EK + 1

K_ONES, K_HALF, K_LATER, K_IDENT, K_STRICT, K_PA, K_PB = (P * i for i in range(7))
K_EPS, K_ONE, K_FREQ, K_QC, K_QS, K_KS = (7 * P + i for i in range(6))
NCONST = 7 * P + 6
ROUNDER = 1.5 * 2.0 ** 23


def build(nc, stream, xT, memT, positions, params, consts, outT):
    F32, F32R, I32 = mybir.dt.float32, mybir.dt.float32r, mybir.dt.int32
    ALU, ACT, AX = mybir.AluOpType, mybir.ActivationFunctionType, mybir.AxisListType
    SB_SCALE = float(HEAD_DIM) ** -0.5
    MLA_SCALE = float(HEAD_DIM + ROPE) ** -0.5
    TOTAL = DEPTH * NBLK + AHEAD
    BANK_SB, BANK_MLA, BANK_MEM, BANK_NORM = 4, 5, 6, 7

    ctx = ExitStack()
    with ctx:
        def sb(name, shape, dt=F32):
            return ctx.enter_context(nc.sbuf_tensor(name, shape, dt))

        def over(name, shape, dt=F32):
            with nc.sbuf_tensor(name, shape, dt) as t:
                return t

        def sem(name):
            return ctx.enter_context(nc.semaphore(name))

        raw = sb("raw", [P, RING, BLK])
        whi = sb("whi", [P, RING, BLK], F32R)
        wlo = sb("wlo", [P, RING, BLK], F32R)
        x = sb("x", [P, KB, T])
        hhi = sb("hhi", [P, KB, T], F32R)
        hlo = sb("hlo", [P, KB, T], F32R)
        hf = sb("hf", [P, KB, T])
        gates = over("gates", [P, N_BRANCH, KB, T])
        acthi = sb("acthi", [P, 2 * KB, T], F32R)
        actlo = sb("actlo", [P, 2 * KB, T], F32R)
        ypad = over("ypad", [P, 4, PAD + T])
        b0hi, b0lo = sb("b0hi", [P, 4, T], F32R), sb("b0lo", [P, 4, T], F32R)
        b1hi, b1lo = sb("b1hi", [P, 4, T], F32R), sb("b1lo", [P, 4, T], F32R)
        mlaqk = over("mlaqk", [P, 3, 4, T])
        b2hi, b2lo = sb("b2hi", [P, 4, T], F32R), sb("b2lo", [P, 4, T], F32R)
        sb("knope_room", [P, 4, T])
        memq = over("memq", [P, 4, T])
        b3hi, b3lo = sb("b3hi", [P, 4, T], F32R), sb("b3lo", [P, 4, T], F32R)
        bhi, blo = [b0hi, b1hi, b2hi, b3hi], [b0lo, b1lo, b2lo, b3lo]
        lathi, latlo = b1hi, b1lo
        vall = sb("vall", [P, 6, 4 * HEAD_DIM])
        memk = sb("memk", [P, 4, T])
        krsq, krot, qtab = sb("krsq", [P, T]), sb("krot", [P, T]), sb("qtab", [P, T])
        cosT, sinK, ropeQ = sb("cosT", [P, T]), sb("sinK", [P, T]), sb("ropeQ", [P, T])
        con = sb("con", [P, NCONST])
        par = sb("par", [P, NPAR])
        stat = sb("stat", [P, 16])
        work = sb("work", [P, 6144])
        PS = ctx.enter_context(nc.psum_tensor("PS", [P, 8, 512], F32))

        ones, halves, later = con[:, K_ONES:K_ONES + P], con[:, K_HALF:K_HALF + P], con[:, K_LATER:K_LATER + P]
        ident = con[:, K_IDENT:K_IDENT + P]
        strict2 = con[:, K_STRICT:K_STRICT + P].rearrange("p (a n) -> p a n", a=1).broadcast_to([P, 2, P])
        permA, permB = con[:, K_PA:K_PA + P], con[:, K_PB:K_PB + P]
        eps, one = con[:, K_EPS:K_EPS + 1], con[:, K_ONE:K_ONE + 1]

        def rows(ap, n):
            return ap.rearrange("p (a n) -> p a n", a=n)

        def f(ap):
            return ap.bitcast(F32)

        def wide(t):
            return t[:, 0:KB, :].rearrange("p k n -> p (k n)").rearrange("p (r a n) -> p r a n", a=2, n=ROPE)

        def runs(ap):
            return ap.rearrange("p (r a n) -> p r a n", a=1, n=ROPE).broadcast_to([P, BLK // ROPE, 2, ROPE])

        def w2(a):
            return rows(work[:, a:a + 2 * T], 2)

        silu, act32 = [w2(0), w2(512)], [w2(1024), w2(1536)]
        mem32, memr, xr = rows(work[:, 2048:4096], KB), work[:, 4096:4352], work[:, 4352:4608]
        memksq, memkr = work[:, 0:1024], work[:, 1024:2048]
        lat32, latsq, latr = work[:, 0:1024], work[:, 1024:2048], work[:, 2048:2560]
        glu = [w2(2560), w2(3072)]
        krg, krt = work[:, 3584:3840], w2(3840)
        sbr, sbL, sbq, sbk = work[:, 0:512], work[:, 0:384], work[:, 512:768], work[:, 768:1024]
        lk, lw = work[:, 1024:1408], work[:, 1408:1792]
        msq, mr = work[:, 1792:2560], work[:, 1792:2304]
        mP, mPT = work[:, 1792:2176], work[:, 2176:2560]
        mq, mqr, mk, mkr = (work[:, 2560 + T * i:2560 + T * (i + 1)] for i in range(4))
        er, eP, ePT, eq = work[:, 3584:3840], work[:, 3584:4096], work[:, 4096:4608], work[:, 4608:4864]
        vh = rows(work[:, 4864:5632], 6)
        acc = [work[:, 5632:5888], work[:, 5888:6144]]
        yc, ysq, yr, y32 = work[:, 0:1024], work[:, 1024:2048], work[:, 2048:2304], work[:, 2304:3328]
        prod = [w2(3328), w2(3840)]

        names = """act_waited dve_waited pe_waited x_loaded par_loaded mem_loaded const_loaded pos_loaded out_stored
            hi_ready lo_ready block_done rope_step
            x_sq ssq_ready rms_ln rms_ready hf_ready hhi_ready hlo_ready acthi_ready actlo_ready
            mem_sq mem_ssq mem_ln mem_r memh_ready memhi_ready memlo_ready
            memk_sq memk_ssq memk_ln memk_r memk_ready pad_zeroed glu_ready
            lat_sq lat_ssq lat_ln lat_r lat_normed lathi_ready latlo_ready
            widehi_ready widelo_ready kr_ready krsq_ready krg_ready kr_permuted krt_ready krot_ready qtab_ready
            sb_sq mla_sq e_sq vh_ready sb_ssq mla_ssq e_ssq sb_ln sb_r mla_ln mla_r e_ln e_r
            sb_normed mqr_tabled mla_normed e_normed sb_z mla_s e_s
            sb_abs sb_exp sb_L sb_m sb_lk sb_a sb_lkm sb_later sb_logw sb_expw sb_w sb_pv sb_hi sb_lo
            mla_masked mla_max mla_neg mla_p mla_rec mla_pn mla_transposed mla_PT mla_pv mla_hi mla_lo
            e_max e_neg e_p e_rec e_pn e_transposed e_PT e_pv e_hi e_lo
            conv_tap ln_mean ln_c ln_sq ln_var ln_ln ln_r ln_n ln_silu b0hi_ready b0lo_ready
            gate_sig prod_ready merged_ready mergedhi_ready mergedlo_ready""".split()
        S = {n: sem(n) for n in names}
        raw_ready = [sem(f"raw_ready{i}") for i in range(RING)]
        read = [sem(f"group_read{i}") for i in range(2)]
        HALF_OUT = NOUT // 2

        def read_value(o, half_base):
            return half_base + (o // 2 + 2)

        def diag2(ap):
            return ap.rearrange("p (a n) -> p a n", n=P)[:, 0:3:2, :]

        block = ctx.enter_context(nc.Block())

        @block.sync
        def _(sp):
            sp.dma_start(con[:, :], consts).then_inc(S["const_loaded"], 16)
            sp.dma_start(x[:, :, :], xT.rearrange("(k p) t -> p k t", p=P)).then_inc(S["x_loaded"], 16)
            for b in range(RING):
                sp.dma_start(raw[:, b, :], stream[b, :, :]).then_inc(raw_ready[b], 16)
            with sp.Fori(0, DEPTH * NBLK - RING, RING) as i:
                for k in range(RING):
                    sp.wait_ge(S["lo_ready"], i + (k + 1))
                    sp.dma_start(raw[:, k, :], stream[bass.ds(i + (k + RING), 1), :, :]
                                 .rearrange("a p n -> p (a n)")).then_inc(raw_ready[k], 16)
            for b in range(DEPTH * NBLK, TOTAL):
                sp.wait_ge(S["lo_ready"], b - RING + 1)
                sp.dma_start(raw[:, b % RING, :], stream[b, :, :]).then_inc(raw_ready[b % RING], 16)
            for o in (O_G2 + 2, O_G2 + 3):
                sp.wait_ge(read[o % 2], read_value(o, (DEPTH - 1) * HALF_OUT))
            sp.wait_ge(S["x_sq"], 4 + 12 * DEPTH)
            sp.dma_start(outT.rearrange("(k p) t -> p k t", p=P), x[:, :, :]).then_inc(S["out_stored"], 16)
            sp.wait_ge(S["out_stored"], 16)

        @block.gpsimd
        def _(pool):
            pool.dma_start(ropeQ[:, :].bitcast(I32), positions.broadcast_to([P, T])).then_inc(S["pos_loaded"], 16)
            with pool.Fori(0, DEPTH) as l:
                pool.dma_start(par[:, :], params[bass.ds(l, 1), :, :].rearrange("a p n -> p (a n)"))\
                    .then_inc(S["par_loaded"], 16)
                pool.dma_start(mem32, memT.rearrange("(k p) t -> p k t", p=P)).then_inc(S["mem_loaded"], 16)
                pool.wait_ge(S["hlo_ready"], l * (3 * KB) + 3 * KB)

        @block.scalar
        def _(act):
            A = nc.scalar.activation

            def level():
                act.sem_inc(S["act_waited"], 1)

            def hi(base, b):
                b += AHEAD
                act.wait_ge(raw_ready[b % RING], base * (16 // RING) + 16 * (b // RING + 1))
                act.wait_ge(S["block_done"], base + (b + 1))
                A(whi[:, b % RING, :], raw[:, b % RING, :], ACT.Copy).then_inc(S["hi_ready"], 1)

            def group(o, base, b):
                act.wait_ge(S["block_done"], base + (b + 1 + RING))
                return 2 * (o % 2)

            def root(sums, dst, n, s_sum, v, s_ln, s_r):
                act.wait_ge(S[s_sum], v)
                A(dst, sums, ACT.Ln, bias=eps, scale=1.0 / n).then_inc(S[s_ln], 1)
                act.wait_ge(S[s_ln], v)
                A(dst, dst, ACT.Exp, scale=-0.5).then_inc(S[s_r], 1)

            def norm(l, m):
                root(PS[:, BANK_NORM, 0:T], xr, D_MODEL, "ssq_ready", l * 3 + (m + 1), "rms_ln", "rms_ready")
                for k in range(KB):
                    act.wait_ge(S["hf_ready"], l * (3 * KB) + (m * KB + k + 1))
                    A(hhi[:, k, :], hf[:, k, :], ACT.Copy).then_inc(S["hhi_ready"], 1)

            def ffn_in(l, b0, o0, f0):
                with act.Fori(0, 4) as it:
                    base, hb = act.snap(l * NBLK + it * 8), act.snap(l * HALF_OUT + it * 2)
                    for j in range(2):
                        hi(base, b0 + 4 * j)
                        hi(base, b0 + 4 * j + 1)
                        o = o0 + 2 * j
                        q = group(o, base, b0 + 4 * j + 1)
                        A(silu[j], PS[:, q:q + 2, 0:T], ACT.Silu).then_inc(read[0], 1)
                        hi(base, b0 + 4 * j + 2)
                        hi(base, b0 + 4 * j + 3)
                        act.wait_ge(read[1], read_value(o + 1, hb))
                        level()
                        A(acthi[:, bass.ds(it * 4 + 2 * j, 2), :], act32[j], ACT.Copy)\
                            .then_inc(S["acthi_ready"], 1)

            def ffn_out(l, b0, o0):
                with act.Fori(0, 2) as it:
                    base, hb = act.snap(l * NBLK + it * 8), act.snap(l * HALF_OUT + it)
                    for j in range(2):
                        for k in range(4):
                            hi(base, b0 + 4 * j + k)
                        act.wait_ge(read[(o0 + j) % 2], read_value(o0 + j, hb))
                        at = bass.ds(it * 4 + 2 * j, 2)
                        level()
                        A(hf[:, at, :], x[:, at, :], ACT.Square).then_inc(S["x_sq"], 1)

            act.sem_inc(read[0], 1)
            act.sem_inc(read[1], 1)
            act.wait_ge(S["rope_step"], 9)
            A(sinK[:, :], krsq[:, :], ACT.Sin).then_inc(S["rope_step"], 1)
            A(cosT[:, :], krot[:, :], ACT.Sin).then_inc(S["rope_step"], 1)
            act.wait_ge(S["x_loaded"], 16)
            for c in range(4):
                A(hf[:, 2 * c:2 * c + 2, :], x[:, 2 * c:2 * c + 2, :], ACT.Square).then_inc(S["x_sq"], 1)
            act.wait_ge(S["const_loaded"], 16)
            for b in range(-AHEAD, 0):
                hi(0, b)
            with act.Fori(0, DEPTH) as l:
                lb, lh = act.snap(l * NBLK), act.snap(l * HALF_OUT)
                l1 = act.snap(l + 1)
                act.wait_ge(S["par_loaded"], l * 16 + 16)
                norm(l, 0)
                act.wait_ge(S["mem_loaded"], l * 16 + 16)
                act.wait_ge(S["hlo_ready"], l * (3 * KB) + KB)
                A(hf[:, :, :], mem32, ACT.Square).then_inc(S["mem_sq"], 1)
                ffn_in(l, B_F1, O_F1, 0)
                root(PS[:, BANK_MEM, 0:T], memr, D_MODEL, "mem_ssq", l1, "mem_ln", "mem_r")
                ffn_out(l, B_F2, O_F2)
                act.wait_ge(S["memh_ready"], l * KB + KB)
                act.wait_ge(S["block_done"], lb + (B_MEM + RING))
                for c in range(4):
                    A(acthi[:, 2 * c:2 * c + 2, :], mem32[:, 2 * c:2 * c + 2, :], ACT.Copy)\
                        .then_inc(S["memhi_ready"], 1)
                norm(l, 1)
                for c in range(4):
                    hi(lb, B_MEM + 2 * c)
                    hi(lb, B_MEM + 2 * c + 1)
                    o = O_MEM + c
                    q = group(o, lb, B_MEM + 2 * c + 1)
                    dst = memk[:, 2 * c:2 * c + 2, :] if c < 2 else vall[:, 4:6, (c - 2) * 256:(c - 1) * 256]
                    A(dst, PS[:, q:q + 2, 0:T], ACT.Copy).then_inc(read[o % 2], 1)
                    if c == 1:
                        for e in (o - 1, o):
                            act.wait_ge(read[e % 2], read_value(e, lh))
                        A(rows(memksq, 4), memk[:, :, :], ACT.Square).then_inc(S["memk_sq"], 1)
                act.wait_ge(S["pad_zeroed"], l1)
                for c in range(2):
                    for part in range(2):
                        b, o = B_CONV + 4 * c + 2 * part, O_CONV + 2 * c + part
                        hi(lb, b)
                        hi(lb, b + 1)
                        q = group(o, lb, b + 1)
                        if part == 0:
                            A(ypad[:, 2 * c:2 * c + 2, PAD:PAD + T], PS[:, q:q + 2, 0:T], ACT.Copy)\
                                .then_inc(read[o % 2], 1)
                        else:
                            A(glu[c], PS[:, q:q + 2, 0:T], ACT.Sigmoid).then_inc(read[o % 2], 1)
                root(PS[:, 5:7, :], rows(memkr, 2), HEAD_DIM, "memk_ssq", l1, "memk_ln", "memk_r")
                for c in range(4):
                    hi(lb, B_SBQ + 2 * c)
                    hi(lb, B_SBQ + 2 * c + 1)
                    o = O_SBQ + c
                    q = group(o, lb, B_SBQ + 2 * c + 1)
                    A(hf[:, 2 * c:2 * c + 2, :], PS[:, q:q + 2, 0:T], ACT.Copy).then_inc(read[o % 2], 1)
                for c in range(2):
                    hi(lb, B_SBV + 2 * c)
                    hi(lb, B_SBV + 2 * c + 1)
                    o = O_SBV + c
                    q = group(o, lb, B_SBV + 2 * c + 1)
                    A(vall[:, 0:2, c * 256:(c + 1) * 256], PS[:, q:q + 2, 0:T], ACT.Copy).then_inc(read[o % 2], 1)
                act.wait_ge(S["memk_ready"], l1)
                for c in range(2):
                    hi(lb, B_LAT + 2 * c)
                    hi(lb, B_LAT + 2 * c + 1)
                    o = O_LAT + c
                    q = group(o, lb, B_LAT + 2 * c + 1)
                    A(rows(lat32, 4)[:, 2 * c:2 * c + 2, :], PS[:, q:q + 2, 0:T], ACT.Copy).then_inc(read[o % 2], 1)
                for o in (O_LAT, O_LAT + 1):
                    act.wait_ge(read[o % 2], read_value(o, lh))
                A(latsq, lat32, ACT.Square).then_inc(S["lat_sq"], 1)
                for c in range(2):
                    hi(lb, B_MEMQ + 2 * c)
                    if c == 0:
                        root(PS[:, BANK_MLA, :], latr, LORA, "lat_ssq", l1, "lat_ln", "lat_r")
                        act.wait_ge(S["lat_normed"], l * 4 + 4)
                        A(lathi[:, :, :], rows(lat32, 4), ACT.Copy).then_inc(S["lathi_ready"], 1)
                    hi(lb, B_MEMQ + 2 * c + 1)
                    if c == 0:
                        act.wait_ge(S["hi_ready"], lb + (B_UP + 1))
                        A(wide(acthi), runs(f(whi[:, B_UP % RING, :])), ACT.Copy).then_inc(S["widehi_ready"], 1)
                    o = O_MEMQ + c
                    q = group(o, lb, B_MEMQ + 2 * c + 1)
                    A(memq[:, 2 * c:2 * c + 2, :], PS[:, q:q + 2, 0:T], ACT.Copy).then_inc(read[o % 2], 1)
                hi(lb, B_UP)
                act.wait_ge(S["kr_ready"], l1)
                A(krsq[:, :], PS[:, BANK_NORM, 0:T], ACT.Square).then_inc(S["krsq_ready"], 1)
                dsts = [mlaqk[:, 1, :, :], mlaqk[:, 0, :, :], mlaqk[:, 2, :, :], vall[:, 2:4, :]]
                for c in range(4):
                    if c:
                        hi(lb, B_UP + c)
                    o = O_UP + c
                    q = group(o, lb, B_UP + c)
                    src = PS[:, q:q + 2, :] if c == 3 else PS[:, q:q + 2, :].rearrange("p a (b n) -> p (a b) n", b=2)
                    A(dsts[c], src, ACT.Copy).then_inc(read[o % 2], 1)
                for o in (O_UP + 2, O_UP + 3):
                    act.wait_ge(read[o % 2], read_value(o, lh))
                with act.Fori(0, HEADS) as i:
                    n1 = act.snap(l * HEADS + i + 1)
                    base = act.snap(l * NBLK + i * 8)

                    def gate(g):
                        hi(base, B_GATE + 2 * g)
                        hi(base, B_GATE + 2 * g + 1)

                    def keep(g):
                        o = O_GATE + g
                        q = group(o, base, B_GATE + 2 * g + 1)
                        level()
                        A(gates[:, bass.ds(i, 1), 2 * g:2 * g + 2, :].rearrange("p a k n -> p (a k) n"),
                          PS[:, q:q + 2, 0:T], ACT.Copy).then_inc(read[o % 2], 1)

                    A(rows(sbr, 2), hf[:, :, :].rearrange("p (a h) n -> p a h n", a=2)[:, :, i, :], ACT.Square)\
                        .then_inc(S["sb_sq"], 1)
                    A(rows(msq, 3), mlaqk[:, :, i, :], ACT.Square).then_inc(S["mla_sq"], 1)
                    A(er, memq[:, i, :], ACT.Square).then_inc(S["e_sq"], 1)
                    A(vh, vall[:, :, bass.ds(i * HEAD_DIM, HEAD_DIM)], ACT.Copy).then_inc(S["vh_ready"], 1)
                    gate(0)
                    keep(0)
                    root(PS[:, BANK_SB, :], sbr, HEAD_DIM, "sb_ssq", n1, "sb_ln", "sb_r")
                    root(PS[:, BANK_MLA, :], mr, HEAD_DIM + ROPE, "mla_ssq", n1, "mla_ln", "mla_r")
                    root(PS[:, BANK_MEM, 0:T], er, HEAD_DIM, "e_ssq", n1, "e_ln", "e_r")
                    gate(1)
                    keep(1)
                    act.wait_ge(S["sb_z"], n1)
                    A(sbL, PS[:, BANK_SB, 0:384], ACT.Abs, scale=SB_SCALE).then_inc(S["sb_abs"], 1)
                    act.wait_ge(S["sb_abs"], n1)
                    A(sbL, sbL, ACT.Exp, scale=-1.0).then_inc(S["sb_exp"], 1)
                    act.wait_ge(S["sb_exp"], n1)
                    A(sbL, sbL, ACT.Ln, bias=one).then_inc(S["sb_L"], 1)
                    gate(2)
                    act.wait_ge(S["mla_neg"], n1)
                    A(mP[:, 0:P], PS[:, BANK_MLA, 0:P], ACT.Exp, scale=MLA_SCALE, bias=stat[:, 2:3],
                      accum_out=stat[:, 4:5]).then_inc(S["mla_p"], 1)
                    A(mP[:, P:384], PS[:, BANK_MLA, P:384], ACT.Exp, scale=MLA_SCALE, bias=stat[:, 3:4],
                      accum_out=stat[:, 5:6]).then_inc(S["mla_p"], 1)
                    act.wait_ge(S["e_neg"], n1)
                    for j in range(2):
                        A(eP[:, j * T:(j + 1) * T], PS[:, BANK_MEM, j * T:(j + 1) * T], ACT.Exp, scale=SB_SCALE,
                          bias=stat[:, 10 + j:11 + j], accum_out=stat[:, 12 + j:13 + j]).then_inc(S["e_p"], 1)
                    keep(2)
                    gate(3)
                    act.wait_ge(S["sb_logw"], n1)
                    A(lw, lw, ACT.Exp).then_inc(S["sb_expw"], 1)
                    act.wait_ge(S["mla_transposed"], n1)
                    A(mPT, PS[:, BANK_MLA, 0:384], ACT.Copy).then_inc(S["mla_PT"], 1)
                    act.wait_ge(S["e_transposed"], n1)
                    A(ePT, PS[:, BANK_MEM, :], ACT.Copy).then_inc(S["e_PT"], 1)
                    keep(3)
                    act.wait_ge(S["sb_pv"], n1)
                    level()
                    A(b1hi[:, i, :], PS[:, BANK_SB, 0:T], ACT.Copy).then_inc(S["sb_hi"], 1)
                    act.wait_ge(S["mla_pv"], n1)
                    level()
                    A(b2hi[:, i, :], PS[:, BANK_MLA, 0:T], ACT.Copy).then_inc(S["mla_hi"], 1)
                    act.wait_ge(S["e_pv"], n1)
                    level()
                    A(b3hi[:, i, :], PS[:, BANK_MEM, 0:T], ACT.Copy).then_inc(S["e_hi"], 1)
                for o in (O_GATE + 14, O_GATE + 15):
                    act.wait_ge(read[o % 2], read_value(o, lh))
                for u in range(2):
                    for c in range(4):
                        hi(lb, B_BRANCH + 8 * u + 2 * c)
                        hi(lb, B_BRANCH + 8 * u + 2 * c + 1)
                        if u == 0 and c == 1:
                            act.wait_ge(S["ln_c"], l1)
                            A(ysq, yc, ACT.Square).then_inc(S["ln_sq"], 1)
                        if u == 0 and c == 2:
                            root(PS[:, BANK_NORM, 0:T], yr, CONV_CH, "ln_var", l1, "ln_ln", "ln_r")
                        if u == 0 and c == 3:
                            act.wait_ge(S["ln_n"], l1)
                            for k in range(4):
                                A(rows(y32, 4)[:, k, :], rows(yc, 4)[:, k, :], ACT.Silu,
                                  scale=par[:, C_LNG + k:C_LNG + k + 1], bias=par[:, C_LNB + k:C_LNB + k + 1])\
                                    .then_inc(S["ln_silu"], 1)
                            act.wait_ge(S["ln_silu"], l * 4 + 4)
                            A(b0hi[:, :, :], rows(y32, 4), ACT.Copy).then_inc(S["b0hi_ready"], 1)
                        j0 = 2 - 2 * u
                        for j in (j0, j0 + 1):
                            g = gates[:, j, 2 * c:2 * c + 2, :]
                            A(g, g, ACT.Sigmoid).then_inc(S["gate_sig"], 1)
                        if u == 1:
                            act.wait_ge(S["merged_ready"], l * 8 + (4 + c + 1))
                            A(hhi[:, 2 * c:2 * c + 2, :], hf[:, 2 * c:2 * c + 2, :], ACT.Copy)\
                                .then_inc(S["mergedhi_ready"], 1)
                for c in range(4):
                    hi(lb, B_OUT + 2 * c)
                    hi(lb, B_OUT + 2 * c + 1)
                    o = O_OUT + c
                    act.wait_ge(read[o % 2], read_value(o, lh))
                    act.wait_ge(S["mergedlo_ready"], l * 4 + 4)
                    A(hf[:, 2 * c:2 * c + 2, :], x[:, 2 * c:2 * c + 2, :], ACT.Square).then_inc(S["x_sq"], 1)
                norm(l, 2)
                ffn_in(l, B_G1, O_G1, 8)
                ffn_out(l, B_G2, O_G2)

        @block.vector
        def _(dve):
            V = nc.vector
            STT, TT, TS = V.scalar_tensor_tensor, V.tensor_tensor, V.tensor_scalar

            def lo(base, b):
                b += AHEAD
                dve.wait_ge(S["hi_ready"], base + (b + 1))
                TT(wlo[:, b % RING, :], raw[:, b % RING, :], f(whi[:, b % RING, :]), ALU.subtract)\
                    .then_inc(S["lo_ready"], 1)

            def group(o, base, b):
                dve.wait_ge(S["block_done"], base + (b + 1 + RING))
                return 2 * (o % 2)

            def norm(l, m, col):
                def low(k):
                    dve.wait_ge(S["hhi_ready"], l * (3 * KB) + (m * KB + k + 1))
                    TT(hlo[:, k, :], hf[:, k, :], f(hhi[:, k, :]), ALU.subtract).then_inc(S["hlo_ready"], 1)
                dve.wait_ge(S["rms_ready"], l * 3 + (m + 1))
                for k in range(KB):
                    STT(hf[:, k, :], x[:, k, :], par[:, col + k:col + k + 1], xr, ALU.mult, ALU.mult)\
                        .then_inc(S["hf_ready"], 1)
                    if k:
                        low(k - 1)
                low(KB - 1)

            def ffn_in(l, b0, o0, f0):
                with dve.Fori(0, 4) as it:
                    base, hb = dve.snap(l * NBLK + it * 8), dve.snap(l * HALF_OUT + it * 2)
                    for j in range(2):
                        for k in range(4):
                            lo(base, b0 + 4 * j + k)
                        o = o0 + 2 * j + 1
                        q = group(o, base, b0 + 4 * j + 3)
                        dve.wait_ge(read[0], read_value(o - 1, hb))
                        TT(act32[j], PS[:, q:q + 2, 0:T], silu[j], ALU.mult).then_inc(read[1], 1)
                        dve.wait_ge(S["acthi_ready"], l * 16 + it * 2 + (f0 + j + 1))
                        at = bass.ds(it * 4 + 2 * j, 2)
                        TT(actlo[:, at, :], act32[j], f(acthi[:, at, :]), ALU.subtract).then_inc(S["actlo_ready"], 1)

            def update(o, base, b, at, scale):
                q = group(o, base, b)
                STT(x[:, at, :], PS[:, q:q + 2, 0:T], scale, x[:, at, :], ALU.mult, ALU.add).then_inc(read[o % 2], 1)

            def ffn_out(l, b0, o0):
                with dve.Fori(0, 2) as it:
                    base = dve.snap(l * NBLK + it * 8)
                    for j in range(2):
                        for k in range(4):
                            lo(base, b0 + 4 * j + k)
                        update(o0 + j, base, b0 + 4 * j + 3, bass.ds(it * 4 + 2 * j, 2), 0.5)

            for s in ("sb_lo", "mla_lo", "e_lo", "conv_tap"):
                dve.sem_inc(S[s], 1)
            dve.wait_ge(S["pos_loaded"], 16)
            dve.wait_ge(S["const_loaded"], 16)

            def rope(step, ins):
                ins.then_inc(S["rope_step"], 1)
                dve.wait_ge(S["rope_step"], step)

            rope(1, V.tensor_copy(qtab[:, :], ropeQ[:, :].bitcast(I32)))
            rope(2, TS(krsq[:, :], qtab[:, :], con[:, K_FREQ:K_FREQ + 1], None, ALU.mult))
            rope(3, TS(krot[:, :], krsq[:, :], 1.0 / (2 * np.pi), ROUNDER, ALU.mult, ALU.add))
            rope(4, TS(krot[:, :], krot[:, :], ROUNDER, None, ALU.subtract))
            rest, parts = 2 * np.pi, []
            for bits in (5, 13):
                parts.append(float(np.floor(rest * 2.0 ** bits) / 2.0 ** bits))
                rest -= parts[-1]
            for k, part in enumerate(parts + [float(rest)]):
                rope(5 + k, STT(krsq[:, :], krot[:, :], -part, krsq[:, :], ALU.mult, ALU.add))
            rope(8, STT(krot[:, :], krsq[:, :], -1.0, krsq[:, :], ALU.mult, ALU.max))
            rope(9, TS(krot[:, :], krot[:, :], -1.0, np.pi / 2, ALU.mult, ALU.add))
            dve.wait_ge(S["rope_step"], 11)
            rope(12, TS(ropeQ[:, :], cosT[:, :], con[:, K_QC:K_QC + 1], None, ALU.mult))
            rope(13, STT(ropeQ[:, :], sinK[:, :], con[:, K_QS:K_QS + 1], ropeQ[:, :], ALU.mult, ALU.add))
            rope(14, TS(sinK[:, :], sinK[:, :], con[:, K_KS:K_KS + 1], None, ALU.mult))
            for b in range(-AHEAD, 0):
                lo(0, b)
            with dve.Fori(0, DEPTH) as l:
                lb, lh = dve.snap(l * NBLK), dve.snap(l * HALF_OUT)
                l1 = dve.snap(l + 1)
                dve.wait_ge(S["par_loaded"], l * 16 + 16)
                norm(l, 0, C_FFN1)
                ffn_in(l, B_F1, O_F1, 0)
                dve.wait_ge(S["mem_r"], l1)
                for k in range(KB):
                    STT(mem32[:, k, :], mem32[:, k, :], par[:, C_MEM + k:C_MEM + k + 1], memr, ALU.mult, ALU.mult)\
                        .then_inc(S["memh_ready"], 1)
                ffn_out(l, B_F2, O_F2)
                for c in range(4):
                    dve.wait_ge(S["memhi_ready"], l * 4 + (c + 1))
                    TT(actlo[:, 2 * c:2 * c + 2, :], mem32[:, 2 * c:2 * c + 2, :], f(acthi[:, 2 * c:2 * c + 2, :]),
                       ALU.subtract).then_inc(S["memlo_ready"], 1)
                norm(l, 1, C_MIX)
                for k in range(8):
                    lo(lb, B_MEM + k)
                V.memset(ypad[:, :, 0:PAD], 0.0).then_inc(S["pad_zeroed"], 1)
                TS(qtab[:, :], ropeQ[:, :], par[:, C_MQR:C_MQR + 1], None, ALU.mult).then_inc(S["qtab_ready"], 1)
                for c in range(2):
                    for k in range(4):
                        lo(lb, B_CONV + 4 * c + k)
                    for o in (O_CONV + 2 * c, O_CONV + 2 * c + 1):
                        dve.wait_ge(read[o % 2], read_value(o, lh))
                    y = ypad[:, 2 * c:2 * c + 2, PAD:PAD + T]
                    TT(y, y, glu[c], ALU.mult).then_inc(S["glu_ready"], 1)
                lo(lb, B_SBQ)
                dve.wait_ge(S["memk_r"], l1)
                mk_flat = memk[:, :, :].rearrange("p h n -> p (h n)")
                STT(mk_flat, mk_flat, par[:, C_EK:C_EK + 1], memkr, ALU.mult, ALU.mult).then_inc(S["memk_ready"], 1)
                for k in range(1, 8):
                    lo(lb, B_SBQ + k)
                for k in range(4):
                    lo(lb, B_SBV + k)
                for k in range(4):
                    lo(lb, B_LAT + k)
                lo(lb, B_MEMQ)
                dve.wait_ge(S["lat_r"], l1)
                for k in range(4):
                    y = rows(lat32, 4)[:, k, :]
                    STT(y, y, par[:, C_QLAT + k:C_QLAT + k + 1], latr[:, (k // 2) * T:(k // 2 + 1) * T],
                        ALU.mult, ALU.mult).then_inc(S["lat_normed"], 1)
                dve.wait_ge(S["lathi_ready"], l1)
                TT(latlo[:, :, :], rows(lat32, 4), f(lathi[:, :, :]), ALU.subtract).then_inc(S["latlo_ready"], 1)
                lo(lb, B_MEMQ + 1)
                dve.wait_ge(S["lo_ready"], lb + (B_UP + 1))
                V.tensor_copy(wide(actlo), runs(f(wlo[:, B_UP % RING, :]))).then_inc(S["widelo_ready"], 1)
                for k in range(2, 4):
                    lo(lb, B_MEMQ + k)
                lo(lb, B_UP)
                dve.wait_ge(S["krsq_ready"], l1)
                TS(krg, PS[:, BANK_NORM, 0:T], par[:, C_MKR:C_MKR + 1], None, ALU.mult).then_inc(S["krg_ready"], 1)
                lo(lb, B_UP + 1)
                lo(lb, B_UP + 2)
                dve.wait_ge(S["kr_permuted"], l1)
                TT(krt[:, 0, :], PS[:, BANK_NORM, 0:T], cosT[:, :], ALU.mult).then_inc(S["krt_ready"], 1)
                TT(krt[:, 1, :], PS[:, BANK_NORM, T:2 * T], sinK[:, :], ALU.mult).then_inc(S["krt_ready"], 1)
                lo(lb, B_UP + 3)
                dve.wait_ge(S["krt_ready"], l * 2 + 2)
                TT(krot[:, :], krt[:, 0, :], krt[:, 1, :], ALU.add).then_inc(S["krot_ready"], 1)
                dve.wait_ge(S["krot_ready"], l1)
                dve.wait_ge(S["glu_ready"], l * 2 + 2)
                dve.sem_inc(S["dve_waited"], 1)
                with dve.Fori(0, HEADS) as i:
                    n1 = dve.snap(l * HEADS + i + 1)
                    base = dve.snap(l * NBLK + i * 8)
                    taps = dve.snap((l * HEADS + i) * 32)
                    wcol = dve.snap(i * CONVW)

                    def conv(k0, k1):
                        for k in range(k0, k1):
                            w = par[:, bass.ds(wcol + (C_CONV + min(k, 30)), 1)]
                            y = ypad[:, bass.ds(i, 1), min(k, 30):min(k, 30) + T].rearrange("p a n -> p (a n)")
                            dve.wait_ge(S["conv_tap"], taps + (1 if k < 2 else k if k < 30 else k + 1))
                            if k == 0:
                                bias = par[:, bass.ds(wcol + (C_CONV + TAPS), 1)]
                                ins = TS(acc[0], y, w, bias, ALU.mult, ALU.add)
                            elif k == 1:
                                ins = TS(acc[1], y, w, None, ALU.mult)
                            elif k < 30:
                                ins = STT(acc[k % 2], y, w, acc[k % 2], ALU.mult, ALU.add)
                            elif k == 30:
                                ins = TT(acc[0], acc[0], acc[1], ALU.add)
                            else:
                                ins = STT(y, y, w, acc[0], ALU.mult, ALU.add)
                            ins.then_inc(S["conv_tap"], 1)

                    def gate(g):
                        lo(base, B_GATE + 2 * g)
                        conv(8 * g, 8 * g + 4)
                        lo(base, B_GATE + 2 * g + 1)

                    gate(0)
                    conv(4, 8)
                    dve.wait_ge(S["sb_r"], n1)
                    STT(sbq, hf[:, bass.ds(i, 1), :].rearrange("p a n -> p (a n)"), par[:, C_SBQ:C_SBQ + 1],
                        sbr[:, 0:T], ALU.mult, ALU.mult).then_inc(S["sb_normed"], 1)
                    STT(sbk, hf[:, bass.ds(i + 4, 1), :].rearrange("p a n -> p (a n)"), par[:, C_SBK:C_SBK + 1],
                        sbr[:, T:2 * T], ALU.mult, ALU.mult).then_inc(S["sb_normed"], 1)
                    TT(mqr, mlaqk[:, 1, i, :], qtab[:, :], ALU.mult).then_inc(S["mqr_tabled"], 1)
                    dve.wait_ge(S["mla_r"], n1)
                    STT(mq, mlaqk[:, 0, i, :], par[:, C_MQN:C_MQN + 1], mr[:, 0:T], ALU.mult, ALU.mult)\
                        .then_inc(S["mla_normed"], 1)
                    STT(mk, mlaqk[:, 2, i, :], par[:, C_MKN:C_MKN + 1], mr[:, T:2 * T], ALU.mult, ALU.mult)\
                        .then_inc(S["mla_normed"], 1)
                    dve.wait_ge(S["mqr_tabled"], n1)
                    TT(mqr, mqr, mr[:, 0:T], ALU.mult).then_inc(S["mla_normed"], 1)
                    TT(mkr, krot[:, :], mr[:, T:2 * T], ALU.mult).then_inc(S["mla_normed"], 1)
                    dve.wait_ge(S["e_r"], n1)
                    STT(eq, memq[:, i, :], par[:, C_EQ:C_EQ + 1], er, ALU.mult, ALU.mult).then_inc(S["e_normed"], 1)
                    gate(1)
                    conv(12, 16)
                    dve.wait_ge(S["mla_s"], n1)
                    V.memset(rows(PS[0:CHUNK, BANK_MLA, :], 2)[:, :, CHUNK:P], -1e30).then_inc(S["mla_masked"], 1)
                    dve.wait_ge(S["e_s"], n1)
                    V.reduce_max(stat[:, 8:10], rows(PS[:, BANK_MEM, :], 2), axis=AX.X).then_inc(S["e_max"], 1)
                    dve.wait_ge(S["mla_masked"], n1)
                    V.reduce_max(stat[:, 0:1], PS[:, BANK_MLA, 0:P], axis=AX.X).then_inc(S["mla_max"], 1)
                    V.reduce_max(stat[:, 1:2], PS[:, BANK_MLA, P:384], axis=AX.X).then_inc(S["mla_max"], 1)
                    dve.wait_ge(S["e_max"], n1)
                    TS(stat[:, 10:12], stat[:, 8:10], -SB_SCALE, None, ALU.mult).then_inc(S["e_neg"], 1)
                    dve.wait_ge(S["mla_max"], n1 * 2)
                    TS(stat[:, 2:4], stat[:, 0:2], -MLA_SCALE, None, ALU.mult).then_inc(S["mla_neg"], 1)
                    z = PS[:, BANK_SB, 0:384]
                    dve.wait_ge(S["sb_abs"], n1)
                    TS(lk, z, SB_SCALE, 0.0, ALU.mult, ALU.max).then_inc(S["sb_m"], 1)
                    lo(base, B_GATE + 4)
                    dve.wait_ge(S["sb_m"], n1)
                    dve.wait_ge(S["sb_L"], n1)
                    STT(lk, lk, -1.0, sbL, ALU.mult, ALU.subtract).then_inc(S["sb_lk"], 1)
                    conv(16, 18)
                    dve.wait_ge(S["sb_lk"], n1)
                    STT(lw, z, SB_SCALE, lk, ALU.mult, ALU.add).then_inc(S["sb_a"], 1)
                    dve.wait_ge(S["sb_a"], n1)
                    TT(diag2(lk), diag2(lk), strict2, ALU.mult).then_inc(S["sb_lkm"], 1)
                    lo(base, B_GATE + 5)
                    dve.wait_ge(S["mla_p"], n1 * 2)
                    V.reciprocal(stat[:, 6:8], stat[:, 4:6]).then_inc(S["mla_rec"], 1)
                    dve.wait_ge(S["e_p"], n1 * 2)
                    V.reciprocal(stat[:, 14:16], stat[:, 12:14]).then_inc(S["e_rec"], 1)
                    dve.wait_ge(S["mla_rec"], n1)
                    TS(mP[:, 0:P], mP[:, 0:P], stat[:, 6:7], None, ALU.mult).then_inc(S["mla_pn"], 1)
                    TS(mP[:, P:384], mP[:, P:384], stat[:, 7:8], None, ALU.mult).then_inc(S["mla_pn"], 1)
                    dve.wait_ge(S["e_rec"], n1)
                    for j in range(2):
                        p = eP[:, j * T:(j + 1) * T]
                        TS(p, p, stat[:, 14 + j:15 + j], None, ALU.mult).then_inc(S["e_pn"], 1)
                    conv(18, 24)
                    gate(3)
                    dve.wait_ge(S["sb_later"], n1)
                    TT(lw, PS[:, BANK_SB, 0:384], lw, ALU.add).then_inc(S["sb_logw"], 1)
                    conv(28, 30)
                    dve.wait_ge(S["sb_expw"], n1)
                    TT(diag2(lw), diag2(lw), strict2, ALU.mult).then_inc(S["sb_w"], 1)
                    conv(30, 32)
                    for s, bank, dhi, dlo in (("sb", BANK_SB, b1hi, b1lo), ("mla", BANK_MLA, b2hi, b2lo),
                                              ("e", BANK_MEM, b3hi, b3lo)):
                        dve.wait_ge(S[s + "_hi"], n1)
                        TT(dlo[:, i, :], PS[:, bank, 0:T], f(dhi[:, i, :]), ALU.subtract).then_inc(S[s + "_lo"], 1)
                for u in range(2):
                    for c in range(4):
                        lo(lb, B_BRANCH + 8 * u + 2 * c)
                        lo(lb, B_BRANCH + 8 * u + 2 * c + 1)
                        if u == 0 and c == 0:
                            dve.wait_ge(S["ln_mean"], l1)
                            mean = rows(PS[:, BANK_NORM, 0:T], 1).broadcast_to([P, 4, T])
                            STT(rows(yc, 4), mean, -1.0 / CONV_CH, ypad[:, :, PAD:PAD + T], ALU.mult, ALU.add)\
                                .then_inc(S["ln_c"], 1)
                        if u == 0 and c == 2:
                            dve.wait_ge(S["ln_r"], l1)
                            TT(rows(yc, 4), rows(yc, 4), rows(yr, 1).broadcast_to([P, 4, T]), ALU.mult)\
                                .then_inc(S["ln_n"], 1)
                        if u == 0 and c == 3:
                            dve.wait_ge(S["b0hi_ready"], l1)
                            TT(b0lo[:, :, :], rows(y32, 4), f(b0hi[:, :, :]), ALU.subtract).then_inc(S["b0lo_ready"], 1)
                        o = O_BRANCH + 4 * u + c
                        q = group(o, lb, B_BRANCH + 8 * u + 2 * c + 1)
                        j0 = 2 - 2 * u
                        g = [gates[:, j0 + s, 2 * c:2 * c + 2, :] for s in range(2)]
                        m = hf[:, 2 * c:2 * c + 2, :]
                        dve.wait_ge(S["gate_sig"], l * 16 + (8 * u + 2 * c + 2))
                        first = m if u == 0 else prod[0]
                        if u or c:
                            dve.wait_ge(S["merged_ready"], l * 8 + (4 * u + c))
                        TT(first, PS[:, q:q + 2, 0:T], g[0], ALU.mult).then_inc(S["prod_ready"], 1)
                        TT(prod[1], PS[:, q:q + 2, T:2 * T], g[1], ALU.mult).then_inc(read[o % 2], 1)
                        dve.wait_ge(read[o % 2], read_value(o, lh))
                        dve.wait_ge(S["prod_ready"], l * 12 + (c + 1 if u == 0 else 4 + 2 * c + 1))
                        if u == 0:
                            TT(m, m, prod[1], ALU.add).then_inc(S["merged_ready"], 1)
                        else:
                            TT(prod[0], prod[0], prod[1], ALU.add).then_inc(S["prod_ready"], 1)
                            dve.wait_ge(S["prod_ready"], l * 12 + (4 + 2 * c + 2))
                            TT(m, m, prod[0], ALU.add).then_inc(S["merged_ready"], 1)
                            dve.wait_ge(S["mergedhi_ready"], l * 4 + (c + 1))
                            TT(hlo[:, 2 * c:2 * c + 2, :], m, f(hhi[:, 2 * c:2 * c + 2, :]), ALU.subtract)\
                                .then_inc(S["mergedlo_ready"], 1)
                for c in range(4):
                    lo(lb, B_OUT + 2 * c)
                    lo(lb, B_OUT + 2 * c + 1)
                    update(O_OUT + c, lb, B_OUT + 2 * c + 1, slice(2 * c, 2 * c + 2), 1.0)
                norm(l, 2, C_FFN2)
                ffn_in(l, B_G1, O_G1, 8)
                ffn_out(l, B_G2, O_G2)

        @block.tensor
        def _(pe):
            MM = nc.tensor.matmul

            def split(out, whi_, wlo_, xhi, xlo, start, stop):
                MM(out, whi_, xhi, start=start, stop=False)
                MM(out, whi_, xlo, start=False, stop=False)
                return MM(out, wlo_, xhi, start=False, stop=stop)

            def turn(o, hb):
                pe.wait_ge(read[o % 2], hb + (o // 2 + 1))
                return 2 * (o % 2)

            def arrived(base, b):
                pe.wait_ge(S["lo_ready"], base + (b + 1))

            def feature_block(base, b, out, xhi, xlo, kbs, first=True, last=True, each=None):
                arrived(base, b)
                s = b % RING
                for n, kb in enumerate(kbs):
                    if each:
                        each(n)
                    w = slice(n * P, (n + 1) * P)
                    ins = split(out, whi[:, s, w], wlo[:, s, w], xhi[:, kb, :], xlo[:, kb, :],
                                first and n == 0, last and n == len(kbs) - 1)
                ins.then_inc(S["block_done"], 1)

            def token_pair(base, b, q, xhi, xlo, hb, o):
                for half in range(2):
                    arrived(base, b + half)
                    s = (b + half) % RING
                    for k in range(4):
                        kb, w = 4 * half + k, slice(k * 2 * P, (k + 1) * 2 * P)
                        for t in range(2):
                            tt = slice(t * P, (t + 1) * P)
                            out = PS[:, q + t, 0:T]
                            MM(out, xhi[:, kb, tt], whi[:, s, w], start=kb == 0, stop=False)
                            MM(out, xhi[:, kb, tt], wlo[:, s, w], start=False, stop=False)
                            ins = MM(out, xlo[:, kb, tt], whi[:, s, w], start=False, stop=kb == KB - 1)
                    ins.then_inc(S["block_done"], 1)

            def feature_pair(base, b, o, hb, each=None):
                q = turn(o, hb)
                for m in range(2):
                    feature_block(base, b + m, PS[:, q + m, 0:T], hhi, hlo, range(KB), each=each if m == 0 else None)

            def x_sums(c, value):
                pe.wait_ge(S["x_sq"], value)
                for k in (2 * c, 2 * c + 1):
                    ins = MM(PS[:, BANK_NORM, 0:T], ones, hf[:, k, :], start=k == 0, stop=k == KB - 1)
                if c == 3:
                    ins.then_inc(S["ssq_ready"], 1)

            def ffn_in(l, b0, o0):
                pe.sem_inc(S["pe_waited"], 1)
                with pe.Fori(0, 4) as it:
                    base, hb = pe.snap(l * NBLK + it * 8), pe.snap(l * HALF_OUT + it * 2)
                    for j in range(4):
                        feature_pair(base, b0 + 2 * j, o0 + j, hb)

            def ffn_out(l, b0, o0, f0, sq0):
                with pe.Fori(0, 2) as it:
                    base, hb = pe.snap(l * NBLK + it * 8), pe.snap(l * HALF_OUT + it)

                    for j in range(2):
                        q = turn(o0 + j, hb)
                        for half in range(2):
                            pe.wait_ge(S["actlo_ready"], l * 16 + (f0 + 4 * half + 4))
                            for m in range(2):
                                feature_block(base, b0 + 4 * j + 2 * half + m, PS[:, q + m, 0:T], acthi, actlo,
                                              range(8 * half, 8 * half + 8), first=half == 0, last=half == 1)

            def sums_all(l, sq0):
                for c in range(4):
                    x_sums(c, l * 12 + (4 + sq0 + c + 1))

            pe.sem_inc(S["block_done"], RING)
            pe.wait_ge(S["const_loaded"], 16)
            for c in range(4):
                x_sums(c, c + 1)
            with pe.Fori(0, DEPTH) as l:
                lb, lh = pe.snap(l * NBLK), pe.snap(l * HALF_OUT)
                l1 = pe.snap(l + 1)

                def normed(m):
                    def each(k):
                        pe.wait_ge(S["hlo_ready"], l * (3 * KB) + (m * KB + k + 1))
                    return each

                for k in range(KB):
                    normed(0)(k)
                ffn_in(l, B_F1, O_F1)
                pe.wait_ge(S["mem_sq"], l1)
                for k in range(KB):
                    ins = MM(PS[:, BANK_MEM, 0:T], ones, hf[:, k, :], start=k == 0, stop=k == KB - 1)
                ins.then_inc(S["mem_ssq"], 1)
                ffn_out(l, B_F2, O_F2, 0, 0)
                sums_all(l, 0)
                for c in range(4):
                    o, b = O_MEM + c, B_MEM + 2 * c
                    q = turn(o, lh)

                    def mem_arrives(k):
                        if k % 2 == 0:
                            pe.wait_ge(S["memlo_ready"], l * 4 + (k // 2 + 1))

                    if c < 2:
                        for m in range(2):
                            feature_block(lb, b + m, PS[:, q + m, 0:T], acthi, actlo, range(KB),
                                          each=mem_arrives if c == m == 0 else None)
                    else:
                        token_pair(lb, b, q, acthi, actlo, lh, o)
                pe.wait_ge(S["memk_sq"], l1)
                for k in range(2):
                    ins = MM(PS[:, 5 + k, :], ones, memksq[:, k * 512:(k + 1) * 512], start=True, stop=True)
                ins.then_inc(S["memk_ssq"], 1)
                for c in range(4):
                    feature_pair(lb, B_CONV + 2 * c, O_CONV + c, lh, each=normed(1) if c == 0 else None)
                for c in range(4):
                    feature_pair(lb, B_SBQ + 2 * c, O_SBQ + c, lh)
                for c in range(2):
                    q = turn(O_SBV + c, lh)
                    token_pair(lb, B_SBV + 2 * c, q, hhi, hlo, lh, O_SBV + c)
                for c in range(2):
                    feature_pair(lb, B_LAT + 2 * c, O_LAT + c, lh)
                for c in range(2):
                    q = turn(O_MEMQ + c, lh)
                    for m in range(2):
                        feature_block(lb, B_MEMQ + 2 * c + m, PS[:, q + m, 0:T], hhi, hlo, range(KB))
                        if c == m == 0:
                            pe.wait_ge(S["lat_sq"], l1)
                            pe.wait_ge(S["memk_ready"], l1)
                            for k in range(4):
                                ins = MM(PS[:, BANK_MLA, (k // 2) * T:(k // 2 + 1) * T], ones,
                                         latsq[:, k * T:(k + 1) * T], start=k % 2 == 0, stop=k % 2 == 1)
                            ins.then_inc(S["lat_ssq"], 1)
                arrived(lb, B_UP)

                pe.wait_ge(S["widehi_ready"], l1)
                pe.wait_ge(S["widelo_ready"], l1)

                def twice(w, run):
                    return w[:, :, :].rearrange("p k n -> p (k n)")[:, run * P:(run + 1) * P]

                for kb in range(KB):
                    ins = split(PS[:, BANK_NORM, 0:T], twice(acthi, kb), twice(actlo, kb),
                                hhi[:, kb, :], hlo[:, kb, :], kb == 0, kb == KB - 1)
                ins.then_inc(S["kr_ready"], 1)
                pe.wait_ge(S["latlo_ready"], l1)
                for c in range(3):
                    q = turn(O_UP + c, lh)
                    if c:
                        arrived(lb, B_UP + c)
                    s, lat0 = (B_UP + c) % RING, 0 if c < 2 else 2
                    for h in range(HEADS):
                        for kb in range(2):
                            at = (h * 2 + kb) * P
                            if c == 0:
                                w = [twice(t, KB + h * 2 + kb) for t in (acthi, actlo)]
                            else:
                                w = [t[:, s, at:at + P] for t in (whi, wlo)]
                            ins = split(PS[:, q + h // 2, (h % 2) * T:(h % 2 + 1) * T], w[0], w[1],
                                        lathi[:, lat0 + kb, :], latlo[:, lat0 + kb, :], kb == 0, kb == 1)
                    ins.then_inc(S["block_done"], 1)
                    if c == 1:
                        pe.wait_ge(S["krg_ready"], l1)
                        MM(PS[:, BANK_NORM, 0:T], permA, krg, start=True, stop=True)
                        MM(PS[:, BANK_NORM, T:2 * T], permB, krg, start=True, stop=True).then_inc(S["kr_permuted"], 1)
                q = turn(O_UP + 3, lh)
                arrived(lb, B_UP + 3)
                s = (B_UP + 3) % RING
                for t in range(2):
                    tt = slice(t * P, (t + 1) * P)
                    for kb in range(2):
                        w = slice(kb * 512, (kb + 1) * 512)
                        out = PS[:, q + t, :]
                        MM(out, lathi[:, 2 + kb, tt], whi[:, s, w], start=kb == 0, stop=False)
                        MM(out, lathi[:, 2 + kb, tt], wlo[:, s, w], start=False, stop=False)
                        ins = MM(out, latlo[:, 2 + kb, tt], whi[:, s, w], start=False, stop=kb == 1)
                ins.then_inc(S["block_done"], 1)
                with pe.Fori(0, HEADS) as i:
                    n1 = pe.snap(l * HEADS + i + 1)
                    base, hb = pe.snap(l * NBLK + i * 8), pe.snap(l * HALF_OUT + i * 2)

                    def weighted(bank, v0, w):
                        MM(PS[:, bank, 0:T], vh[:, v0, :], w[:, 0:T], start=True, stop=False)
                        return MM(PS[:, bank, P:T], vh[:, v0 + 1, :], w[:, T:384], start=False, stop=True)

                    feature_pair(base, B_GATE, O_GATE, hb)
                    pe.wait_ge(S["sb_sq"], n1)
                    pe.wait_ge(S["sb_lo"], n1)
                    MM(PS[:, BANK_SB, :], ones, sbr, start=True, stop=True).then_inc(S["sb_ssq"], 1)
                    pe.wait_ge(S["mla_sq"], n1)
                    pe.wait_ge(S["mla_lo"], n1)
                    MM(PS[:, BANK_MLA, 0:T], ones, msq[:, 0:T], start=True, stop=False)
                    MM(PS[:, BANK_MLA, 0:T], halves, msq[:, T:2 * T], start=False, stop=True)
                    MM(PS[:, BANK_MLA, T:2 * T], ones, msq[:, 2 * T:3 * T], start=True, stop=False)
                    MM(PS[:, BANK_MLA, T:2 * T], halves, krsq[:, :], start=False, stop=True)\
                        .then_inc(S["mla_ssq"], 1)
                    pe.wait_ge(S["e_sq"], n1)
                    pe.wait_ge(S["e_lo"], n1)
                    MM(PS[:, BANK_MEM, 0:T], ones, er, start=True, stop=True).then_inc(S["e_ssq"], 1)
                    feature_pair(base, B_GATE + 2, O_GATE + 1, hb)
                    pe.wait_ge(S["sb_normed"], n1 * 2)
                    MM(PS[:, BANK_SB, 0:T], sbk[:, 0:P], sbq, start=True, stop=True)
                    MM(PS[:, BANK_SB, T:384], sbk[:, P:T], sbq[:, P:T], start=True, stop=True).then_inc(S["sb_z"], 1)
                    pe.wait_ge(S["mla_normed"], n1 * 4)
                    MM(PS[:, BANK_MLA, 0:P], mq[:, 0:P], mk[:, 0:P], start=True, stop=False)
                    MM(PS[:, BANK_MLA, 0:P], mqr[:, 0:P], mkr[:, 0:P], start=False, stop=True)
                    MM(PS[:, BANK_MLA, P:384], mq[:, P:T], mk, start=True, stop=False)
                    MM(PS[:, BANK_MLA, P:384], mqr[:, P:T], mkr, start=False, stop=True).then_inc(S["mla_s"], 1)
                    pe.wait_ge(S["e_normed"], n1)
                    for t in range(2):
                        ins = MM(PS[:, BANK_MEM, t * T:(t + 1) * T], eq[:, t * P:(t + 1) * P], memk[:, i, :],
                                 start=True, stop=True)
                    ins.then_inc(S["e_s"], 1)
                    feature_pair(base, B_GATE + 4, O_GATE + 2, hb)
                    pe.wait_ge(S["sb_lkm"], n1)
                    MM(PS[:, BANK_SB, 0:384], later, lk, start=True, stop=False)
                    MM(PS[:, BANK_SB, P:T], ones, lk[:, T:384], start=False, stop=True).then_inc(S["sb_later"], 1)
                    pe.wait_ge(S["mla_pn"], n1 * 2)
                    for k in range(3):
                        ins = nc.tensor.transpose(PS[:, BANK_MLA, k * P:(k + 1) * P], mP[:, k * P:(k + 1) * P], ident)
                    ins.then_inc(S["mla_transposed"], 1)
                    pe.wait_ge(S["e_pn"], n1 * 2)
                    for k in range(2):
                        for t in range(2):
                            ins = nc.tensor.transpose(PS[:, BANK_MEM, (2 * k + t) * P:(2 * k + t + 1) * P],
                                                      eP[:, (2 * t + k) * P:(2 * t + k + 1) * P], ident)
                    ins.then_inc(S["e_transposed"], 1)
                    feature_pair(base, B_GATE + 6, O_GATE + 3, hb)
                    pe.wait_ge(S["vh_ready"], n1)
                    pe.wait_ge(S["mla_PT"], n1)
                    weighted(BANK_MLA, 2, mPT).then_inc(S["mla_pv"], 1)
                    pe.wait_ge(S["e_PT"], n1)
                    MM(PS[:, BANK_MEM, 0:T], vh[:, 4, :], ePT[:, 0:T], start=True, stop=False)
                    MM(PS[:, BANK_MEM, 0:T], vh[:, 5, :], ePT[:, T:2 * T], start=False, stop=True)\
                        .then_inc(S["e_pv"], 1)
                    pe.wait_ge(S["sb_w"], n1)
                    weighted(BANK_SB, 0, lw).then_inc(S["sb_pv"], 1)
                for u in range(2):
                    j0 = 2 - 2 * u
                    if u == 0:
                        pe.wait_ge(S["mla_lo"], l * 4 + 5)
                        pe.wait_ge(S["e_lo"], l * 4 + 5)
                    else:
                        pe.wait_ge(S["sb_lo"], l * 4 + 5)
                        pe.wait_ge(S["b0lo_ready"], l1)
                    for c in range(4):
                        o = O_BRANCH + 4 * u + c
                        q = turn(o, lh)
                        for m in range(2):
                            b = B_BRANCH + 8 * u + 2 * c + m
                            arrived(lb, b)
                            for s in range(2):
                                for kb in range(4):
                                    w = slice((4 * s + kb) * P, (4 * s + kb + 1) * P)
                                    ins = split(PS[:, q + m, s * T:(s + 1) * T], whi[:, b % RING, w], wlo[:, b % RING, w],
                                                bhi[j0 + s][:, kb, :], blo[j0 + s][:, kb, :], kb == 0, kb == 3)
                            ins.then_inc(S["block_done"], 1)
                        if u == 0 and c == 0:
                            pe.wait_ge(S["conv_tap"], l * (4 * 32) + (4 * 32 + 1))
                            for k in range(4):
                                ins = MM(PS[:, BANK_NORM, 0:T], ones, ypad[:, k, PAD:PAD + T], start=k == 0, stop=k == 3)
                            ins.then_inc(S["ln_mean"], 1)
                        if u == 0 and c == 1:
                            pe.wait_ge(S["ln_sq"], l1)
                            for k in range(4):
                                ins = MM(PS[:, BANK_NORM, 0:T], ones, ysq[:, k * T:(k + 1) * T], start=k == 0, stop=k == 3)
                            ins.then_inc(S["ln_var"], 1)
                pe.wait_ge(S["mergedlo_ready"], l * 4 + 4)
                for c in range(4):
                    q = turn(O_OUT + c, lh)
                    for m in range(2):
                        feature_block(lb, B_OUT + 2 * c + m, PS[:, q + m, 0:T], hhi, hlo, range(KB))
                        if m == 0 and c:
                            x_sums(c - 1, l * 12 + (4 + 4 + c))
                x_sums(3, l * 12 + (4 + 4 + 4))
                for k in range(KB):
                    normed(2)(k)
                ffn_in(l, B_G1, O_G1)
                ffn_out(l, B_G2, O_G2, 8, 8)
                sums_all(l, 8)
            pe.wait_ge(S["x_sq"], 4 + 12 * DEPTH)


def _features(w, cols):
    return [w[:, c:c + P].reshape(-1, P, P).transpose(1, 0, 2).reshape(P, BLK) for c in cols]


def _tokens(w, cols):
    return [w[r:r + 512, c:c + 256].reshape(4, P, 256).transpose(1, 0, 2).reshape(P, BLK)
            for c in cols for r in (0, 512)]


def _ffn(w_in, w_out):
    cols = [half + c + m for c in range(0, FFN, 256) for half in (0, FFN) for m in (0, P)]
    out = _features(w_in, cols)
    for c in range(0, D_MODEL, 256):
        for rows in (0, 1024):
            out += _features(w_out[rows:rows + 1024], (c, c + P))
    return out


def _small(w, picks):
    blocks = w.reshape(-1, P, w.shape[1])
    return np.concatenate([b[:, c:c + n] for c, n in picks for b in blocks], axis=1)


def _layer_stream(l, a):
    w = a["w_in"][l]
    conv, sbq, sbv = 0, 1024, 1024 + 2 * 512
    qlat = 1024 + 3 * 512
    kr, memq = qlat + 2 * LORA, qlat + 2 * LORA + ROPE
    gate = memq + 512
    kv = a["mem_w_kv"][l]
    out = _ffn(a["ffn1_w_in"][l], a["ffn1_w_out"][l])
    out += _features(kv, range(0, 512, P)) + _tokens(kv, (512, 768))
    out += _features(w, [conv + c + part + m for c in (0, 256) for part in (0, CONV_CH) for m in (0, P)])
    out += _features(w, range(sbq, sbq + 1024, P)) + _tokens(w, (sbv, sbv + 256))
    out += _features(w, range(qlat, qlat + 512, P)) + _features(w, range(memq, memq + 512, P))
    uq, ukv, hd = a["mla_w_uq"][l], a["mla_w_ukv"][l], HEAD_DIM
    krw = w[:, kr:kr + ROPE].reshape(KB, P, ROPE).transpose(1, 0, 2).reshape(P, KB * ROPE)
    out.append(np.concatenate([krw, _small(uq, [(h * (hd + ROPE) + hd, ROPE) for h in range(HEADS)])], axis=1))
    out.append(_small(uq, [(h * (hd + ROPE), hd) for h in range(HEADS)]))
    out.append(_small(ukv, [(h * 2 * hd, hd) for h in range(HEADS)]))
    v = ukv.reshape(2, P, HEADS, 2, hd)[:, :, :, 1, :].reshape(2, P, HEADS * hd)
    out.append(v.transpose(1, 0, 2).reshape(P, BLK))
    out += _features(w, range(gate, gate + N_BRANCH * D_MODEL, P))
    wb = a["w_branch"][l].reshape(N_BRANCH * 512, D_MODEL)
    out += _features(wb[1024:], range(0, D_MODEL, P)) + _features(wb[:1024], range(0, D_MODEL, P))
    out += _features(a["w_out"][l], range(0, D_MODEL, P))
    return out + _ffn(a["ffn2_w_in"][l], a["ffn2_w_out"][l])


def _layer_params(l, a):
    def col(v):
        return v.reshape(-1, P).T

    def rope(v):
        return np.concatenate([v[HEAD_DIM:], v[HEAD_DIM:]]).reshape(1, P).T

    conv = [np.concatenate([a["conv_dw"][l][:, k * P:(k + 1) * P].T, a["conv_b"][l][k * P:(k + 1) * P, None]], axis=1)
            for k in range(4)]
    mq, mk = a["mla_q_hnorm"][l], a["mla_k_hnorm"][l]
    return np.concatenate(
        [col(a[n][l]) for n in ("ffn1_norm", "mix_norm", "ffn2_norm", "mem_norm")] + conv
        + [col(a[n][l]) for n in ("conv_ln_g", "conv_ln_b", "sb_q_hnorm", "sb_k_hnorm", "mla_q_norm", "mla_kv_norm")]
        + [col(mq[:HEAD_DIM]), rope(mq), col(mk[:HEAD_DIM]), rope(mk)]
        + [col(a[n][l]) for n in ("mem_q_hnorm", "mem_k_hnorm")], axis=1)


def _constants():
    r = np.arange(P)
    quarter, j = r // 32, r % 32
    row_a, row_b = np.array([0, 1, 1, 0])[quarter] * 32 + j, np.array([1, 0, 0, 1])[quarter] * 32 + j
    freq = np.float32(ROPE_BASE) ** (-np.arange(0, ROPE, 2, dtype=np.float32) / np.float32(ROPE))
    cols = [np.array(c, np.float64)[quarter][:, None] for c in ([1, 1, 0, 0], [0, 0, 1, -1], [-1, 1, 1, -1])]
    return np.concatenate(
        [np.ones((P, P)), np.full((P, P), 0.5), r[:, None] > r[None, :], np.eye(P), r[:, None] < r[None, :],
         r[:, None] == row_a[None, :], r[:, None] == row_b[None, :],
         np.full((P, 1), EPS), np.ones((P, 1)), freq[j][:, None]] + cols, axis=1).astype(np.float32)


def kernel(**inputs):
    import concourse.bacc as bacc
    from concourse.bass_utils import run_bass_kernel_spmd as run

    a = {n: np.asarray(v) for n, v in inputs.items()}
    blocks = [b for l in range(DEPTH) for b in _layer_stream(l, a)]
    arrays = {
        "stream": np.stack(blocks + blocks[:AHEAD]),
        "xT": np.ascontiguousarray(a["x"][0].T),
        "memT": np.ascontiguousarray(a["mem"][0].T),
        "positions": np.ascontiguousarray(a["positions"]),
        "params": np.stack([_layer_params(l, a) for l in range(DEPTH)]),
        "consts": _constants(),
    }
    nc = bacc.Bacc("TRN2", target_bir_lowering=False, num_devices=1)
    args = [nc.dram_tensor(n, v.shape, mybir.dt.from_np(v.dtype), kind="ExternalInput").ap() for n, v in arrays.items()]
    args.append(nc.dram_tensor("outT", (D_MODEL, SEQ), mybir.dt.float32, kind="ExternalOutput").ap())
    build(nc, *args)
    r = run(nc, [arrays], core_ids=[0])
    return np.ascontiguousarray(r.results[0]["outT"].T).reshape(1, SEQ, D_MODEL)
```

```python
import numpy as np

import concourse.bass as bass
from concourse import mybir
from contextlib import ExitStack

D_MODEL, SEQ, DEPTH, MEM_LEN = 1024, 256, 2, 256
FFN, CONV_CH, TAPS, HEADS, HEAD_DIM = 2048, 512, 31, 4, 128
LORA, ROPE, CHUNK, N_BRANCH, EPS = 256, 64, 64, 4, 1e-6
ROPE_BASE = 10000.0
P = 128
T = SEQ
KB = D_MODEL // P
PAD = TAPS - 1

BLK = 1024
RING = 4
AHEAD = 3
B_F1 = 0
B_F2 = B_F1 + 32
B_MEM = B_F2 + 16
B_LAT = B_MEM + 8
B_CONV = B_LAT + 4
B_UP = B_CONV + 8
B_SBQ = B_UP + 4
B_MEMQ = B_SBQ + 8
B_SBV = B_MEMQ + 4
B_GATE = B_SBV + 4
B_BRANCH = B_GATE + 32
B_OUT = B_BRANCH + 16
B_G1 = B_OUT + 8
B_G2 = B_G1 + 32
NBLK = B_G2 + 16
TURNS = NBLK // RING
assert NBLK == RING * TURNS

O_F1 = 0
O_F2 = O_F1 + 16
O_MEM = O_F2 + 4
O_LAT = O_MEM + 4
O_CONV = O_LAT + 2
O_UP = O_CONV + 4
O_SBQ = O_UP + 4
O_MEMQ = O_SBQ + 4
O_SBV = O_MEMQ + 2
O_GATE = O_SBV + 2
O_BRANCH = O_GATE + 16
O_OUT = O_BRANCH + 8
O_G1 = O_OUT + 4
O_G2 = O_G1 + 16
NOUT = O_G2 + 4
assert NOUT % 2 == 0

R_MEM, R_MIX, R_MEMK, R_LAT, R_MQ, R_MK, R_SBQ, R_SBK, R_EQ, R_CONV, R_FFN2, R_NEXT = range(12)
NROOT = 12

C_FFN1, C_MIX, C_FFN2, C_MEM = 0, KB, 2 * KB, 3 * KB
C_CONV = 4 * KB
CONVW = TAPS + 1
C_LNG = C_CONV + 4 * CONVW
C_LNB = C_LNG + 4
C_SBQ = C_LNB + 4
C_SBK = C_SBQ + 1
C_QLAT = C_SBK + 1
C_KVLAT = C_QLAT + 2
C_MQN, C_MQR, C_MKN, C_MKR = C_KVLAT + 2, C_KVLAT + 3, C_KVLAT + 4, C_KVLAT + 5
C_EQ, C_EK = C_KVLAT + 6, C_KVLAT + 7
C_NEXT = C_EK + 1
NPAR = C_NEXT + KB

K_ONES, K_HALF, K_LATER, K_IDENT, K_STRICT, K_PA, K_PB = (P * i for i in range(7))
K_EPS, K_ONE, K_FREQ, K_QC, K_QS, K_KS = (7 * P + i for i in range(6))
NCONST = 7 * P + 6
ROUNDER = 1.5 * 2.0 ** 23


def build(nc, stream, xT, memT, positions, params, consts, outT):
    F32, F32R, I32 = mybir.dt.float32, mybir.dt.float32r, mybir.dt.int32
    ALU, ACT, AX = mybir.AluOpType, mybir.ActivationFunctionType, mybir.AxisListType
    SB_SCALE = float(HEAD_DIM) ** -0.5
    MLA_SCALE = float(HEAD_DIM + ROPE) ** -0.5
    TOTAL = DEPTH * NBLK + AHEAD
    BANK_SB, BANK_MLA, BANK_MEM, BANK_NORM = 4, 5, 6, 7

    ctx = ExitStack()
    with ctx:
        def sb(name, shape, dt=F32):
            return ctx.enter_context(nc.sbuf_tensor(name, shape, dt))

        def over(name, shape, dt=F32):
            with nc.sbuf_tensor(name, shape, dt) as t:
                return t

        def sem(name):
            return ctx.enter_context(nc.semaphore(name))

        raw = sb("raw", [P, RING, BLK])
        whi = sb("whi", [P, RING, BLK], F32R)
        wlo = sb("wlo", [P, RING, BLK], F32R)
        x = sb("x", [P, KB, T])
        hhi = sb("hhi", [P, KB, T], F32R)
        hlo = sb("hlo", [P, KB, T], F32R)
        hf = sb("hf", [P, KB, T])
        gates = over("gates", [P, N_BRANCH, KB, T])
        acthi = sb("acthi", [P, 2 * KB, T], F32R)
        actlo = sb("actlo", [P, 2 * KB, T], F32R)
        ypad = over("ypad", [P, 4, PAD + T])
        b0hi, b0lo = sb("b0hi", [P, 4, T], F32R), sb("b0lo", [P, 4, T], F32R)
        b1hi, b1lo = sb("b1hi", [P, 4, T], F32R), sb("b1lo", [P, 4, T], F32R)
        mlaqk = over("mlaqk", [P, 4, 4, T])
        b2hi, b2lo = sb("b2hi", [P, 4, T], F32R), sb("b2lo", [P, 4, T], F32R)
        sb("mla_k_room", [P, 2, 4, T])
        memq = over("memq", [P, 4, T])
        b3hi, b3lo = sb("b3hi", [P, 4, T], F32R), sb("b3lo", [P, 4, T], F32R)
        bhi, blo = [b0hi, b1hi, b2hi, b3hi], [b0lo, b1lo, b2lo, b3lo]
        lathi, latlo = b1hi, b1lo
        vall = sb("vall", [P, 6, 4 * HEAD_DIM])
        memk = sb("memk", [P, 4, T])
        krsq, krot, qtab = sb("krsq", [P, T]), sb("krot", [P, T]), sb("qtab", [P, T])
        cosT, sinK, ropeQ = sb("cosT", [P, T]), sb("sinK", [P, T]), sb("ropeQ", [P, T])
        con = sb("con", [P, NCONST])
        par = sb("par", [P, NPAR])
        stat = sb("stat", [P, 16])
        work = sb("work", [P, 6144])
        PS = ctx.enter_context(nc.psum_tensor("PS", [P, 8, 512], F32))

        h_hi, h_lo = [hhi[:, k, :] for k in range(KB)], [hlo[:, k, :] for k in range(KB)]
        act_hi, act_lo = [acthi[:, k, :] for k in range(2 * KB)], [actlo[:, k, :] for k in range(2 * KB)]
        m_hi = [t[:, k, :] for t in (b2hi, b3hi) for k in range(4)]
        m_lo = [t[:, k, :] for t in (b2lo, b3lo) for k in range(4)]
        m_hi2 = [t[:, k:k + 2, :] for t in (b2hi, b3hi) for k in (0, 2)]
        m_lo2 = [t[:, k:k + 2, :] for t in (b2lo, b3lo) for k in (0, 2)]

        ones, halves, later = con[:, K_ONES:K_ONES + P], con[:, K_HALF:K_HALF + P], con[:, K_LATER:K_LATER + P]
        ident = con[:, K_IDENT:K_IDENT + P]
        strict2 = con[:, K_STRICT:K_STRICT + P].rearrange("p (a n) -> p a n", a=1).broadcast_to([P, 2, P])
        permA, permB = con[:, K_PA:K_PA + P], con[:, K_PB:K_PB + P]
        eps, one = con[:, K_EPS:K_EPS + 1], con[:, K_ONE:K_ONE + 1]

        def rows(ap, n):
            return ap.rearrange("p (a n) -> p a n", a=n)

        def each_of(ap, n):
            return rows(ap, 1).broadcast_to([P, n, T])

        def f(ap):
            return ap.bitcast(F32)

        def wide(t):
            return t[:, 0:KB, :].rearrange("p k n -> p (k n)").rearrange("p (r a n) -> p r a n", a=2, n=ROPE)

        def runs(ap):
            return ap.rearrange("p (r a n) -> p r a n", a=1, n=ROPE).broadcast_to([P, BLK // ROPE, 2, ROPE])

        def w2(a):
            return rows(work[:, a:a + 2 * T], 2)

        def w4(a):
            return rows(work[:, a:a + 4 * T], 4)

        def two_banks(tile):
            return rows(tile.rearrange("p k n -> p (k n)"), 2)

        def flat(tile):
            return tile.rearrange("p k n -> p (k n)")

        def at(i, k, n=1):
            return slice(i + k, i + k + n) if isinstance(i, int) else bass.ds(i + k, n)

        silu, up32, act32 = [w2(0), w2(512)], [w2(1024), w2(1536)], [w2(2048), w2(2560)]
        mem32, memr, xr = rows(work[:, 3072:5120], KB), work[:, 5120:5376], work[:, 5376:5632]
        memksq, memkr = w4(0), w4(1024)
        lat32, latsq, latr = w4(2048), w4(3072), work[:, 4096:4608]
        glu = [w2(4608), w2(5120)]
        krt, krg = w2(3072), work[:, 3584:3840]
        mqsq, mqrsq, mqR = w4(0), w4(1024), w4(2048)
        mksq, mkR = w4(4864), w4(3840)
        sbqsq, sbqR = w4(0), w4(1024)
        sbksq, sbkR = w4(2048), w4(0)
        eqsq, eqR = w4(3840), w4(4864)
        vh = rows(work[:, 0:768], 6)
        sbk, mq, mqr, eq = (work[:, 768 + T * i:768 + T * (i + 1)] for i in range(4))
        sbL, relu, lk, lw = (work[:, 1792 + 384 * i:1792 + 384 * (i + 1)] for i in range(4))
        mP, mPT = work[:, 3328:3712], work[:, 3712:4096]
        eP, ePT = work[:, 4096:4608], work[:, 4608:5120]
        acc = [work[:, 5120:5376], work[:, 5376:5632]]
        yc, ysq, yr, y32 = w4(0), w4(1024), work[:, 2048:2304], w4(2304)
        prod = [[w2(3328), w2(3840)], [w2(4352), w2(4864)]]

        names = """act_waited dve_waited pe_waited pool_waited x0_loaded x1_loaded par0_loaded par_loaded mem_loaded const_loaded
            pos_loaded out_stored hi_ready block_done rope_step
            x_sq sq_added ssq_ready root_ln rms_ready hf_ready hhi_ready hlo_ready
            silu_ready act_ready acthi_ready actlo_ready
            mem_sq mem_ssq mem_r memh_ready memhi_ready memlo_ready pad_zeroed glu_ready
            lat_sq lat_ssq lat_r lat_normed lathi_ready latlo_ready
            widehi_ready widelo_ready kr_ready krsq_ready krg_ready kr_permuted krt_ready krot_ready qtab_ready
            memk_sq memk_ssq memk_r memk_normed mq_sq mq_sq_all mq_ssq mq_r mq_tabled mq_normed mk_sq mk_sq_all mk_ssq mk_r mk_normed
            sbq_sq sbq_ssq sbq_r sbq_normed sbk_sq sbk_ssq sbk_r sbk_normed eq_sq eq_ssq eq_r eq_normed
            fixed_ready vh_ready sb_z mla_s e_s
            sb_abs sb_exp sb_L sb_relu sb_lk sb_a sb_lkm sb_later sb_logw sb_expw sb_w sb_pv sb_hi sb_lo
            mla_masked mla_max mla_neg mla_p mla_rec mla_pn mla_transposed mla_PT mla_pv mla_hi mla_lo
            e_max e_neg e_p e_rec e_pn e_transposed e_PT e_pv e_hi e_lo
            conv_tap ln_mean ln_c ln_sq ln_var ln_r ln_n ln_silu b0hi_ready b0lo_ready
            gate_sig first_ready prod_added merged_ready mergedhi_ready mergedlo_ready""".split()
        S = {n: sem(n) for n in names}
        raw_ready = [sem(f"raw_ready{i}") for i in range(RING)]
        lo_ready = [sem(f"lo_ready{i}") for i in range(RING)]
        read = [sem(f"group_read{i}") for i in range(2)]
        HALF_OUT = NOUT // 2

        def read_value(o, half_base):
            return half_base + (o // 2 + 2)

        def diag2(ap):
            return ap.rearrange("p (a n) -> p a n", n=P)[:, 0:3:2, :]

        block = ctx.enter_context(nc.Block())

        @block.sync
        def _(sp):
            xin = xT.rearrange("(k p) t -> p k t", p=P)
            sp.dma_start(par[:, :], params[0, :, :]).then_inc(S["par0_loaded"], 16)
            for b in range(2):
                sp.dma_start(raw[:, b, :], stream[b, :, :]).then_inc(raw_ready[b], 16)
                sp.dma_start(x[:, 4 * b:4 * b + 4, :], xin[:, 4 * b:4 * b + 4, :]).then_inc(S[f"x{b}_loaded"], 16)
            for b in range(2, RING):
                sp.dma_start(raw[:, b, :], stream[b, :, :]).then_inc(raw_ready[b], 16)
            with sp.Fori(0, DEPTH * TURNS - 1) as t:
                for k in range(RING):
                    sp.wait_ge(lo_ready[k], t + 1)
                    sp.dma_start(raw[:, k, :], stream[bass.ds(t * RING + (k + RING), 1), :, :]
                                 .rearrange("a p n -> p (a n)")).then_inc(raw_ready[k], 16)
            for k in range(AHEAD):
                sp.wait_ge(lo_ready[k], DEPTH * TURNS)
                sp.dma_start(raw[:, k, :], stream[DEPTH * NBLK + k, :, :]).then_inc(raw_ready[k], 16)
            for o in (O_G2 + 2, O_G2 + 3):
                sp.wait_ge(read[o % 2], read_value(o, (DEPTH - 1) * HALF_OUT))
            sp.dma_start(outT.rearrange("(k p) t -> p k t", p=P), x[:, :, :]).then_inc(S["out_stored"], 16)
            sp.wait_ge(S["out_stored"], 16)

        @block.gpsimd
        def _(pool):
            TT = nc.gpsimd.tensor_tensor

            def squares_sum(value, s, first):
                for c in range(1, 4):
                    pool.wait_ge(S[s], value(c))
                    pool.wait_ge(S["sq_added"], first + (c - 1))
                    TT(hf[:, 0:2, :], hf[:, 0:2, :], hf[:, 2 * c:2 * c + 2, :], ALU.add).then_inc(S["sq_added"], 1)

            def lo(base, b):
                b += AHEAD
                pool.wait_ge(S["hi_ready"], base * RING + (b + 1))
                TT(wlo[:, b % RING, :], raw[:, b % RING, :], f(whi[:, b % RING, :]), ALU.subtract)\
                    .then_inc(lo_ready[b % RING], 1)

            def ffn_in_step(l, it, f0):
                n0 = pool.snap(l * 16 + it * 2)
                for j in range(2):
                    n = f0 + j + 1
                    pool.wait_ge(S["silu_ready"], n0 + n)
                    pool.wait_ge(read[1], l * HALF_OUT + it * 2 + ((O_F1 if f0 == 0 else O_G1) // 2 + j + 2))
                    pool.wait_ge(S["actlo_ready"], n0 + n)
                    TT(act32[j], up32[j], silu[j], ALU.mult).then_inc(S["act_ready"], 1)
                    pool.wait_ge(S["acthi_ready"], n0 + n)
                    pool.sem_inc(S["pool_waited"], 1)
                    pair = at(it * 4, 2 * j, 2)
                    TT(actlo[:, pair, :], act32[j], f(acthi[:, pair, :]), ALU.subtract).then_inc(S["actlo_ready"], 1)

            def ffn_in(l, f0, between=None):
                ffn_in_step(l, 0, f0)
                if between:
                    between()
                with pool.Fori(1, 4) as it:
                    ffn_in_step(l, it, f0)

            pool.sem_inc(S["act_ready"], 2)
            pool.sem_inc(S["actlo_ready"], 2)
            pool.sem_inc(S["sq_added"], 1)
            pool.dma_start(con[:, :], consts).then_inc(S["const_loaded"], 16)
            pool.dma_start(ropeQ[:, :].bitcast(I32), positions.broadcast_to([P, T])).then_inc(S["pos_loaded"], 16)
            with pool.Fori(0, DEPTH) as l:
                squares_sum(lambda c: l * 12 + (c + 1), "x_sq", l * 12 + 1)
                pool.wait_ge(S["hlo_ready"], l * (3 * KB) + KB)
                pool.sem_inc(S["pool_waited"], 1)
                pool.dma_start(mem32, memT.rearrange("(k p) t -> p k t", p=P)).then_inc(S["mem_loaded"], 16)
                pool.dma_start(par[:, :], params[bass.ds(l, 1), :, :].rearrange("a p n -> p (a n)"))\
                    .then_inc(S["par_loaded"], 16)
                ffn_in(l, 0, lambda: squares_sum(lambda c: l + 1, "mem_sq", l * 12 + 4))
                squares_sum(lambda c: l * 12 + (4 + c + 1), "x_sq", l * 12 + 7)
                half = slice(0, ROPE)
                pool.wait_ge(S["mq_sq"], l * 2 + 2)
                TT(mqsq[half], mqsq[half], mqrsq[half], ALU.add).then_inc(S["mq_sq_all"], 1)
                pool.wait_ge(S["mk_sq"], l + 1)
                pool.wait_ge(S["krsq_ready"], l + 1)
                TT(mksq[half], mksq[half], rows(krsq[half, :], 1).broadcast_to([ROPE, HEADS, T]), ALU.add).then_inc(S["mk_sq_all"], 1)
                with pool.Fori(0, HEADS) as i:
                    base = pool.snap(l * TURNS + i * 2)
                    for k in (0, 4):
                        lo(base, B_GATE + k)
                for u in range(2):
                    for c in range(4 - u):
                        if u == 0 and c % 2 == 0:
                            lo(l * TURNS, B_BRANCH + 2 * c)
                        o = O_BRANCH + 4 * u + c
                        m, p = hf[:, 2 * c:2 * c + 2, :], prod[c % 2]
                        pool.wait_ge(read[o % 2], read_value(o, l * HALF_OUT))
                        if u == 1:
                            pool.wait_ge(S["merged_ready"], l * 8 + (c + 1))
                            TT(m, m, p[0], ALU.add).then_inc(S["prod_added"], 1)
                            pool.wait_ge(S["prod_added"], l * 4 + (c + 1))
                        TT(m, m, p[1], ALU.add).then_inc(S["merged_ready"], 1)
                squares_sum(lambda c: l * 12 + (8 + c + 1), "x_sq", l * 12 + 10)
                ffn_in(l, 8)

        @block.scalar
        def _(act):
            A = nc.scalar.activation

            def exp_ln_table():
                nc.scalar.preload_act_table_set("natural_log_exp_and_others")

            def level():
                act.sem_inc(S["act_waited"], 1)

            def hi(base, b):
                b += AHEAD
                act.wait_ge(raw_ready[b % RING], base * 16 + 16 * (b // RING + 1))
                act.wait_ge(S["block_done"], base * RING + (b + 1))
                A(whi[:, b % RING, :], raw[:, b % RING, :], ACT.Copy).then_inc(S["hi_ready"], 1)

            def group(o, base, b):
                act.wait_ge(S["block_done"], base * RING + (b + 1 + RING))
                return 2 * (o % 2)

            def root(sums, dst, n, s_sum, v, number, s_r):
                act.wait_ge(S[s_sum], v)
                A(dst, sums, ACT.Ln, bias=eps, scale=1.0 / n).then_inc(S["root_ln"], 1)
                act.wait_ge(S["root_ln"], number)
                A(dst, dst, ACT.Exp, scale=-0.5).then_inc(S[s_r], 1)

            def x_root(value, number):
                root(PS[:, BANK_NORM, 0:T], xr, D_MODEL, "ssq_ready", value, number, "rms_ready")

            def x_high(i, k, col):
                for m in (0, 1):
                    A(hhi[:, at(i, k + m), :].rearrange("p a n -> p (a n)"),
                      x[:, at(i, k + m), :].rearrange("p a n -> p (a n)"), ACT.Identity,
                      scale=par[:, at(i, col + k + m)]).then_inc(S["hhi_ready"], 1)
                A(hf[:, at(i, k, 2), :], x[:, at(i, k, 2), :], ACT.Square).then_inc(S["x_sq"], 1)

            def act_high(n0, n, place):
                act.wait_ge(S["act_ready"], n0 + (n + 2))
                level()
                A(acthi[:, place, :], act32[(n + 1) % 2], ACT.Copy).then_inc(S["acthi_ready"], 1)

            def ffn_in_step(l, it, b0, o0, f0, value=None, number=None):
                base, hb = act.snap(l * TURNS + it * 2), act.snap(l * HALF_OUT + it * 2)
                n0 = act.snap(l * 16 + it * 2)
                for j in range(2):
                    hi(base, b0 + 4 * j)
                    hi(base, b0 + 4 * j + 1)
                    if value is not None and j == 0:
                        x_root(value, number)
                        nc.scalar.preload_act_table(ACT.Silu)
                    if value is None or j:
                        act_high(n0, f0 + j, at(it * 4, 2 * j - 2, 2))
                    o = o0 + 2 * j
                    act.wait_ge(read[0], read_value(o, hb))
                    A(silu[j], silu[j], ACT.Silu).then_inc(S["silu_ready"], 1)
                    hi(base, b0 + 4 * j + 2)
                    hi(base, b0 + 4 * j + 3)
                    if f0 == 0 and value is not None and j == 1:
                        act.wait_ge(S["mem_loaded"], l * 16 + 16)
                        A(hf[:, :, :], mem32, ACT.Square).then_inc(S["mem_sq"], 1)

            def ffn_in(l, b0, o0, f0, value, number):
                ffn_in_step(l, 0, b0, o0, f0, value, number)
                with act.Fori(1, 4) as it:
                    ffn_in_step(l, it, b0, o0, f0)
                act_high(act.snap(l * 16), f0 + 8, slice(2 * KB - 2, 2 * KB))

            def ffn_out_step(l, it, b0, o0, col=None):
                base, hb = act.snap(l * TURNS + it * 2), act.snap(l * HALF_OUT + it)
                for j in range(2):
                    for k in range(4):
                        hi(base, b0 + 4 * j + k)
                    act.wait_ge(read[(o0 + j) % 2], read_value(o0 + j, hb))
                    level()
                    if col is None:
                        two = at(it * 4, 2 * j, 2)
                        A(hf[:, two, :], x[:, two, :], ACT.Square).then_inc(S["x_sq"], 1)
                    else:
                        x_high(it * 4, 2 * j, col)

            act.sem_inc(read[0], 1)
            act.sem_inc(read[1], 1)
            hi(0, -AHEAD)
            act.wait_ge(S["par0_loaded"], 16)
            for c in range(4):
                if c % 2 == 0:
                    act.wait_ge(S[f"x{c // 2}_loaded"], 16)
                x_high(0, 2 * c, C_FFN1)
                if c < 2:
                    hi(0, c + 1 - AHEAD)
            act.wait_ge(S["const_loaded"], 16)
            act.wait_ge(S["rope_step"], 9)
            A(sinK[:, :], krsq[:, :], ACT.Sin).then_inc(S["rope_step"], 1)
            A(cosT[:, :], krot[:, :], ACT.Sin).then_inc(S["rope_step"], 1)
            exp_ln_table()
            with act.Fori(0, DEPTH) as l:
                lb, lh, lr = act.snap(l * TURNS), act.snap(l * HALF_OUT), act.snap(l * NROOT + 2)
                l1 = act.snap(l + 1)
                ffn_in(l, B_F1, O_F1, 0, l * 3 + 1, l * NROOT + 1)
                exp_ln_table()
                for step in range(2):
                    if step == 0:
                        root(PS[:, BANK_MEM, 0:T], memr, D_MODEL, "mem_ssq", l1, lr + R_MEM, "mem_r")
                    ffn_out_step(l, step, B_F2, O_F2)
                    if step == 0:
                        act.wait_ge(S["memh_ready"], l * KB + KB)
                        for c in range(4):
                            A(m_hi2[c], mem32[:, 2 * c:2 * c + 2, :], ACT.Copy).then_inc(S["memhi_ready"], 1)
                for c in range(4):
                    hi(lb, B_MEM + 2 * c)
                    hi(lb, B_MEM + 2 * c + 1)
                    o = O_MEM + c
                    q = group(o, lb, B_MEM + 2 * c + 1)
                    dst = memk[:, 2 * c:2 * c + 2, :] if c < 2 else vall[:, 4:6, (c - 2) * 256:(c - 1) * 256]
                    A(dst, PS[:, q:q + 2, 0:T], ACT.Copy).then_inc(read[o % 2], 1)
                    if c == 0:
                        x_root(l * 3 + 2, lr + R_MIX)
                    if c in (1, 2):
                        for k in range(4 * c - 4, 4 * c):
                            act.wait_ge(S["hf_ready"], l * KB + (k + 1))
                            A(hhi[:, k, :], hf[:, k, :], ACT.Copy).then_inc(S["hhi_ready"], 1)
                    if c == 1:
                        for e in (o - 1, o):
                            act.wait_ge(read[e % 2], read_value(e, lh))
                        A(memksq, memk[:, :, :], ACT.Square).then_inc(S["memk_sq"], 1)
                for c in range(2):
                    hi(lb, B_LAT + 2 * c)
                    if c == 0:
                        root(PS[:, 4:6, :], two_banks(memkr), HEAD_DIM, "memk_ssq", l1, lr + R_MEMK, "memk_r")
                    hi(lb, B_LAT + 2 * c + 1)
                    o = O_LAT + c
                    q = group(o, lb, B_LAT + 2 * c + 1)
                    A(lat32[:, 2 * c:2 * c + 2, :], PS[:, q:q + 2, 0:T], ACT.Copy).then_inc(read[o % 2], 1)
                for o in (O_LAT, O_LAT + 1):
                    act.wait_ge(read[o % 2], read_value(o, lh))
                A(latsq, lat32, ACT.Square).then_inc(S["lat_sq"], 1)
                act.wait_ge(S["pad_zeroed"], l1)
                for c in range(2):
                    for part in range(2):
                        b, o = B_CONV + 4 * c + 2 * part, O_CONV + 2 * c + part
                        hi(lb, b)
                        hi(lb, b + 1)
                        if c == 1 and part == 0:
                            act.wait_ge(S["lat_normed"], l * 4 + 4)
                            A(lathi[:, :, :], lat32, ACT.Copy).then_inc(S["lathi_ready"], 1)
                            act.wait_ge(S["hi_ready"], lb * RING + (B_UP + 1))
                            A(wide(acthi), runs(f(whi[:, B_UP % RING, :])), ACT.Copy).then_inc(S["widehi_ready"], 1)
                        q = group(o, lb, b + 1)
                        if part == 0:
                            A(ypad[:, 2 * c:2 * c + 2, PAD:PAD + T], PS[:, q:q + 2, 0:T], ACT.Copy)\
                                .then_inc(read[o % 2], 1)
                        else:
                            A(glu[c], PS[:, q:q + 2, 0:T], ACT.Sigmoid).then_inc(read[o % 2], 1)
                        if c == part == 0:
                            root(PS[:, BANK_MLA, :], latr, LORA, "lat_ssq", l1, lr + R_LAT, "lat_r")
                exp_ln_table()
                act.wait_ge(S["glu_ready"], l * 2 + 2)
                dsts = [mlaqk[:, 1, :, :], mlaqk[:, 0, :, :], mlaqk[:, 2, :, :], vall[:, 2:4, :]]
                squares = [(mqrsq, "mq_sq"), (mqsq, "mq_sq"), (mksq, "mk_sq")]
                for c in range(4):
                    hi(lb, B_UP + c)
                    if c == 0:
                        act.wait_ge(S["kr_ready"], l1)
                        A(krsq[:, :], PS[:, BANK_NORM, 0:T], ACT.Square).then_inc(S["krsq_ready"], 1)
                    o = O_UP + c
                    q = group(o, lb, B_UP + c)
                    src = PS[:, q:q + 2, :] if c == 3 else PS[:, q:q + 2, :].rearrange("p a (b n) -> p (a b) n", b=2)
                    A(dsts[c], src, ACT.Copy).then_inc(read[o % 2], 1)
                    if c < 3:
                        act.wait_ge(read[o % 2], read_value(o, lh))
                        A(squares[c][0], dsts[c], ACT.Square).then_inc(S[squares[c][1]], 1)
                stages = [(B_SBQ + 2 * c, O_SBQ + c, hf[:, 2 * c:2 * c + 2, :]) for c in range(4)]
                stages += [(B_MEMQ + 2 * c, O_MEMQ + c, memq[:, 2 * c:2 * c + 2, :]) for c in range(2)]
                stages += [(B_SBV + 2 * c, O_SBV + c, vall[:, 0:2, c * 256:(c + 1) * 256]) for c in range(2)]
                for c, (b, o, dst) in enumerate(stages):
                    hi(lb, b)
                    if c == 1:
                        root(PS[:, 4:6, :], two_banks(mqR), HEAD_DIM + ROPE, "mq_ssq", l1, lr + R_MQ, "mq_r")
                    if c == 2:
                        root(PS[:, 6:8, :], two_banks(mkR), HEAD_DIM + ROPE, "mk_ssq", l1, lr + R_MK, "mk_r")
                    if c == 4:
                        root(PS[:, 4:6, :], two_banks(sbqR), HEAD_DIM, "sbq_ssq", l1, lr + R_SBQ, "sbq_r")
                    if c == 5:
                        root(PS[:, 6:8, :], two_banks(sbkR), HEAD_DIM, "sbk_ssq", l1, lr + R_SBK, "sbk_r")
                    hi(lb, b + 1)
                    if c == 7:
                        root(PS[:, 4:6, :], two_banks(eqR), HEAD_DIM, "eq_ssq", l1, lr + R_EQ, "eq_r")
                    q = group(o, lb, b + 1)
                    A(dst, PS[:, q:q + 2, 0:T], ACT.Copy).then_inc(read[o % 2], 1)
                    if c in (1, 3, 5):
                        for e in (o - 1, o):
                            act.wait_ge(read[e % 2], read_value(e, lh))
                    if c == 1:
                        A(sbqsq, hf[:, 0:4, :], ACT.Square).then_inc(S["sbq_sq"], 1)
                    if c == 3:
                        act.wait_ge(S["mq_normed"], l * 2 + 2)
                        A(sbksq, hf[:, 4:8, :], ACT.Square).then_inc(S["sbk_sq"], 1)
                    if c == 5:
                        act.wait_ge(S["mk_normed"], l * 2 + 2)
                        A(eqsq, memq[:, :, :], ACT.Square).then_inc(S["eq_sq"], 1)
                for o in (O_SBV, O_SBV + 1):
                    act.wait_ge(read[o % 2], read_value(o, lh))
                act.wait_ge(S["mq_normed"], l * 2 + 2)
                act.wait_ge(S["sbk_normed"], l1)
                act.wait_ge(S["sbq_normed"], l1)
                act.wait_ge(S["eq_normed"], l1)
                with act.Fori(0, HEADS) as i:
                    n1 = act.snap(l * HEADS + i + 1)
                    base = act.snap(l * TURNS + i * 2)

                    def gate(g):
                        hi(base, B_GATE + 2 * g)
                        hi(base, B_GATE + 2 * g + 1)

                    def keep(g):
                        o = O_GATE + g
                        q = group(o, base, B_GATE + 2 * g + 1)
                        level()
                        A(gates[:, bass.ds(i, 1), 2 * g:2 * g + 2, :].rearrange("p a k n -> p (a k) n"),
                          PS[:, q:q + 2, 0:T], ACT.Copy).then_inc(read[o % 2], 1)

                    for dst, src in ((sbk, hf[:, bass.ds(i + 4, 1), :].rearrange("p a n -> p (a n)")),
                                     (mq, mlaqk[:, 0, i, :]), (mqr, mlaqk[:, 1, i, :]), (eq, memq[:, i, :])):
                        A(dst, src, ACT.Copy).then_inc(S["fixed_ready"], 1)
                    A(vh, vall[:, :, bass.ds(i * HEAD_DIM, HEAD_DIM)], ACT.Copy).then_inc(S["vh_ready"], 1)
                    gate(0)
                    keep(0)
                    act.wait_ge(S["sb_z"], n1)
                    A(sbL, PS[:, BANK_SB, 0:384], ACT.Abs, scale=SB_SCALE).then_inc(S["sb_abs"], 1)
                    A(relu, PS[:, BANK_SB, 0:384], ACT.Relu, scale=SB_SCALE).then_inc(S["sb_relu"], 1)
                    act.wait_ge(S["sb_abs"], n1)
                    A(sbL, sbL, ACT.Exp, scale=-1.0).then_inc(S["sb_exp"], 1)
                    act.wait_ge(S["sb_exp"], n1)
                    A(sbL, sbL, ACT.Ln, bias=one).then_inc(S["sb_L"], 1)
                    gate(1)
                    act.wait_ge(S["mla_neg"], n1)
                    A(mP[:, 0:P], PS[:, BANK_MLA, 0:P], ACT.Exp, scale=MLA_SCALE, bias=stat[:, 2:3],
                      accum_out=stat[:, 4:5]).then_inc(S["mla_p"], 1)
                    A(mP[:, P:384], PS[:, BANK_MLA, P:384], ACT.Exp, scale=MLA_SCALE, bias=stat[:, 3:4],
                      accum_out=stat[:, 5:6]).then_inc(S["mla_p"], 1)
                    act.wait_ge(S["e_neg"], n1)
                    for j in range(2):
                        A(eP[:, j * T:(j + 1) * T], PS[:, BANK_MEM, j * T:(j + 1) * T], ACT.Exp, scale=SB_SCALE,
                          bias=stat[:, 10 + j:11 + j], accum_out=stat[:, 12 + j:13 + j]).then_inc(S["e_p"], 1)
                    keep(1)
                    gate(2)
                    keep(2)
                    gate(3)
                    act.wait_ge(S["sb_logw"], n1)
                    A(lw, lw, ACT.Exp).then_inc(S["sb_expw"], 1)
                    act.wait_ge(S["mla_transposed"], n1)
                    A(mPT, PS[:, BANK_MLA, 0:384], ACT.Copy).then_inc(S["mla_PT"], 1)
                    act.wait_ge(S["e_transposed"], n1)
                    A(ePT, PS[:, BANK_MEM, :], ACT.Copy).then_inc(S["e_PT"], 1)
                    keep(3)
                    act.wait_ge(S["mla_pv"], n1)
                    level()
                    A(b2hi[:, i, :], PS[:, BANK_MLA, 0:T], ACT.Copy).then_inc(S["mla_hi"], 1)
                    act.wait_ge(S["e_pv"], n1)
                    level()
                    A(b3hi[:, i, :], PS[:, BANK_MEM, 0:T], ACT.Copy).then_inc(S["e_hi"], 1)
                    act.wait_ge(S["sb_pv"], n1)
                    level()
                    A(b1hi[:, i, :], PS[:, BANK_SB, 0:T], ACT.Copy).then_inc(S["sb_hi"], 1)
                for o in (O_GATE + 14, O_GATE + 15):
                    act.wait_ge(read[o % 2], read_value(o, lh))
                def merge_high(c):
                    act.wait_ge(S["merged_ready"], l * 8 + (4 + c + 1))
                    A(m_hi2[c], hf[:, 2 * c:2 * c + 2, :], ACT.Copy).then_inc(S["mergedhi_ready"], 1)

                for u in range(2):
                    for c in range(4):
                        hi(lb, B_BRANCH + 8 * u + 2 * c)
                        hi(lb, B_BRANCH + 8 * u + 2 * c + 1)
                        j0 = 2 - 2 * u
                        for e in ((2, 3) if (u, c) == (0, 2) else () if (u, c) == (0, 3) else (c,)):
                            for j in (j0, j0 + 1):
                                g = gates[:, j, 2 * e:2 * e + 2, :]
                                A(g, g, ACT.Sigmoid).then_inc(S["gate_sig"], 1)
                        if u == 0 and c == 0:
                            act.wait_ge(S["ln_c"], l1)
                            A(ysq, yc, ACT.Square).then_inc(S["ln_sq"], 1)
                        if u == 0 and c == 1:
                            exp_ln_table()
                            root(PS[:, BANK_NORM, 0:T], yr, CONV_CH, "ln_var", l1, lr + R_CONV, "ln_r")
                        if u == 0 and c == 2:
                            act.wait_ge(S["ln_n"], l1)
                            for k in range(4):
                                A(y32[:, k, :], yc[:, k, :], ACT.Silu,
                                  scale=par[:, C_LNG + k:C_LNG + k + 1], bias=par[:, C_LNB + k:C_LNB + k + 1])\
                                    .then_inc(S["ln_silu"], 1)
                        if u == 0 and c == 3:
                            act.wait_ge(S["ln_silu"], l * 4 + 4)
                            A(b0hi[:, :, :], y32, ACT.Copy).then_inc(S["b0hi_ready"], 1)
                        if u == 1 and c:
                            merge_high(c - 1)
                merge_high(3)
                exp_ln_table()
                for c in range(4):
                    hi(lb, B_OUT + 2 * c)
                    hi(lb, B_OUT + 2 * c + 1)
                    o = O_OUT + c
                    act.wait_ge(read[o % 2], read_value(o, lh))
                    act.wait_ge(S["mergedlo_ready"], l * 4 + 4)
                    x_high(0, 2 * c, C_FFN2)
                ffn_in(l, B_G1, O_G1, 8, l * 3 + 3, lr + R_FFN2)
                exp_ln_table()
                with act.Fori(0, 2) as it:
                    ffn_out_step(l, it, B_G2, O_G2, C_NEXT)

        @block.vector
        def _(dve):
            V = nc.vector
            STT, TT, TS = V.scalar_tensor_tensor, V.tensor_tensor, V.tensor_scalar

            def lo(base, b):
                b += AHEAD
                dve.wait_ge(S["hi_ready"], base * RING + (b + 1))
                TT(wlo[:, b % RING, :], raw[:, b % RING, :], f(whi[:, b % RING, :]), ALU.subtract)\
                    .then_inc(lo_ready[b % RING], 1)

            def group(o, base, b):
                dve.wait_ge(S["block_done"], base * RING + (b + 1 + RING))
                return 2 * (o % 2)

            def x_low(h0, i, k, col):
                for m in (0, 1):
                    dve.wait_ge(S["hhi_ready"], h0 + (k + m + 1))
                    STT(hlo[:, at(i, k + m), :], x[:, at(i, k + m), :], par[:, at(i, col + k + m)],
                        f(hhi[:, at(i, k + m), :]), ALU.mult, ALU.subtract).then_inc(S["hlo_ready"], 1)

            def ffn_in_step(l, it, b0, o0, f0, value=None):
                base, hb = dve.snap(l * TURNS + it * 2), dve.snap(l * HALF_OUT + it * 2)
                n0 = dve.snap(l * 16 + it * 2)
                for j in range(2):
                    for part, place in ((0, silu), (1, up32)):
                        lo(base, b0 + 4 * j + 2 * part)
                        lo(base, b0 + 4 * j + 2 * part + 1)
                        if value is not None and j == part == 0:
                            dve.wait_ge(S["rms_ready"], value)
                        o = o0 + 2 * j + part
                        q = group(o, base, b0 + 4 * j + 2 * part + 1)
                        dve.wait_ge(S["act_ready"], n0 + (f0 + j + 1))
                        TT(place[j], PS[:, q:q + 2, 0:T], each_of(xr, 2), ALU.mult).then_inc(read[part], 1)

            def ffn_in(l, b0, o0, f0, value):
                ffn_in_step(l, 0, b0, o0, f0, value)
                with dve.Fori(1, 4) as it:
                    ffn_in_step(l, it, b0, o0, f0)

            def update(o, base, b, two, scale):
                q = group(o, base, b)
                STT(x[:, two, :], PS[:, q:q + 2, 0:T], scale, x[:, two, :], ALU.mult, ALU.add).then_inc(read[o % 2], 1)

            def ffn_out_step(l, it, b0, o0, col=None):
                base = dve.snap(l * TURNS + it * 2)
                for j in range(2):
                    for k in range(4):
                        lo(base, b0 + 4 * j + k)
                    update(o0 + j, base, b0 + 4 * j + 3, at(it * 4, 2 * j, 2), 0.5)
                    if col is not None:
                        for e in (o0 + j,):
                            dve.wait_ge(read[e % 2], read_value(e, l * HALF_OUT + it))
                        x_low(l * (3 * KB) + it * 4 + 3 * KB, it * 4, 2 * j, col)

            def head_norm(tile, gain, r, s_r, v, s_normed):
                dve.wait_ge(S[s_r], v)
                STT(flat(tile), flat(tile), par[:, gain:gain + 1], flat(r), ALU.mult, ALU.mult).then_inc(S[s_normed], 1)

            for s in ("sb_lo", "mla_lo", "e_lo", "conv_tap"):
                dve.sem_inc(S[s], 1)
            dve.wait_ge(S["par0_loaded"], 16)
            lo(0, -AHEAD)
            for c in range(4):
                x_low(0, 0, 2 * c, C_FFN1)
                if c < 2:
                    lo(0, c + 1 - AHEAD)
            dve.wait_ge(S["pos_loaded"], 16)
            dve.wait_ge(S["const_loaded"], 16)

            def rope(step, ins):
                ins.then_inc(S["rope_step"], 1)
                dve.wait_ge(S["rope_step"], step)

            rope(1, V.tensor_copy(qtab[:, :], ropeQ[:, :].bitcast(I32)))
            rope(2, TS(krsq[:, :], qtab[:, :], con[:, K_FREQ:K_FREQ + 1], None, ALU.mult))
            rope(3, TS(krot[:, :], krsq[:, :], 1.0 / (2 * np.pi), ROUNDER, ALU.mult, ALU.add))
            rope(4, TS(krot[:, :], krot[:, :], ROUNDER, None, ALU.subtract))
            rest, parts = 2 * np.pi, []
            for bits in (5, 13):
                parts.append(float(np.floor(rest * 2.0 ** bits) / 2.0 ** bits))
                rest -= parts[-1]
            for k, part in enumerate(parts + [float(rest)]):
                rope(5 + k, STT(krsq[:, :], krot[:, :], -part, krsq[:, :], ALU.mult, ALU.add))
            rope(8, STT(krot[:, :], krsq[:, :], -1.0, krsq[:, :], ALU.mult, ALU.max))
            rope(9, TS(krot[:, :], krot[:, :], -1.0, np.pi / 2, ALU.mult, ALU.add))
            dve.wait_ge(S["rope_step"], 11)
            rope(12, TS(ropeQ[:, :], cosT[:, :], con[:, K_QC:K_QC + 1], None, ALU.mult))
            rope(13, STT(ropeQ[:, :], sinK[:, :], con[:, K_QS:K_QS + 1], ropeQ[:, :], ALU.mult, ALU.add))
            rope(14, TS(sinK[:, :], sinK[:, :], con[:, K_KS:K_KS + 1], None, ALU.mult))
            with dve.Fori(0, DEPTH) as l:
                lb, lh = dve.snap(l * TURNS), dve.snap(l * HALF_OUT)
                l1 = dve.snap(l + 1)
                ffn_in(l, B_F1, O_F1, 0, l * 3 + 1)
                for step in range(2):
                    ffn_out_step(l, step, B_F2, O_F2)
                    if step == 0:
                        dve.wait_ge(S["par_loaded"], l * 16 + 16)
                        dve.wait_ge(S["mem_r"], l1)
                        for k in range(KB):
                            STT(mem32[:, k, :], mem32[:, k, :], par[:, C_MEM + k:C_MEM + k + 1], memr,
                                ALU.mult, ALU.mult).then_inc(S["memh_ready"], 1)
                        for c in range(4):
                            dve.wait_ge(S["memhi_ready"], l * 4 + (c + 1))
                            TT(m_lo2[c], mem32[:, 2 * c:2 * c + 2, :], f(m_hi2[c]), ALU.subtract)\
                                .then_inc(S["memlo_ready"], 1)
                for k in range(8):
                    lo(lb, B_MEM + k)
                    if k == 1:
                        dve.wait_ge(S["rms_ready"], l * 3 + 2)
                        for kb in range(4):
                            STT(hf[:, kb, :], x[:, kb, :], par[:, C_MIX + kb:C_MIX + kb + 1], xr, ALU.mult, ALU.mult)\
                                .then_inc(S["hf_ready"], 1)
                    if k == 2:
                        for kb in range(4, 8):
                            STT(hf[:, kb, :], x[:, kb, :], par[:, C_MIX + kb:C_MIX + kb + 1], xr, ALU.mult, ALU.mult)\
                                .then_inc(S["hf_ready"], 1)
                    if k in (4, 6):
                        for kb in range(2 * k - 8, 2 * k - 4):
                            dve.wait_ge(S["hhi_ready"], l * (3 * KB) + (KB + kb + 1))
                            TT(hlo[:, kb, :], hf[:, kb, :], f(hhi[:, kb, :]), ALU.subtract).then_inc(S["hlo_ready"], 1)
                V.memset(ypad[:, :, 0:PAD], 0.0).then_inc(S["pad_zeroed"], 1)
                TS(qtab[:, :], ropeQ[:, :], par[:, C_MQR:C_MQR + 1], None, ALU.mult).then_inc(S["qtab_ready"], 1)
                for k in range(4):
                    lo(lb, B_LAT + k)
                    if k == 2:
                        head_norm(memk[:, :, :], C_EK, memkr, "memk_r", l1, "memk_normed")
                for c in range(2):
                    for k in range(4):
                        lo(lb, B_CONV + 4 * c + k)
                        if c == 0 and k == 3:
                            dve.wait_ge(S["lat_r"], l1)
                            for kb in range(4):
                                STT(lat32[:, kb, :], lat32[:, kb, :], par[:, C_QLAT + kb:C_QLAT + kb + 1],
                                    latr[:, (kb // 2) * T:(kb // 2 + 1) * T], ALU.mult, ALU.mult)\
                                    .then_inc(S["lat_normed"], 1)
                        if c == 1 and k == 1:
                            dve.wait_ge(S["lathi_ready"], l1)
                            TT(latlo[:, :, :], lat32, f(lathi[:, :, :]), ALU.subtract).then_inc(S["latlo_ready"], 1)
                            dve.wait_ge(lo_ready[B_UP % RING], lb + (B_UP // RING + 1))
                            V.tensor_copy(wide(actlo), runs(f(wlo[:, B_UP % RING, :]))).then_inc(S["widelo_ready"], 1)
                    for o in (O_CONV + 2 * c, O_CONV + 2 * c + 1):
                        dve.wait_ge(read[o % 2], read_value(o, lh))
                    y = ypad[:, 2 * c:2 * c + 2, PAD:PAD + T]
                    TT(y, y, glu[c], ALU.mult).then_inc(S["glu_ready"], 1)
                lo(lb, B_UP)
                dve.wait_ge(S["krsq_ready"], l1)
                TS(krg, PS[:, BANK_NORM, 0:T], par[:, C_MKR:C_MKR + 1], None, ALU.mult).then_inc(S["krg_ready"], 1)
                lo(lb, B_UP + 1)
                lo(lb, B_UP + 2)
                dve.wait_ge(S["kr_permuted"], l1)
                TT(krt[:, 0, :], PS[:, BANK_NORM, 0:T], cosT[:, :], ALU.mult).then_inc(S["krt_ready"], 1)
                TT(krt[:, 1, :], PS[:, BANK_NORM, T:2 * T], sinK[:, :], ALU.mult).then_inc(S["krt_ready"], 1)
                lo(lb, B_UP + 3)
                dve.wait_ge(S["krt_ready"], l * 2 + 2)
                TT(krot[:, :], krt[:, 0, :], krt[:, 1, :], ALU.add).then_inc(S["krot_ready"], 1)
                for c, b in enumerate([B_SBQ, B_SBQ + 2, B_SBQ + 4, B_SBQ + 6, B_MEMQ, B_MEMQ + 2, B_SBV, B_SBV + 2]):
                    lo(lb, b)
                    lo(lb, b + 1)
                    if c == 1:
                        qr = mlaqk[:, 1, :, :]
                        dve.wait_ge(S["mq_sq"], l * 2 + 2)
                        dve.wait_ge(S["qtab_ready"], l1)
                        TT(qr, qr, each_of(qtab[:, :], HEADS), ALU.mult).then_inc(S["mq_tabled"], 1)
                        head_norm(mlaqk[:, 0, :, :], C_MQN, mqR, "mq_r", l1, "mq_normed")
                        dve.wait_ge(S["mq_tabled"], l1)
                        TT(qr, qr, mqR, ALU.mult).then_inc(S["mq_normed"], 1)
                    if c == 2:
                        head_norm(mlaqk[:, 2, :, :], C_MKN, mkR, "mk_r", l1, "mk_normed")
                        dve.wait_ge(S["krot_ready"], l1)
                        TT(mlaqk[:, 3, :, :], each_of(krot[:, :], HEADS), mkR, ALU.mult).then_inc(S["mk_normed"], 1)
                    if c == 4:
                        head_norm(hf[:, 0:4, :], C_SBQ, sbqR, "sbq_r", l1, "sbq_normed")
                    if c == 5:
                        head_norm(hf[:, 4:8, :], C_SBK, sbkR, "sbk_r", l1, "sbk_normed")
                    if c == 7:
                        head_norm(memq[:, :, :], C_EQ, eqR, "eq_r", l1, "eq_normed")
                dve.wait_ge(S["eq_normed"], l1)
                dve.wait_ge(S["glu_ready"], l * 2 + 2)
                dve.sem_inc(S["dve_waited"], 1)
                with dve.Fori(0, HEADS) as i:
                    n1 = dve.snap(l * HEADS + i + 1)
                    base = dve.snap(l * TURNS + i * 2)
                    taps = dve.snap((l * HEADS + i) * 32)
                    wcol = dve.snap(i * CONVW)

                    def conv(k0, k1):
                        for k in range(k0, k1):
                            w = par[:, bass.ds(wcol + (C_CONV + min(k, 30)), 1)]
                            y = ypad[:, bass.ds(i, 1), min(k, 30):min(k, 30) + T].rearrange("p a n -> p (a n)")
                            dve.wait_ge(S["conv_tap"], taps + (1 if k < 2 else k if k < 30 else k + 1))
                            if k == 0:
                                bias = par[:, bass.ds(wcol + (C_CONV + TAPS), 1)]
                                ins = TS(acc[0], y, w, bias, ALU.mult, ALU.add)
                            elif k == 1:
                                ins = TS(acc[1], y, w, None, ALU.mult)
                            elif k < 30:
                                ins = STT(acc[k % 2], y, w, acc[k % 2], ALU.mult, ALU.add)
                            elif k == 30:
                                ins = TT(acc[0], acc[0], acc[1], ALU.add)
                            else:
                                ins = STT(y, y, w, acc[0], ALU.mult, ALU.add)
                            ins.then_inc(S["conv_tap"], 1)

                    conv(0, 4)
                    lo(base, B_GATE + 1)
                    conv(4, 8)
                    lo(base, B_GATE + 2)
                    dve.wait_ge(S["mla_s"], n1)
                    V.memset(rows(PS[0:CHUNK, BANK_MLA, :], 2)[:, :, CHUNK:P], -1e30).then_inc(S["mla_masked"], 1)
                    dve.wait_ge(S["mla_masked"], n1)
                    V.reduce_max(stat[:, 0:1], PS[:, BANK_MLA, 0:P], axis=AX.X).then_inc(S["mla_max"], 1)
                    V.reduce_max(stat[:, 1:2], PS[:, BANK_MLA, P:384], axis=AX.X).then_inc(S["mla_max"], 1)
                    dve.wait_ge(S["e_s"], n1)
                    V.reduce_max(stat[:, 8:10], rows(PS[:, BANK_MEM, :], 2), axis=AX.X).then_inc(S["e_max"], 1)
                    dve.wait_ge(S["mla_max"], n1 * 2)
                    TS(stat[:, 2:4], stat[:, 0:2], -MLA_SCALE, None, ALU.mult).then_inc(S["mla_neg"], 1)
                    dve.wait_ge(S["e_max"], n1)
                    TS(stat[:, 10:12], stat[:, 8:10], -SB_SCALE, None, ALU.mult).then_inc(S["e_neg"], 1)
                    dve.wait_ge(S["sb_relu"], n1)
                    dve.wait_ge(S["sb_L"], n1)
                    STT(lk, relu, -1.0, sbL, ALU.mult, ALU.subtract).then_inc(S["sb_lk"], 1)
                    lo(base, B_GATE + 3)
                    dve.wait_ge(S["sb_lk"], n1)
                    STT(lw, PS[:, BANK_SB, 0:384], SB_SCALE, lk, ALU.mult, ALU.add).then_inc(S["sb_a"], 1)
                    dve.wait_ge(S["sb_a"], n1)
                    TT(diag2(lk), diag2(lk), strict2, ALU.mult).then_inc(S["sb_lkm"], 1)
                    conv(8, 12)
                    dve.wait_ge(S["mla_p"], n1 * 2)
                    V.reciprocal(stat[:, 6:8], stat[:, 4:6]).then_inc(S["mla_rec"], 1)
                    dve.wait_ge(S["e_p"], n1 * 2)
                    V.reciprocal(stat[:, 14:16], stat[:, 12:14]).then_inc(S["e_rec"], 1)
                    dve.wait_ge(S["mla_rec"], n1)
                    TS(mP[:, 0:P], mP[:, 0:P], stat[:, 6:7], None, ALU.mult).then_inc(S["mla_pn"], 1)
                    TS(mP[:, P:384], mP[:, P:384], stat[:, 7:8], None, ALU.mult).then_inc(S["mla_pn"], 1)
                    dve.wait_ge(S["e_rec"], n1)
                    for j in range(2):
                        p = eP[:, j * T:(j + 1) * T]
                        TS(p, p, stat[:, 14 + j:15 + j], None, ALU.mult).then_inc(S["e_pn"], 1)
                    conv(12, 16)
                    lo(base, B_GATE + 5)
                    conv(16, 22)
                    dve.wait_ge(S["sb_later"], n1)
                    TT(lw, PS[:, BANK_SB, 0:384], lw, ALU.add).then_inc(S["sb_logw"], 1)
                    lo(base, B_GATE + 6)
                    conv(22, 26)
                    dve.wait_ge(S["sb_expw"], n1)
                    TT(diag2(lw), diag2(lw), strict2, ALU.mult).then_inc(S["sb_w"], 1)
                    lo(base, B_GATE + 7)
                    conv(26, 28)
                    for s, bank, dhi, dlo in (("mla", BANK_MLA, b2hi, b2lo), ("e", BANK_MEM, b3hi, b3lo),
                                              ("sb", BANK_SB, b1hi, b1lo)):
                        dve.wait_ge(S[s + "_hi"], n1)
                        TT(dlo[:, i, :], PS[:, bank, 0:T], f(dhi[:, i, :]), ALU.subtract).then_inc(S[s + "_lo"], 1)
                    conv(28, 32)
                for u in range(2):
                    for c in range(4):
                        if u or c % 2:
                            lo(lb, B_BRANCH + 8 * u + 2 * c)
                        lo(lb, B_BRANCH + 8 * u + 2 * c + 1)
                        if u == 0 and c == 0:
                            dve.wait_ge(S["ln_mean"], l1)
                            STT(yc, each_of(PS[:, BANK_NORM, 0:T], 4), -1.0 / CONV_CH, ypad[:, :, PAD:PAD + T],
                                ALU.mult, ALU.add).then_inc(S["ln_c"], 1)
                        if u == 0 and c == 1:
                            dve.wait_ge(S["ln_r"], l1)
                            TT(yc, yc, each_of(yr, 4), ALU.mult).then_inc(S["ln_n"], 1)
                        n = 4 * u + c
                        o = O_BRANCH + n
                        q = group(o, lb, B_BRANCH + 2 * n + 1)
                        j0 = 2 - 2 * u
                        g = [gates[:, j0 + s, 2 * c:2 * c + 2, :] for s in range(2)]
                        m, p = hf[:, 2 * c:2 * c + 2, :], prod[c % 2]
                        dve.wait_ge(S["gate_sig"], l * 16 + (2 * n + 2))
                        if n >= 2:
                            dve.wait_ge(S["merged_ready"], l * 8 + (n - 1))
                        first = m if u == 0 else p[0]
                        TT(first, PS[:, q:q + 2, 0:T], g[0], ALU.mult).then_inc(S["first_ready"], 1)
                        TT(p[1], PS[:, q:q + 2, T:2 * T], g[1], ALU.mult).then_inc(read[o % 2], 1)

                        def low(e):
                            dve.wait_ge(S["mergedhi_ready"], l * 4 + (e + 1))
                            TT(m_lo2[e], hf[:, 2 * e:2 * e + 2, :], f(m_hi2[e]), ALU.subtract)\
                                .then_inc(S["mergedlo_ready"], 1)

                        if u == 0 and c == 3:
                            dve.wait_ge(S["b0hi_ready"], l1)
                            TT(b0lo[:, :, :], y32, f(b0hi[:, :, :]), ALU.subtract).then_inc(S["b0lo_ready"], 1)
                        if u == 1 and c:
                            low(c - 1)
                        if n == 7:
                            dve.wait_ge(S["first_ready"], l * 8 + 8)
                            TT(m, m, p[0], ALU.add).then_inc(S["prod_added"], 1)
                            dve.wait_ge(read[o % 2], read_value(o, lh))
                            dve.wait_ge(S["prod_added"], l * 4 + 4)
                            TT(m, m, p[1], ALU.add).then_inc(S["merged_ready"], 1)
                            low(3)
                for c in range(4):
                    lo(lb, B_OUT + 2 * c)
                    lo(lb, B_OUT + 2 * c + 1)
                    update(O_OUT + c, lb, B_OUT + 2 * c + 1, slice(2 * c, 2 * c + 2), 1.0)
                    dve.wait_ge(read[(O_OUT + c) % 2], read_value(O_OUT + c, lh))
                    x_low(l * (3 * KB) + 2 * KB, 0, 2 * c, C_FFN2)
                ffn_in(l, B_G1, O_G1, 8, l * 3 + 3)
                with dve.Fori(0, 2) as it:
                    ffn_out_step(l, it, B_G2, O_G2, C_NEXT)

        @block.tensor
        def _(pe):
            MM = nc.tensor.matmul

            def split(out, whi_, wlo_, xhi, xlo, start, stop):
                MM(out, whi_, xhi, start=start, stop=False)
                MM(out, whi_, xlo, start=False, stop=False)
                return MM(out, wlo_, xhi, start=False, stop=stop)

            def turn(o, hb):
                pe.wait_ge(read[o % 2], hb + (o // 2 + 1))
                return 2 * (o % 2)

            def arrived(base, b):
                pe.wait_ge(lo_ready[b % RING], base + (b // RING + 1))

            def feature_block(base, b, out, xhi, xlo, first=True, last=True, each=None):
                arrived(base, b)
                s = b % RING
                for k in range(KB):
                    if each:
                        each(k)
                    w = slice(k * P, (k + 1) * P)
                    ins = split(out, whi[:, s, w], wlo[:, s, w], xhi[k], xlo[k], first and k == 0, last and k == KB - 1)
                ins.then_inc(S["block_done"], 1)

            def feature_pair(base, b, o, hb, xhi=h_hi, xlo=h_lo, each=None):
                q = turn(o, hb)
                for m in range(2):
                    feature_block(base, b + m, PS[:, q + m, 0:T], xhi, xlo, each=each if m == 0 else None)

            def token_pair(base, b, o, hb, xhi, xlo):
                q = turn(o, hb)
                for half in range(2):
                    arrived(base, b + half)
                    s = (b + half) % RING
                    for k in range(4):
                        kb, w = 4 * half + k, slice(k * 2 * P, (k + 1) * 2 * P)
                        for t in range(2):
                            tt = slice(t * P, (t + 1) * P)
                            out = PS[:, q + t, 0:T]
                            MM(out, xhi[kb][:, tt], whi[:, s, w], start=kb == 0, stop=False)
                            MM(out, xhi[kb][:, tt], wlo[:, s, w], start=False, stop=False)
                            ins = MM(out, xlo[kb][:, tt], whi[:, s, w], start=False, stop=kb == KB - 1)
                    ins.then_inc(S["block_done"], 1)

            def total(bank, value, s_sum):
                pe.wait_ge(S["const_loaded"], 16)
                pe.wait_ge(S["sq_added"], value)
                MM(PS[:, bank, 0:T], ones, hf[:, 0, :], start=True, stop=False)
                MM(PS[:, bank, 0:T], ones, hf[:, 1, :], start=False, stop=True).then_inc(S[s_sum], 1)

            def head_sums(bank, squares, s_sum):
                for half in range(2):
                    ins = MM(PS[:, bank + half, :], ones, flat(squares)[:, half * 512:(half + 1) * 512], start=True, stop=True)
                ins.then_inc(S[s_sum], 1)

            def ffn_in_step(l, it, b0, o0, m, value=None):
                base, hb = pe.snap(l * TURNS + it * 2), pe.snap(l * HALF_OUT + it * 2)
                for j in range(4):
                    feature_pair(base, b0 + 2 * j, o0 + j, hb, each=normed(l, m) if value is not None and j == 0 else None)
                    if value is not None and j == 0:
                        total(BANK_NORM, value, "ssq_ready")

            def ffn_in(l, b0, o0, m, value):
                ffn_in_step(l, 0, b0, o0, m, value)
                with pe.Fori(1, 4) as it:
                    ffn_in_step(l, it, b0, o0, m)

            def ffn_out(l, b0, o0, f0):
                with pe.Fori(0, 2) as it:
                    base, hb = pe.snap(l * TURNS + it * 2), pe.snap(l * HALF_OUT + it)
                    for j in range(2):
                        q = turn(o0 + j, hb)
                        for half in range(2):
                            pe.wait_ge(S["actlo_ready"], l * 16 + (f0 + 4 * half + 6))
                            hs = slice(8 * half, 8 * half + 8)
                            for m in range(2):
                                feature_block(base, b0 + 4 * j + 2 * half + m, PS[:, q + m, 0:T], act_hi[hs], act_lo[hs],
                                              first=half == 0, last=half == 1)

            def normed(l, m):
                return lambda k: pe.wait_ge(S["hlo_ready"], l * (3 * KB) + (m * KB + k + 1))

            pe.sem_inc(S["block_done"], RING)
            with pe.Fori(0, DEPTH) as l:
                lb, lh = pe.snap(l * TURNS), pe.snap(l * HALF_OUT)
                l1 = pe.snap(l + 1)
                ffn_in(l, B_F1, O_F1, 0, l * 12 + 4)
                total(BANK_MEM, l * 12 + 7, "mem_ssq")
                ffn_out(l, B_F2, O_F2, 0)
                pe.wait_ge(S["memlo_ready"], l * 4 + 4)
                for c in range(2):
                    feature_pair(lb, B_MEM + 2 * c, O_MEM + c, lh, m_hi, m_lo)
                    if c == 0:
                        total(BANK_NORM, l * 12 + 10, "ssq_ready")
                for c in range(2, 4):
                    token_pair(lb, B_MEM + 2 * c, O_MEM + c, lh, m_hi, m_lo)
                    if c == 2:
                        pe.wait_ge(S["memk_sq"], l1)
                        head_sums(4, memksq, "memk_ssq")
                for c in range(2):
                    feature_pair(lb, B_LAT + 2 * c, O_LAT + c, lh, each=normed(l, 1) if c == 0 else None)
                for c in range(4):
                    feature_pair(lb, B_CONV + 2 * c, O_CONV + c, lh)
                    if c == 0:
                        pe.wait_ge(S["lat_sq"], l1)
                        for k in range(4):
                            ins = MM(PS[:, BANK_MLA, (k // 2) * T:(k // 2 + 1) * T], ones, latsq[:, k, :],
                                     start=k % 2 == 0, stop=k % 2 == 1)
                        ins.then_inc(S["lat_ssq"], 1)
                arrived(lb, B_UP)
                pe.wait_ge(S["widehi_ready"], l1)
                pe.wait_ge(S["widelo_ready"], l1)

                def twice(w, run):
                    return w[:, :, :].rearrange("p k n -> p (k n)")[:, run * P:(run + 1) * P]

                for kb in range(KB):
                    ins = split(PS[:, BANK_NORM, 0:T], twice(acthi, kb), twice(actlo, kb),
                                h_hi[kb], h_lo[kb], kb == 0, kb == KB - 1)
                ins.then_inc(S["kr_ready"], 1)
                pe.wait_ge(S["latlo_ready"], l1)
                for c in range(3):
                    q = turn(O_UP + c, lh)
                    if c:
                        arrived(lb, B_UP + c)
                    s, lat0 = (B_UP + c) % RING, 0 if c < 2 else 2
                    for h in range(HEADS):
                        for kb in range(2):
                            place = (h * 2 + kb) * P
                            if c == 0:
                                w = [twice(t, KB + h * 2 + kb) for t in (acthi, actlo)]
                            else:
                                w = [t[:, s, place:place + P] for t in (whi, wlo)]
                            ins = split(PS[:, q + h // 2, (h % 2) * T:(h % 2 + 1) * T], w[0], w[1],
                                        lathi[:, lat0 + kb, :], latlo[:, lat0 + kb, :], kb == 0, kb == 1)
                    ins.then_inc(S["block_done"], 1)
                    if c == 1:
                        pe.wait_ge(S["krg_ready"], l1)
                        MM(PS[:, BANK_NORM, 0:T], permA, krg, start=True, stop=True)
                        MM(PS[:, BANK_NORM, T:2 * T], permB, krg, start=True, stop=True).then_inc(S["kr_permuted"], 1)
                q = turn(O_UP + 3, lh)
                arrived(lb, B_UP + 3)
                s = (B_UP + 3) % RING
                for t in range(2):
                    tt = slice(t * P, (t + 1) * P)
                    for kb in range(2):
                        w = slice(kb * 512, (kb + 1) * 512)
                        out = PS[:, q + t, :]
                        MM(out, lathi[:, 2 + kb, tt], whi[:, s, w], start=kb == 0, stop=False)
                        MM(out, lathi[:, 2 + kb, tt], wlo[:, s, w], start=False, stop=False)
                        ins = MM(out, latlo[:, 2 + kb, tt], whi[:, s, w], start=False, stop=kb == 1)
                ins.then_inc(S["block_done"], 1)
                for c in range(4):
                    feature_pair(lb, B_SBQ + 2 * c, O_SBQ + c, lh)
                    if c == 0:
                        pe.wait_ge(S["mq_sq_all"], l1)
                        head_sums(4, mqsq, "mq_ssq")
                    if c == 1:
                        pe.wait_ge(S["mk_sq_all"], l1)
                        pe.wait_ge(S["krt_ready"], l * 2 + 2)
                        head_sums(6, mksq, "mk_ssq")
                for c in range(2):
                    feature_pair(lb, B_MEMQ + 2 * c, O_MEMQ + c, lh)
                    if c == 0:
                        pe.wait_ge(S["sbq_sq"], l1)
                        head_sums(4, sbqsq, "sbq_ssq")
                        pe.wait_ge(S["sbk_sq"], l1)
                        head_sums(6, sbksq, "sbk_ssq")
                for c in range(2):
                    token_pair(lb, B_SBV + 2 * c, O_SBV + c, lh, h_hi, h_lo)
                    if c == 0:
                        pe.wait_ge(S["eq_sq"], l1)
                        head_sums(4, eqsq, "eq_ssq")
                with pe.Fori(0, HEADS) as i:
                    n1 = pe.snap(l * HEADS + i + 1)
                    base, hb = pe.snap(l * TURNS + i * 2), pe.snap(l * HALF_OUT + i * 2)

                    def weighted(bank, v0, w):
                        MM(PS[:, bank, 0:T], vh[:, v0, :], w[:, 0:T], start=True, stop=False)
                        return MM(PS[:, bank, P:T], vh[:, v0 + 1, :], w[:, T:384], start=False, stop=True)

                    feature_pair(base, B_GATE, O_GATE, hb)
                    for s in ("sbq_normed", "sbk_normed", "eq_normed", "memk_normed"):
                        pe.wait_ge(S[s], l1)
                    pe.wait_ge(S["mk_normed"], l * 2 + 2)
                    pe.wait_ge(S["fixed_ready"], n1 * 4)
                    pe.wait_ge(S["sb_lo"], n1)
                    pe.wait_ge(S["mla_lo"], n1)
                    pe.wait_ge(S["e_lo"], n1)
                    MM(PS[:, BANK_SB, 0:T], sbk[:, 0:P], hf[:, i, :], start=True, stop=True)
                    MM(PS[:, BANK_SB, T:384], sbk[:, P:T], hf[:, i, P:T], start=True, stop=True).then_inc(S["sb_z"], 1)
                    MM(PS[:, BANK_MLA, 0:P], mq[:, 0:P], mlaqk[:, 2, i, 0:P], start=True, stop=False)
                    MM(PS[:, BANK_MLA, 0:P], mqr[:, 0:P], mlaqk[:, 3, i, 0:P], start=False, stop=True)
                    MM(PS[:, BANK_MLA, P:384], mq[:, P:T], mlaqk[:, 2, i, :], start=True, stop=False)
                    MM(PS[:, BANK_MLA, P:384], mqr[:, P:T], mlaqk[:, 3, i, :], start=False, stop=True)\
                        .then_inc(S["mla_s"], 1)
                    for t in range(2):
                        ins = MM(PS[:, BANK_MEM, t * T:(t + 1) * T], eq[:, t * P:(t + 1) * P], memk[:, i, :],
                                 start=True, stop=True)
                    ins.then_inc(S["e_s"], 1)
                    feature_pair(base, B_GATE + 2, O_GATE + 1, hb)
                    feature_pair(base, B_GATE + 4, O_GATE + 2, hb)
                    pe.wait_ge(S["sb_lkm"], n1)
                    MM(PS[:, BANK_SB, 0:384], later, lk, start=True, stop=False)
                    MM(PS[:, BANK_SB, P:T], ones, lk[:, T:384], start=False, stop=True).then_inc(S["sb_later"], 1)
                    pe.wait_ge(S["mla_pn"], n1 * 2)
                    for k in range(3):
                        ins = nc.tensor.transpose(PS[:, BANK_MLA, k * P:(k + 1) * P], mP[:, k * P:(k + 1) * P], ident)
                    ins.then_inc(S["mla_transposed"], 1)
                    pe.wait_ge(S["e_pn"], n1 * 2)
                    for k in range(2):
                        for t in range(2):
                            ins = nc.tensor.transpose(PS[:, BANK_MEM, (2 * k + t) * P:(2 * k + t + 1) * P],
                                                      eP[:, (2 * t + k) * P:(2 * t + k + 1) * P], ident)
                    ins.then_inc(S["e_transposed"], 1)
                    feature_pair(base, B_GATE + 6, O_GATE + 3, hb)
                    pe.wait_ge(S["vh_ready"], n1)
                    pe.wait_ge(S["mla_PT"], n1)
                    weighted(BANK_MLA, 2, mPT).then_inc(S["mla_pv"], 1)
                    pe.wait_ge(S["e_PT"], n1)
                    MM(PS[:, BANK_MEM, 0:T], vh[:, 4, :], ePT[:, 0:T], start=True, stop=False)
                    MM(PS[:, BANK_MEM, 0:T], vh[:, 5, :], ePT[:, T:2 * T], start=False, stop=True)\
                        .then_inc(S["e_pv"], 1)
                    pe.wait_ge(S["sb_w"], n1)
                    weighted(BANK_SB, 0, lw).then_inc(S["sb_pv"], 1)
                for u in range(2):
                    j0 = 2 - 2 * u
                    if u == 0:
                        pe.wait_ge(S["mla_lo"], l * 4 + 5)
                        pe.wait_ge(S["e_lo"], l * 4 + 5)
                    else:
                        pe.wait_ge(S["sb_lo"], l * 4 + 5)
                        pe.wait_ge(S["b0lo_ready"], l1)
                    for c in range(4):
                        o = O_BRANCH + 4 * u + c
                        q = turn(o, lh)
                        for m in range(2):
                            b = B_BRANCH + 8 * u + 2 * c + m
                            arrived(lb, b)
                            for s in range(2):
                                for kb in range(4):
                                    w = slice((4 * s + kb) * P, (4 * s + kb + 1) * P)
                                    ins = split(PS[:, q + m, s * T:(s + 1) * T], whi[:, b % RING, w], wlo[:, b % RING, w],
                                                bhi[j0 + s][:, kb, :], blo[j0 + s][:, kb, :], kb == 0, kb == 3)
                            ins.then_inc(S["block_done"], 1)
                        if u == 0 and c == 0:
                            pe.wait_ge(S["conv_tap"], l * (4 * 32) + (4 * 32 + 1))
                            for k in range(4):
                                ins = MM(PS[:, BANK_NORM, 0:T], ones, ypad[:, k, PAD:PAD + T], start=k == 0, stop=k == 3)
                            ins.then_inc(S["ln_mean"], 1)
                        if u == 0 and c == 1:
                            pe.wait_ge(S["ln_sq"], l1)
                            for k in range(4):
                                ins = MM(PS[:, BANK_NORM, 0:T], ones, ysq[:, k, :], start=k == 0, stop=k == 3)
                            ins.then_inc(S["ln_var"], 1)
                q = turn(O_OUT, lh)
                for ks in (range(6), range(6, 8)):
                    for m in range(2):
                        arrived(lb, B_OUT + m)
                        for k in ks:
                            pe.wait_ge(S["mergedlo_ready"], l * 4 + (k // 2 + 1))
                            w = slice(k * P, (k + 1) * P)
                            ins = split(PS[:, q + m, 0:T], whi[:, (B_OUT + m) % RING, w], wlo[:, (B_OUT + m) % RING, w],
                                        m_hi[k], m_lo[k], k == 0, k == KB - 1)
                        if k == KB - 1:
                            ins.then_inc(S["block_done"], 1)
                for c in range(1, 4):
                    feature_pair(lb, B_OUT + 2 * c, O_OUT + c, lh, m_hi, m_lo)
                ffn_in(l, B_G1, O_G1, 2, l * 12 + 13)
                ffn_out(l, B_G2, O_G2, 8)


def _features(w, cols):
    return [w[:, c:c + P].reshape(-1, P, P).transpose(1, 0, 2).reshape(P, BLK) for c in cols]


def _tokens(w, cols):
    return [w[r:r + 512, c:c + 256].reshape(4, P, 256).transpose(1, 0, 2).reshape(P, BLK)
            for c in cols for r in (0, 512)]


def _ffn(w_in, w_out):
    cols = [half + c + m for c in range(0, FFN, 256) for half in (0, FFN) for m in (0, P)]
    out = _features(w_in, cols)
    for c in range(0, D_MODEL, 256):
        for rows in (0, 1024):
            out += _features(w_out[rows:rows + 1024], (c, c + P))
    return out


def _small(w, picks):
    blocks = w.reshape(-1, P, w.shape[1])
    return np.concatenate([b[:, c:c + n] for c, n in picks for b in blocks], axis=1)


def _layer_stream(l, a):
    w = a["w_in"][l]
    conv, sbq, sbv = 0, 1024, 1024 + 2 * 512
    qlat = 1024 + 3 * 512
    kr, memq = qlat + 2 * LORA, qlat + 2 * LORA + ROPE
    gate = memq + 512
    kv = a["mem_w_kv"][l]
    out = _ffn(a["ffn1_w_in"][l], a["ffn1_w_out"][l])
    out += _features(kv, range(0, 512, P)) + _tokens(kv, (512, 768))
    out += _features(w, range(qlat, qlat + 512, P))
    out += _features(w, [conv + c + part + m for c in (0, 256) for part in (0, CONV_CH) for m in (0, P)])
    uq, ukv, hd = a["mla_w_uq"][l], a["mla_w_ukv"][l], HEAD_DIM
    krw = w[:, kr:kr + ROPE].reshape(KB, P, ROPE).transpose(1, 0, 2).reshape(P, KB * ROPE)
    out.append(np.concatenate([krw, _small(uq, [(h * (hd + ROPE) + hd, ROPE) for h in range(HEADS)])], axis=1))
    out.append(_small(uq, [(h * (hd + ROPE), hd) for h in range(HEADS)]))
    out.append(_small(ukv, [(h * 2 * hd, hd) for h in range(HEADS)]))
    v = ukv.reshape(2, P, HEADS, 2, hd)[:, :, :, 1, :].reshape(2, P, HEADS * hd)
    out.append(v.transpose(1, 0, 2).reshape(P, BLK))
    out += _features(w, range(sbq, sbq + 1024, P)) + _features(w, range(memq, memq + 512, P))
    out += _tokens(w, (sbv, sbv + 256))
    out += _features(w, range(gate, gate + N_BRANCH * D_MODEL, P))
    wb = a["w_branch"][l].reshape(N_BRANCH * 512, D_MODEL)
    out += _features(wb[1024:], range(0, D_MODEL, P)) + _features(wb[:1024], range(0, D_MODEL, P))
    out += _features(a["w_out"][l], range(0, D_MODEL, P))
    return out + _ffn(a["ffn2_w_in"][l], a["ffn2_w_out"][l])


def _layer_params(l, a):
    def col(v):
        return v.reshape(-1, P).T

    def rope(v):
        return np.concatenate([v[HEAD_DIM:], v[HEAD_DIM:]]).reshape(1, P).T

    conv = [np.concatenate([a["conv_dw"][l][:, k * P:(k + 1) * P].T, a["conv_b"][l][k * P:(k + 1) * P, None]], axis=1)
            for k in range(4)]
    mq, mk = a["mla_q_hnorm"][l], a["mla_k_hnorm"][l]
    return np.concatenate(
        [col(a[n][l]) for n in ("ffn1_norm", "mix_norm", "ffn2_norm", "mem_norm")] + conv
        + [col(a[n][l]) for n in ("conv_ln_g", "conv_ln_b", "sb_q_hnorm", "sb_k_hnorm", "mla_q_norm", "mla_kv_norm")]
        + [col(mq[:HEAD_DIM]), rope(mq), col(mk[:HEAD_DIM]), rope(mk)]
        + [col(a[n][l]) for n in ("mem_q_hnorm", "mem_k_hnorm")] + [col(a["ffn1_norm"][(l + 1) % DEPTH])], axis=1)


def _constants():
    r = np.arange(P)
    quarter, j = r // 32, r % 32
    row_a, row_b = np.array([0, 1, 1, 0])[quarter] * 32 + j, np.array([1, 0, 0, 1])[quarter] * 32 + j
    freq = (ROPE_BASE ** (-np.arange(0, ROPE, 2) / ROPE)).astype(np.float32)
    cols = [np.array(c, np.float64)[quarter][:, None] for c in ([1, 1, 0, 0], [0, 0, 1, -1], [-1, 1, 1, -1])]
    return np.concatenate(
        [np.ones((P, P)), np.full((P, P), 0.5), r[:, None] > r[None, :], np.eye(P), r[:, None] < r[None, :],
         r[:, None] == row_a[None, :], r[:, None] == row_b[None, :],
         np.full((P, 1), EPS), np.ones((P, 1)), freq[j][:, None]] + cols, axis=1).astype(np.float32)


def kernel(**inputs):
    import concourse.bacc as bacc
    from concourse.bass_utils import run_bass_kernel_spmd as run

    a = {n: np.asarray(v) for n, v in inputs.items()}
    blocks = [b for l in range(DEPTH) for b in _layer_stream(l, a)]
    arrays = {
        "stream": np.stack(blocks + blocks[:AHEAD]),
        "xT": np.ascontiguousarray(a["x"][0].T),
        "memT": np.ascontiguousarray(a["mem"][0].T),
        "positions": np.ascontiguousarray(a["positions"]),
        "params": np.stack([_layer_params(l, a) for l in range(DEPTH)]),
        "consts": _constants(),
    }
    nc = bacc.Bacc("TRN2", target_bir_lowering=False, num_devices=1)
    args = [nc.dram_tensor(n, v.shape, mybir.dt.from_np(v.dtype), kind="ExternalInput").ap() for n, v in arrays.items()]
    args.append(nc.dram_tensor("outT", (D_MODEL, SEQ), mybir.dt.float32, kind="ExternalOutput").ap())
    build(nc, *args)
    r = run(nc, [arrays], core_ids=[0])
    return np.ascontiguousarray(r.results[0]["outT"].T).reshape(1, SEQ, D_MODEL)
```

```python
import numpy as np

import concourse.bass as bass
from concourse import mybir
from contextlib import ExitStack

D_MODEL, SEQ, DEPTH, MEM_LEN = 1024, 256, 2, 256
FFN, CONV_CH, TAPS, HEADS, HEAD_DIM = 2048, 512, 31, 4, 128
LORA, ROPE, CHUNK, N_BRANCH, EPS = 256, 64, 64, 4, 1e-6
ROPE_BASE = 10000.0
P = 128
T = SEQ
KB = D_MODEL // P
PAD = TAPS - 1

BLK = 1024
RING = 4
AHEAD = 3
B_F1 = 0
B_F2 = B_F1 + 32
B_MEM = B_F2 + 16
B_LAT = B_MEM + 8
B_CONV = B_LAT + 4
B_UP = B_CONV + 8
B_SBQ = B_UP + 4
B_MEMQ = B_SBQ + 8
B_SBV = B_MEMQ + 4
B_GATE = B_SBV + 4
B_BRANCH = B_GATE + 32
B_OUT = B_BRANCH + 16
B_G1 = B_OUT + 8
B_G2 = B_G1 + 32
NBLK = B_G2 + 16
TURNS = NBLK // RING
assert NBLK == RING * TURNS

O_F1 = 0
O_F2 = O_F1 + 16
O_MEM = O_F2 + 4
O_LAT = O_MEM + 4
O_CONV = O_LAT + 2
O_UP = O_CONV + 4
O_SBQ = O_UP + 4
O_MEMQ = O_SBQ + 4
O_SBV = O_MEMQ + 2
O_GATE = O_SBV + 2
O_BRANCH = O_GATE + 16
O_OUT = O_BRANCH + 8
O_G1 = O_OUT + 4
O_G2 = O_G1 + 16
NOUT = O_G2 + 4
assert NOUT % 2 == 0

R_MEM, R_MIX, R_MEMK, R_LAT, R_MQ, R_MK, R_SBQ, R_SBK, R_EQ, R_CONV, R_FFN2, R_NEXT = range(12)
NROOT = 12

C_FFN1, C_MIX, C_FFN2, C_MEM = 0, KB, 2 * KB, 3 * KB
C_CONV = 4 * KB
CONVW = TAPS + 1
C_LNG = C_CONV + 4 * CONVW
C_LNB = C_LNG + 4
C_SBQ = C_LNB + 4
C_SBK = C_SBQ + 1
C_QLAT = C_SBK + 1
C_KVLAT = C_QLAT + 2
C_MQN, C_MQR, C_MKN, C_MKR = C_KVLAT + 2, C_KVLAT + 3, C_KVLAT + 4, C_KVLAT + 5
C_EQ, C_EK = C_KVLAT + 6, C_KVLAT + 7
C_NEXT = C_EK + 1
NPAR = C_NEXT + KB

K_ONES, K_LATER, K_IDENT, K_STRICT, K_PA, K_PB = (P * i for i in range(6))
K_EPS, K_ONE, K_FREQ, K_QC, K_QS, K_KS = (6 * P + i for i in range(6))
NCONST = 6 * P + 6
ROUNDER = 1.5 * 2.0 ** 23


def build(nc, stream, xT, memT, positions, params, consts, outT):
    F32, F32R, I32 = mybir.dt.float32, mybir.dt.float32r, mybir.dt.int32
    ALU, ACT, AX = mybir.AluOpType, mybir.ActivationFunctionType, mybir.AxisListType
    SB_SCALE = float(HEAD_DIM) ** -0.5
    MLA_SCALE = float(HEAD_DIM + ROPE) ** -0.5
    BANK_SB, BANK_MLA, BANK_MEM, BANK_NORM = 4, 5, 6, 7

    ctx = ExitStack()
    with ctx:
        def sb(name, shape, dt=F32):
            return ctx.enter_context(nc.sbuf_tensor(name, shape, dt))

        def over(name, shape, dt=F32):
            with nc.sbuf_tensor(name, shape, dt) as t:
                return t

        def sem(name):
            return ctx.enter_context(nc.semaphore(name))

        raw = sb("raw", [P, RING, BLK])
        whi = sb("whi", [P, RING, BLK], F32R)
        wlo = sb("wlo", [P, RING, BLK], F32R)
        x = sb("x", [P, KB, T])
        hhi = sb("hhi", [P, KB, T], F32R)
        hlo = sb("hlo", [P, KB, T], F32R)
        hf = sb("hf", [P, KB, T])
        gates = over("gates", [P, N_BRANCH, KB, T])
        acthi = sb("acthi", [P, 2 * KB, T], F32R)
        actlo = sb("actlo", [P, 2 * KB, T], F32R)
        ypad = over("ypad", [P, 4, PAD + T])
        b0hi, b0lo = sb("b0hi", [P, 4, T], F32R), sb("b0lo", [P, 4, T], F32R)
        b1hi, b1lo = sb("b1hi", [P, 4, T], F32R), sb("b1lo", [P, 4, T], F32R)
        mlaqk = over("mlaqk", [P, 4, 4, T])
        b2hi, b2lo = sb("b2hi", [P, 4, T], F32R), sb("b2lo", [P, 4, T], F32R)
        sb("mla_k_room", [P, 2, 4, T])
        memq = over("memq", [P, 4, T])
        b3hi, b3lo = sb("b3hi", [P, 4, T], F32R), sb("b3lo", [P, 4, T], F32R)
        bhi, blo = [b0hi, b1hi, b2hi, b3hi], [b0lo, b1lo, b2lo, b3lo]
        lathi, latlo = b1hi, b1lo
        vall = sb("vall", [P, 6, 4 * HEAD_DIM])
        memk = sb("memk", [P, 4, T])
        krsq, krot, qtab = sb("krsq", [P, T]), sb("krot", [P, T]), sb("qtab", [P, T])
        cosT, sinK, ropeQ = sb("cosT", [P, T]), sb("sinK", [P, T]), sb("ropeQ", [P, T])
        con = sb("con", [P, NCONST])
        con_r = sb("con_r", [P, 2 * P], F32R)
        par = sb("par", [P, NPAR])
        stat = sb("stat", [P, 16])
        work = sb("work", [P, 6144])
        PS = ctx.enter_context(nc.psum_tensor("PS", [P, 8, 512], F32))

        h_hi, h_lo = [hhi[:, k, :] for k in range(KB)], [hlo[:, k, :] for k in range(KB)]
        act_hi, act_lo = [acthi[:, k, :] for k in range(2 * KB)], [actlo[:, k, :] for k in range(2 * KB)]
        m_hi = [t[:, k, :] for t in (b2hi, b3hi) for k in range(4)]
        m_lo = [t[:, k, :] for t in (b2lo, b3lo) for k in range(4)]
        m_hi2 = [t[:, k:k + 2, :] for t in (b2hi, b3hi) for k in (0, 2)]
        m_lo2 = [t[:, k:k + 2, :] for t in (b2lo, b3lo) for k in (0, 2)]

        ones, later = con[:, K_ONES:K_ONES + P], con[:, K_LATER:K_LATER + P]
        ones_r, later_r = con_r[:, 0:P], con_r[:, P:2 * P]
        ident = con[:, K_IDENT:K_IDENT + P]
        strict2 = con[:, K_STRICT:K_STRICT + P].rearrange("p (a n) -> p a n", a=1).broadcast_to([P, 2, P])
        permA, permB = con[:, K_PA:K_PA + P], con[:, K_PB:K_PB + P]
        eps, one = con[:, K_EPS:K_EPS + 1], con[:, K_ONE:K_ONE + 1]

        def rows(ap, n):
            return ap.rearrange("p (a n) -> p a n", a=n)

        def each_of(ap, n):
            return rows(ap, 1).broadcast_to([P, n, T])

        def f(ap):
            return ap.bitcast(F32)

        def wide(t):
            return t[:, 0:KB, :].rearrange("p k n -> p (k n)").rearrange("p (r a n) -> p r a n", a=2, n=ROPE)

        def runs(ap):
            return ap.rearrange("p (r a n) -> p r a n", a=1, n=ROPE).broadcast_to([P, BLK // ROPE, 2, ROPE])

        def w2(a):
            return rows(work[:, a:a + 2 * T], 2)

        def w4(a):
            return rows(work[:, a:a + 4 * T], 4)

        def two_banks(tile):
            return rows(tile.rearrange("p k n -> p (k n)"), 2)

        def flat(tile):
            return tile.rearrange("p k n -> p (k n)")

        def at(i, k, n=1):
            return slice(i + k, i + k + n) if isinstance(i, int) else bass.ds(i + k, n)

        silu, up32, act32 = [w2(0), w2(512)], [w2(1024), w2(1536)], [w2(2048), w2(2560)]
        mem32, memr, xr = rows(work[:, 3072:5120], KB), work[:, 5120:5376], work[:, 5376:5632]
        memksq, memkr = w4(0), w4(1024)
        lat32, latsq, latr = w4(2048), w4(3072), work[:, 4096:4608]
        glu = [w2(4608), w2(5120)]
        krt, krg = w2(3072), work[:, 3584:3840]
        mqsq, mqrsq, mqR = w4(0), w4(1024), w4(2048)
        mksq, mkR = w4(4864), w4(3840)
        sbqsq, sbqR = w4(0), w4(1024)
        sbksq, sbkR = w4(2048), w4(0)
        eqsq, eqR = w4(3840), w4(4864)
        vh = rows(work[:, 0:768], 6)
        sbk, mq, mqr, eq = (work[:, 768 + T * i:768 + T * (i + 1)] for i in range(4))
        sbL, relu, lk, lw = (work[:, 1792 + 384 * i:1792 + 384 * (i + 1)] for i in range(4))
        mP, mPT = work[:, 3328:3712], work[:, 3712:4096]
        eP, ePT = work[:, 4096:4608], work[:, 4608:5120]
        acc = [work[:, 5120:5376], work[:, 5376:5632]]
        sq_place = [(acthi[:, k:k + 4, :], actlo[:, k:k + 4, :]) for k in (KB, KB + 4)]
        lkh, lkl = (b0lo[:, 1:4, :].rearrange("p k n -> p (k n)")[:, k:k + 384] for k in (0, 384))
        assert 4 * (PAD + T) <= 5 * T
        yc, ysq, yr, y32 = w4(0), w4(1024), work[:, 2048:2304], w4(2304)
        ysum = w2(5632)
        prod = [[w2(3328), w2(3840)], [w2(4352), w2(4864)]]

        names = """act_waited dve_waited pool_waited par0_loaded par_loaded mem_loaded const_loaded
            pos_loaded out_stored hi_ready block_done rope_step
            x_sq sq_added sq_high sq_low rounded_ready ssq_ready root_ln rms_ready hf_ready hhi_ready hlo_ready
            silu_ready act_ready acthi_ready actlo_ready
            mem_sq mem_ssq mem_r memh_ready memhi_ready memlo_ready pad_zeroed glu_ready
            lat_sq lat_sq_all lat_ssq lat_r lat_normed lathi_ready latlo_ready
            widehi_ready widelo_ready kr_ready krsq_ready krg_ready kr_permuted krt_ready krot_ready qtab_ready
            memk_sq memk_ssq memk_r memk_normed mq_sq mq_sq_all mq_ssq mq_r mq_tabled mq_normed
            mk_sq mk_sq_all mk_ssq mk_r mk_normed
            sbq_sq sbq_ssq sbq_r sbq_normed sbk_sq sbk_ssq sbk_r sbk_normed eq_sq eq_ssq eq_r eq_normed
            fixed_ready vh_ready sb_z mla_s e_s
            sb_abs sb_exp sb_L sb_relu sb_lk sb_a sb_lkm sb_lkh sb_lkl sb_later sb_logw sb_expw sb_w sb_pv sb_hi sb_lo
            mla_masked mla_max mla_neg mla_p mla_rec mla_pn mla_transposed mla_PT mla_pv mla_hi mla_lo
            e_max e_neg e_p e_rec e_pn e_transposed e_PT e_pv e_hi e_lo
            conv_tap y_paired ln_mean ln_c ln_sq ysq_paired ln_var ln_r ln_n ln_silu b0hi_ready b0lo_ready
            gate_sig first_ready prod_added merged_ready mergedhi_ready mergedlo_ready""".split()
        S = {n: sem(n) for n in names}
        raw_ready = [sem(f"raw_ready{i}") for i in range(RING)]
        x_loaded = [sem(f"x_loaded{c}") for c in range(KB // 2)]
        lo_ready = [sem(f"lo_ready{i}") for i in range(RING)]
        read = [sem(f"group_read{i}") for i in range(2)]
        HALF_OUT = NOUT // 2

        def read_value(o, half_base):
            return half_base + (o // 2 + 2)

        def diag2(ap):
            return ap.rearrange("p (a n) -> p a n", n=P)[:, 0:3:2, :]

        block = ctx.enter_context(nc.Block())

        @block.sync
        def _(sp):
            xin = xT.rearrange("(k p) t -> p k t", p=P)
            sp.dma_start(par[:, :], params[0, :, :]).then_inc(S["par0_loaded"], 16)
            for b in range(RING):
                sp.dma_start(raw[:, b, :], stream[b, :, :]).then_inc(raw_ready[b], 16)
                if b == 2:
                    sp.dma_start(con[:, :], consts).then_inc(S["const_loaded"], 16)
                for c in (2 * b, 2 * b + 1) if b < 2 else ():
                    sp.dma_start(x[:, 2 * c:2 * c + 2, :], xin[:, 2 * c:2 * c + 2, :]).then_inc(x_loaded[c], 16)
            with sp.Fori(0, DEPTH * TURNS - 1) as t:
                for k in range(RING):
                    sp.wait_ge(lo_ready[k], t + 1)
                    sp.dma_start(raw[:, k, :], stream[bass.ds(t * RING + (k + RING), 1), :, :]
                                 .rearrange("a p n -> p (a n)")).then_inc(raw_ready[k], 16)
            for k in range(AHEAD):
                sp.wait_ge(lo_ready[k], DEPTH * TURNS)
                sp.dma_start(raw[:, k, :], stream[DEPTH * NBLK + k, :, :]).then_inc(raw_ready[k], 16)
            xout = outT.rearrange("(k p) t -> p k t", p=P)
            for c in range(4):
                sp.wait_ge(read[(O_G2 + c % 2) % 2], read_value(O_G2 + c % 2, (DEPTH - 1) * HALF_OUT + c // 2))
                sp.dma_start(xout[:, 2 * c:2 * c + 2, :], x[:, 2 * c:2 * c + 2, :]).then_inc(S["out_stored"], 16)
            sp.wait_ge(S["out_stored"], 64)

        @block.gpsimd
        def _(pool):
            TT = nc.gpsimd.tensor_tensor

            def squares_sum(value, s, first):
                for c in range(1, 4):
                    pool.wait_ge(S[s], value(c))
                    pool.wait_ge(S["sq_added"], first + (c - 1))
                    TT(hf[:, 0:2, :], hf[:, 0:2, :], hf[:, 2 * c:2 * c + 2, :], ALU.add).then_inc(S["sq_added"], 1)
                pool.wait_ge(S["sq_added"], first + 3)
                TT(hf[:, 0, :], hf[:, 0, :], hf[:, 1, :], ALU.add).then_inc(S["sq_added"], 1)

            def lo(base, b):
                b += AHEAD
                pool.wait_ge(S["hi_ready"], base * RING + (b + 1))
                TT(wlo[:, b % RING, :], raw[:, b % RING, :], f(whi[:, b % RING, :]), ALU.subtract)\
                    .then_inc(lo_ready[b % RING], 1)

            def ffn_in_step(l, it, f0):
                n0 = pool.snap(l * 16 + it * 2)
                for j in range(2):
                    n = f0 + j + 1
                    pool.wait_ge(S["silu_ready"], n0 + n)
                    pool.wait_ge(read[1], l * HALF_OUT + it * 2 + ((O_F1 if f0 == 0 else O_G1) // 2 + j + 2))
                    pool.wait_ge(S["actlo_ready"], n0 + n)
                    TT(act32[j], up32[j], silu[j], ALU.mult).then_inc(S["act_ready"], 1)
                    pool.wait_ge(S["acthi_ready"], n0 + n)
                    pool.sem_inc(S["pool_waited"], 1)
                    pair = at(it * 4, 2 * j, 2)
                    TT(actlo[:, pair, :], act32[j], f(acthi[:, pair, :]), ALU.subtract).then_inc(S["actlo_ready"], 1)

            def ffn_in(l, f0, between=None):
                ffn_in_step(l, 0, f0)
                if between:
                    between()
                with pool.Fori(1, 4) as it:
                    ffn_in_step(l, it, f0)

            pool.sem_inc(S["act_ready"], 2)
            pool.sem_inc(S["actlo_ready"], 2)
            pool.sem_inc(S["sq_added"], 1)
            pool.dma_start(ropeQ[:, :].bitcast(I32), positions.broadcast_to([P, T])).then_inc(S["pos_loaded"], 16)
            with pool.Fori(0, DEPTH) as l:
                squares_sum(lambda c: l * 12 + (c + 1), "x_sq", l * 16 + 1)
                pool.wait_ge(S["hlo_ready"], l * (3 * KB) + KB)
                pool.sem_inc(S["pool_waited"], 1)
                pool.dma_start(mem32, memT.rearrange("(k p) t -> p k t", p=P)).then_inc(S["mem_loaded"], 16)
                pool.dma_start(par[:, :], params[bass.ds(l, 1), :, :].rearrange("a p n -> p (a n)"))\
                    .then_inc(S["par_loaded"], 16)
                ffn_in(l, 0, lambda: squares_sum(lambda c: l + 1, "mem_sq", l * 16 + 5))
                squares_sum(lambda c: l * 12 + (4 + c + 1), "x_sq", l * 16 + 9)

                def squares_low(n, sq, place):
                    pool.wait_ge(S["sq_high"], l * 5 + n)
                    TT(place[1], sq, f(place[0]), ALU.subtract).then_inc(S["sq_low"], 1)

                squares_low(1, memksq, sq_place[0])
                pool.wait_ge(S["lat_sq"], l + 1)
                lq = latsq.rearrange("p (a b) n -> p a b n", b=2)
                TT(lq[:, :, 0, :], lq[:, :, 0, :], lq[:, :, 1, :], ALU.add).then_inc(S["lat_sq_all"], 1)
                half = slice(0, ROPE)
                pool.wait_ge(S["mq_sq"], l * 2 + 2)
                TT(mqsq[half], mqsq[half], mqrsq[half], ALU.add).then_inc(S["mq_sq_all"], 1)
                pool.wait_ge(S["mk_sq"], l + 1)
                pool.wait_ge(S["krsq_ready"], l + 1)
                TT(mksq[half], mksq[half], rows(krsq[half, :], 1).broadcast_to([ROPE, HEADS, T]), ALU.add)\
                    .then_inc(S["mk_sq_all"], 1)
                squares_low(2, mqsq, sq_place[0])
                squares_low(3, mksq, sq_place[1])
                squares_low(4, sbqsq, sq_place[0])
                squares_low(5, sbksq, sq_place[1])
                with pool.Fori(0, HEADS) as i:
                    base = pool.snap(l * TURNS + i * 2)
                    lo(base, B_GATE)
                    pool.wait_ge(S["sb_lkh"], l * HEADS + i + 1)
                    TT(lkl, lk, f(lkh), ALU.subtract).then_inc(S["sb_lkl"], 1)
                    lo(base, B_GATE + 4)
                for u in range(2):
                    for c in range(4 - u):
                        if u == 0 and c % 2 == 0:
                            lo(l * TURNS, B_BRANCH + 2 * c)
                        if u == 0 and c == 0:
                            pool.wait_ge(S["conv_tap"], l * (4 * 32) + (4 * 32 + 1))
                            TT(ysum, ypad[:, 0:2, PAD:PAD + T], ypad[:, 2:4, PAD:PAD + T], ALU.add)\
                                .then_inc(S["y_paired"], 1)
                        if u == 0 and c == 1:
                            pool.wait_ge(S["ln_sq"], l + 1)
                            TT(ysum, ysq[:, 0:2, :], ysq[:, 2:4, :], ALU.add).then_inc(S["ysq_paired"], 1)
                        o = O_BRANCH + 4 * u + c
                        m, p = hf[:, 2 * c:2 * c + 2, :], prod[c % 2]
                        pool.wait_ge(read[o % 2], read_value(o, l * HALF_OUT))
                        if u == 1:
                            pool.wait_ge(S["merged_ready"], l * 8 + (c + 1))
                            TT(m, m, p[0], ALU.add).then_inc(S["prod_added"], 1)
                            pool.wait_ge(S["prod_added"], l * 4 + (c + 1))
                        TT(m, m, p[1], ALU.add).then_inc(S["merged_ready"], 1)
                squares_sum(lambda c: l * 12 + (8 + c + 1), "x_sq", l * 16 + 13)
                ffn_in(l, 8)

        @block.scalar
        def _(act):
            A = nc.scalar.activation

            def exp_ln_table():
                nc.scalar.preload_act_table_set("natural_log_exp_and_others")

            def level():
                act.sem_inc(S["act_waited"], 1)

            def hi(base, b):
                b += AHEAD
                act.wait_ge(raw_ready[b % RING], base * 16 + 16 * (b // RING + 1))
                act.wait_ge(S["block_done"], base * RING + (b + 1))
                A(whi[:, b % RING, :], raw[:, b % RING, :], ACT.Copy).then_inc(S["hi_ready"], 1)

            def group(o, base, b):
                act.wait_ge(S["block_done"], base * RING + (b + 1 + RING))
                return 2 * (o % 2)

            def root(sums, dst, n, s_sum, v, number, s_r):
                act.wait_ge(S[s_sum], v)
                A(dst, sums, ACT.Ln, bias=eps, scale=1.0 / n).then_inc(S["root_ln"], 1)
                act.wait_ge(S["root_ln"], number)
                A(dst, dst, ACT.Exp, scale=-0.5).then_inc(S[s_r], 1)

            def x_root(value, number):
                root(PS[:, BANK_NORM, 0:T], xr, D_MODEL, "ssq_ready", value, number, "rms_ready")

            def x_square(i, k):
                A(hf[:, at(i, k, 2), :], x[:, at(i, k, 2), :], ACT.Square).then_inc(S["x_sq"], 1)

            def x_high(i, k, col):
                for m in (0, 1):
                    A(hhi[:, at(i, k + m), :].rearrange("p a n -> p (a n)"),
                      x[:, at(i, k + m), :].rearrange("p a n -> p (a n)"), ACT.Identity,
                      scale=par[:, at(i, col + k + m)]).then_inc(S["hhi_ready"], 1)

            def act_high(n0, n, place):
                act.wait_ge(S["act_ready"], n0 + (n + 2))
                level()
                A(acthi[:, place, :], act32[(n + 1) % 2], ACT.Copy).then_inc(S["acthi_ready"], 1)

            def ffn_in_step(l, it, b0, o0, f0, value=None, number=None):
                base, hb = act.snap(l * TURNS + it * 2), act.snap(l * HALF_OUT + it * 2)
                n0 = act.snap(l * 16 + it * 2)
                for j in range(2):
                    hi(base, b0 + 4 * j)
                    hi(base, b0 + 4 * j + 1)
                    if value is not None and j == 0:
                        x_root(value, number)
                        nc.scalar.preload_act_table(ACT.Silu)
                    if value is None or j:
                        act_high(n0, f0 + j, at(it * 4, 2 * j - 2, 2))
                    o = o0 + 2 * j
                    act.wait_ge(read[0], read_value(o, hb))
                    A(silu[j], silu[j], ACT.Silu).then_inc(S["silu_ready"], 1)
                    hi(base, b0 + 4 * j + 2)
                    hi(base, b0 + 4 * j + 3)
                    if f0 == 0 and value is not None and j == 1:
                        act.wait_ge(S["mem_loaded"], l * 16 + 16)
                        A(hf[:, :, :], mem32, ACT.Square).then_inc(S["mem_sq"], 1)

            def ffn_in(l, b0, o0, f0, value, number):
                ffn_in_step(l, 0, b0, o0, f0, value, number)
                with act.Fori(1, 4) as it:
                    ffn_in_step(l, it, b0, o0, f0)
                act_high(act.snap(l * 16), f0 + 8, slice(2 * KB - 2, 2 * KB))

            def squares_high(sq, place, s_sq, v):
                act.wait_ge(S[s_sq], v)
                A(place[0], sq, ACT.Copy).then_inc(S["sq_high"], 1)

            def ffn_out_step(l, it, b0, o0, col=None, between=None):
                base, hb = act.snap(l * TURNS + it * 2), act.snap(l * HALF_OUT + it)
                for j in range(2):
                    for k in range(4):
                        if between and (j, k) == (0, 2):
                            between()
                        hi(base, b0 + 4 * j + k)
                    act.wait_ge(read[(o0 + j) % 2], read_value(o0 + j, hb))
                    level()
                    if col is not None:
                        x_high(it * 4, 2 * j, col)
                    x_square(it * 4, 2 * j)

            act.sem_inc(read[0], 1)
            act.sem_inc(read[1], 1)
            hi(0, -AHEAD)
            act.wait_ge(S["par0_loaded"], 16)
            for c in range(4):
                act.wait_ge(x_loaded[c], 16)
                x_high(0, 2 * c, C_FFN1)
                if c in (1, 3):
                    hi(0, c // 2 + 1 - AHEAD)
            for c in range(4):
                x_square(0, 2 * c)
            act.wait_ge(S["const_loaded"], 16)
            A(ones_r, ones, ACT.Copy).then_inc(S["rounded_ready"], 1)
            A(later_r, later, ACT.Copy).then_inc(S["rounded_ready"], 1)
            act.wait_ge(S["rope_step"], 9)
            A(sinK[:, :], krsq[:, :], ACT.Sin).then_inc(S["rope_step"], 1)
            A(cosT[:, :], krot[:, :], ACT.Sin).then_inc(S["rope_step"], 1)
            exp_ln_table()
            with act.Fori(0, DEPTH) as l:
                lb, lh, lr = act.snap(l * TURNS), act.snap(l * HALF_OUT), act.snap(l * NROOT + 2)
                l1 = act.snap(l + 1)
                ffn_in(l, B_F1, O_F1, 0, l * 3 + 1, l * NROOT + 1)
                exp_ln_table()
                root(PS[:, BANK_MEM, 0:T], memr, D_MODEL, "mem_ssq", l1, lr + R_MEM, "mem_r")
                ffn_out_step(l, 0, B_F2, O_F2)

                def mem_high():
                    act.wait_ge(S["memh_ready"], l * KB + KB)
                    for c in range(4):
                        A(m_hi2[c], mem32[:, 2 * c:2 * c + 2, :], ACT.Copy).then_inc(S["memhi_ready"], 1)

                ffn_out_step(l, 1, B_F2, O_F2, between=mem_high)
                for c in range(4):
                    hi(lb, B_MEM + 2 * c)
                    hi(lb, B_MEM + 2 * c + 1)
                    o = O_MEM + c
                    q = group(o, lb, B_MEM + 2 * c + 1)
                    dst = memk[:, 2 * c:2 * c + 2, :] if c < 2 else vall[:, 4:6, (c - 2) * 256:(c - 1) * 256]
                    A(dst, PS[:, q:q + 2, 0:T], ACT.Copy).then_inc(read[o % 2], 1)
                    if c == 0:
                        x_root(l * 3 + 2, lr + R_MIX)
                    if c in (1, 2):
                        for k in range(4 * c - 4, 4 * c):
                            act.wait_ge(S["hf_ready"], l * KB + (k + 1))
                            A(hhi[:, k, :], hf[:, k, :], ACT.Copy).then_inc(S["hhi_ready"], 1)
                    if c == 1:
                        for e in (o - 1, o):
                            act.wait_ge(read[e % 2], read_value(e, lh))
                        A(memksq, memk[:, :, :], ACT.Square).then_inc(S["memk_sq"], 1)
                        squares_high(memksq, sq_place[0], "memk_sq", l1)
                for c in range(2):
                    hi(lb, B_LAT + 2 * c)
                    if c == 0:
                        root(PS[:, 4:6, :], two_banks(memkr), HEAD_DIM, "memk_ssq", l1, lr + R_MEMK, "memk_r")
                    hi(lb, B_LAT + 2 * c + 1)
                    o = O_LAT + c
                    q = group(o, lb, B_LAT + 2 * c + 1)
                    A(lat32[:, 2 * c:2 * c + 2, :], PS[:, q:q + 2, 0:T], ACT.Copy).then_inc(read[o % 2], 1)
                for o in (O_LAT, O_LAT + 1):
                    act.wait_ge(read[o % 2], read_value(o, lh))
                A(latsq, lat32, ACT.Square).then_inc(S["lat_sq"], 1)
                act.wait_ge(S["pad_zeroed"], l1)
                for c in range(2):
                    for part in range(2):
                        b, o = B_CONV + 4 * c + 2 * part, O_CONV + 2 * c + part
                        hi(lb, b)
                        hi(lb, b + 1)
                        if c == 1 and part == 0:
                            act.wait_ge(S["lat_normed"], l * 4 + 4)
                            A(lathi[:, :, :], lat32, ACT.Copy).then_inc(S["lathi_ready"], 1)
                            act.wait_ge(S["hi_ready"], lb * RING + (B_UP + 1))
                            A(wide(acthi), runs(f(whi[:, B_UP % RING, :])), ACT.Copy).then_inc(S["widehi_ready"], 1)
                        q = group(o, lb, b + 1)
                        if part == 0:
                            A(ypad[:, 2 * c:2 * c + 2, PAD:PAD + T], PS[:, q:q + 2, 0:T], ACT.Copy)\
                                .then_inc(read[o % 2], 1)
                        else:
                            A(glu[c], PS[:, q:q + 2, 0:T], ACT.Sigmoid).then_inc(read[o % 2], 1)
                        if c == part == 0:
                            root(PS[:, BANK_MLA, :], latr, LORA, "lat_ssq", l1, lr + R_LAT, "lat_r")
                exp_ln_table()
                act.wait_ge(S["glu_ready"], l * 2 + 2)
                dsts = [mlaqk[:, 1, :, :], mlaqk[:, 0, :, :], mlaqk[:, 2, :, :], vall[:, 2:4, :]]
                squares = [(mqrsq, "mq_sq"), (mqsq, "mq_sq"), (mksq, "mk_sq")]
                for c in range(4):
                    hi(lb, B_UP + c)
                    if c == 0:
                        act.wait_ge(S["kr_ready"], l1)
                        A(krsq[:, :], PS[:, BANK_NORM, 0:T], ACT.Square).then_inc(S["krsq_ready"], 1)
                    o = O_UP + c
                    q = group(o, lb, B_UP + c)
                    src = PS[:, q:q + 2, :] if c == 3 else PS[:, q:q + 2, :].rearrange("p a (b n) -> p (a b) n", b=2)
                    A(dsts[c], src, ACT.Copy).then_inc(read[o % 2], 1)
                    if c < 3:
                        act.wait_ge(read[o % 2], read_value(o, lh))
                        A(squares[c][0], dsts[c], ACT.Square).then_inc(S[squares[c][1]], 1)
                stages = [(B_SBQ + 2 * c, O_SBQ + c, hf[:, 2 * c:2 * c + 2, :]) for c in range(4)]
                stages += [(B_MEMQ + 2 * c, O_MEMQ + c, memq[:, 2 * c:2 * c + 2, :]) for c in range(2)]
                stages += [(B_SBV + 2 * c, O_SBV + c, vall[:, 0:2, c * 256:(c + 1) * 256]) for c in range(2)]
                for c, (b, o, dst) in enumerate(stages):
                    hi(lb, b)
                    if c == 0:
                        squares_high(mqsq, sq_place[0], "mq_sq_all", l1)
                    if c == 2:
                        root(PS[:, 4:6, :], two_banks(mqR), HEAD_DIM + ROPE, "mq_ssq", l1, lr + R_MQ, "mq_r")
                        squares_high(sbqsq, sq_place[0], "sbq_sq", l1)
                    if c == 3:
                        root(PS[:, 6:8, :], two_banks(mkR), HEAD_DIM + ROPE, "mk_ssq", l1, lr + R_MK, "mk_r")
                    if c == 5:
                        root(PS[:, 4:6, :], two_banks(sbqR), HEAD_DIM, "sbq_ssq", l1, lr + R_SBQ, "sbq_r")
                    if c == 6:
                        root(PS[:, 6:8, :], two_banks(sbkR), HEAD_DIM, "sbk_ssq", l1, lr + R_SBK, "sbk_r")
                    hi(lb, b + 1)
                    if c == 7:
                        root(PS[:, 4:6, :], two_banks(eqR), HEAD_DIM, "eq_ssq", l1, lr + R_EQ, "eq_r")
                    q = group(o, lb, b + 1)
                    A(dst, PS[:, q:q + 2, 0:T], ACT.Copy).then_inc(read[o % 2], 1)
                    if c in (1, 3, 5):
                        for e in (o - 1, o):
                            act.wait_ge(read[e % 2], read_value(e, lh))
                    if c == 0:
                        squares_high(mksq, sq_place[1], "mk_sq_all", l1)
                    if c == 1:
                        act.wait_ge(S["sq_low"], l * 5 + 2)
                        A(sbqsq, hf[:, 0:4, :], ACT.Square).then_inc(S["sbq_sq"], 1)
                    if c == 3:
                        act.wait_ge(S["mq_normed"], l * 2 + 2)
                        A(sbksq, hf[:, 4:8, :], ACT.Square).then_inc(S["sbk_sq"], 1)
                        squares_high(sbksq, sq_place[1], "sbk_sq", l1)
                    if c == 5:
                        act.wait_ge(S["mk_normed"], l * 2 + 2)
                        A(eqsq, memq[:, :, :], ACT.Square).then_inc(S["eq_sq"], 1)
                for o in (O_SBV, O_SBV + 1):
                    act.wait_ge(read[o % 2], read_value(o, lh))
                act.wait_ge(S["mq_normed"], l * 2 + 2)
                act.wait_ge(S["sbk_normed"], l1)
                act.wait_ge(S["sbq_normed"], l1)
                act.wait_ge(S["eq_normed"], l1)
                with act.Fori(0, HEADS) as i:
                    n1 = act.snap(l * HEADS + i + 1)
                    base = act.snap(l * TURNS + i * 2)

                    def gate(g):
                        hi(base, B_GATE + 2 * g)
                        hi(base, B_GATE + 2 * g + 1)

                    def keep(g):
                        o = O_GATE + g
                        q = group(o, base, B_GATE + 2 * g + 1)
                        level()
                        A(gates[:, bass.ds(i, 1), 2 * g:2 * g + 2, :].rearrange("p a k n -> p (a k) n"),
                          PS[:, q:q + 2, 0:T], ACT.Copy).then_inc(read[o % 2], 1)

                    for dst, src in ((sbk, hf[:, bass.ds(i + 4, 1), :].rearrange("p a n -> p (a n)")),
                                     (mq, mlaqk[:, 0, i, :]), (mqr, mlaqk[:, 1, i, :]), (eq, memq[:, i, :])):
                        A(dst, src, ACT.Copy).then_inc(S["fixed_ready"], 1)
                    A(vh, vall[:, :, bass.ds(i * HEAD_DIM, HEAD_DIM)], ACT.Copy).then_inc(S["vh_ready"], 1)
                    gate(0)
                    keep(0)
                    act.wait_ge(S["sb_z"], n1)
                    A(sbL, PS[:, BANK_SB, 0:384], ACT.Abs, scale=SB_SCALE).then_inc(S["sb_abs"], 1)
                    A(relu, PS[:, BANK_SB, 0:384], ACT.Relu, scale=SB_SCALE).then_inc(S["sb_relu"], 1)
                    act.wait_ge(S["sb_abs"], n1)
                    A(sbL, sbL, ACT.Exp, scale=-1.0).then_inc(S["sb_exp"], 1)
                    act.wait_ge(S["sb_exp"], n1)
                    A(sbL, sbL, ACT.Ln, bias=one).then_inc(S["sb_L"], 1)
                    gate(1)
                    act.wait_ge(S["mla_neg"], n1)
                    A(mP[:, 0:P], PS[:, BANK_MLA, 0:P], ACT.Exp, scale=MLA_SCALE, bias=stat[:, 2:3],
                      accum_out=stat[:, 4:5]).then_inc(S["mla_p"], 1)
                    A(mP[:, P:384], PS[:, BANK_MLA, P:384], ACT.Exp, scale=MLA_SCALE, bias=stat[:, 3:4],
                      accum_out=stat[:, 5:6]).then_inc(S["mla_p"], 1)
                    act.wait_ge(S["e_neg"], n1)
                    for j in range(2):
                        A(eP[:, j * T:(j + 1) * T], PS[:, BANK_MEM, j * T:(j + 1) * T], ACT.Exp, scale=SB_SCALE,
                          bias=stat[:, 10 + j:11 + j], accum_out=stat[:, 12 + j:13 + j]).then_inc(S["e_p"], 1)
                    act.wait_ge(S["sb_lkm"], n1)
                    A(lkh, lk, ACT.Copy).then_inc(S["sb_lkh"], 1)
                    keep(1)
                    gate(2)
                    keep(2)
                    gate(3)
                    act.wait_ge(S["sb_logw"], n1)
                    A(lw, lw, ACT.Exp).then_inc(S["sb_expw"], 1)
                    act.wait_ge(S["mla_transposed"], n1)
                    A(mPT, PS[:, BANK_MLA, 0:384], ACT.Copy).then_inc(S["mla_PT"], 1)
                    act.wait_ge(S["e_transposed"], n1)
                    A(ePT, PS[:, BANK_MEM, :], ACT.Copy).then_inc(S["e_PT"], 1)
                    keep(3)
                    act.wait_ge(S["mla_pv"], n1)
                    level()
                    A(b2hi[:, i, :], PS[:, BANK_MLA, 0:T], ACT.Copy).then_inc(S["mla_hi"], 1)
                    act.wait_ge(S["e_pv"], n1)
                    level()
                    A(b3hi[:, i, :], PS[:, BANK_MEM, 0:T], ACT.Copy).then_inc(S["e_hi"], 1)
                    act.wait_ge(S["sb_pv"], n1)
                    level()
                    A(b1hi[:, i, :], PS[:, BANK_SB, 0:T], ACT.Copy).then_inc(S["sb_hi"], 1)
                for o in (O_GATE + 14, O_GATE + 15):
                    act.wait_ge(read[o % 2], read_value(o, lh))
                def merge_high(c):
                    act.wait_ge(S["merged_ready"], l * 8 + (4 + c + 1))
                    A(m_hi2[c], hf[:, 2 * c:2 * c + 2, :], ACT.Copy).then_inc(S["mergedhi_ready"], 1)

                for u in range(2):
                    for c in range(4):
                        hi(lb, B_BRANCH + 8 * u + 2 * c)
                        hi(lb, B_BRANCH + 8 * u + 2 * c + 1)
                        j0 = 2 - 2 * u
                        for e in (c,) if u else ((0, 1), (2, 3), (), ())[c]:
                            for j in (j0, j0 + 1):
                                g = gates[:, j, 2 * e:2 * e + 2, :]
                                A(g, g, ACT.Sigmoid).then_inc(S["gate_sig"], 1)
                        if u == 0 and c == 0:
                            act.wait_ge(S["ln_c"], l1)
                            A(ysq, yc, ACT.Square).then_inc(S["ln_sq"], 1)
                        if u == 0 and c == 1:
                            exp_ln_table()
                            root(PS[:, BANK_NORM, 0:T], yr, CONV_CH, "ln_var", l1, lr + R_CONV, "ln_r")
                        if u == 0 and c == 2:
                            act.wait_ge(S["ln_n"], l1)
                            for k in range(4):
                                A(y32[:, k, :], yc[:, k, :], ACT.Silu,
                                  scale=par[:, C_LNG + k:C_LNG + k + 1], bias=par[:, C_LNB + k:C_LNB + k + 1])\
                                    .then_inc(S["ln_silu"], 1)
                            act.wait_ge(S["ln_silu"], l * 4 + 4)
                            A(b0hi[:, :, :], y32, ACT.Copy).then_inc(S["b0hi_ready"], 1)
                        if u == 1 and c:
                            merge_high(c - 1)
                merge_high(3)
                exp_ln_table()
                for c in range(4):
                    hi(lb, B_OUT + 2 * c)
                    hi(lb, B_OUT + 2 * c + 1)
                    o = O_OUT + c
                    act.wait_ge(read[o % 2], read_value(o, lh))
                    act.wait_ge(S["mergedlo_ready"], l * 4 + 4)
                    x_high(0, 2 * c, C_FFN2)
                    x_square(0, 2 * c)
                ffn_in(l, B_G1, O_G1, 8, l * 3 + 3, lr + R_FFN2)
                exp_ln_table()
                with act.Fori(0, 2) as it:
                    ffn_out_step(l, it, B_G2, O_G2, C_NEXT)

        @block.vector
        def _(dve):
            V = nc.vector
            STT, TT, TS = V.scalar_tensor_tensor, V.tensor_tensor, V.tensor_scalar

            def lo(base, b):
                b += AHEAD
                dve.wait_ge(S["hi_ready"], base * RING + (b + 1))
                TT(wlo[:, b % RING, :], raw[:, b % RING, :], f(whi[:, b % RING, :]), ALU.subtract)\
                    .then_inc(lo_ready[b % RING], 1)

            def group(o, base, b):
                dve.wait_ge(S["block_done"], base * RING + (b + 1 + RING))
                return 2 * (o % 2)

            def x_low(h0, i, k, col):
                for m in (0, 1):
                    dve.wait_ge(S["hhi_ready"], h0 + (k + m + 1))
                    STT(hlo[:, at(i, k + m), :], x[:, at(i, k + m), :], par[:, at(i, col + k + m)],
                        f(hhi[:, at(i, k + m), :]), ALU.mult, ALU.subtract).then_inc(S["hlo_ready"], 1)

            def ffn_in_step(l, it, b0, o0, f0, value=None):
                base, hb = dve.snap(l * TURNS + it * 2), dve.snap(l * HALF_OUT + it * 2)
                n0 = dve.snap(l * 16 + it * 2)
                for j in range(2):
                    for part, place in ((0, silu), (1, up32)):
                        lo(base, b0 + 4 * j + 2 * part)
                        lo(base, b0 + 4 * j + 2 * part + 1)
                        if value is not None and j == part == 0:
                            dve.wait_ge(S["rms_ready"], value)
                        o = o0 + 2 * j + part
                        q = group(o, base, b0 + 4 * j + 2 * part + 1)
                        dve.wait_ge(S["act_ready"], n0 + (f0 + j + 1))
                        TT(place[j], PS[:, q:q + 2, 0:T], each_of(xr, 2), ALU.mult).then_inc(read[part], 1)

            def ffn_in(l, b0, o0, f0, value):
                ffn_in_step(l, 0, b0, o0, f0, value)
                with dve.Fori(1, 4) as it:
                    ffn_in_step(l, it, b0, o0, f0)

            def update(o, base, b, two, scale):
                q = group(o, base, b)
                STT(x[:, two, :], PS[:, q:q + 2, 0:T], scale, x[:, two, :], ALU.mult, ALU.add).then_inc(read[o % 2], 1)

            def ffn_out_step(l, it, b0, o0, col=None, between=None):
                base = dve.snap(l * TURNS + it * 2)
                for j in range(2):
                    for k in range(3):
                        if between and (j, k) == (0, 2):
                            between()
                        lo(base, b0 + 4 * j + k)
                    update(o0 + j, base, b0 + 4 * j + 3, at(it * 4, 2 * j, 2), 0.5)
                    if col is not None:
                        dve.wait_ge(read[(o0 + j) % 2], read_value(o0 + j, l * HALF_OUT + it))
                        x_low(l * (3 * KB) + it * 4 + 3 * KB, it * 4, 2 * j, col)
                    lo(base, b0 + 4 * j + 3)

            def head_norm(tile, gain, r, s_r, v, s_normed):
                dve.wait_ge(S[s_r], v)
                STT(flat(tile), flat(tile), par[:, gain:gain + 1], flat(r), ALU.mult, ALU.mult).then_inc(S[s_normed], 1)

            for s in ("sb_lo", "mla_lo", "e_lo", "conv_tap"):
                dve.sem_inc(S[s], 1)
            dve.wait_ge(S["par0_loaded"], 16)
            lo(0, -AHEAD)
            for c in range(4):
                x_low(0, 0, 2 * c, C_FFN1)
                if c in (1, 3):
                    lo(0, c // 2 + 1 - AHEAD)
            dve.wait_ge(S["pos_loaded"], 16)
            dve.wait_ge(S["const_loaded"], 16)

            def rope(step, ins):
                ins.then_inc(S["rope_step"], 1)
                dve.wait_ge(S["rope_step"], step)

            rope(1, V.tensor_copy(qtab[:, :], ropeQ[:, :].bitcast(I32)))
            rope(2, TS(krsq[:, :], qtab[:, :], con[:, K_FREQ:K_FREQ + 1], None, ALU.mult))
            rope(3, TS(krot[:, :], krsq[:, :], 1.0 / (2 * np.pi), ROUNDER, ALU.mult, ALU.add))
            rope(4, TS(krot[:, :], krot[:, :], ROUNDER, None, ALU.subtract))
            rest, parts = 2 * np.pi, []
            for bits in (5, 13):
                parts.append(float(np.floor(rest * 2.0 ** bits) / 2.0 ** bits))
                rest -= parts[-1]
            for k, part in enumerate(parts + [float(rest)]):
                rope(5 + k, STT(krsq[:, :], krot[:, :], -part, krsq[:, :], ALU.mult, ALU.add))
            rope(8, STT(krot[:, :], krsq[:, :], -1.0, krsq[:, :], ALU.mult, ALU.max))
            rope(9, TS(krot[:, :], krot[:, :], -1.0, np.pi / 2, ALU.mult, ALU.add))
            dve.wait_ge(S["rope_step"], 11)
            rope(12, TS(ropeQ[:, :], cosT[:, :], con[:, K_QC:K_QC + 1], None, ALU.mult))
            rope(13, STT(ropeQ[:, :], sinK[:, :], con[:, K_QS:K_QS + 1], ropeQ[:, :], ALU.mult, ALU.add))
            rope(14, TS(sinK[:, :], sinK[:, :], con[:, K_KS:K_KS + 1], None, ALU.mult))
            with dve.Fori(0, DEPTH) as l:
                lb, lh = dve.snap(l * TURNS), dve.snap(l * HALF_OUT)
                l1 = dve.snap(l + 1)
                ffn_in(l, B_F1, O_F1, 0, l * 3 + 1)
                ffn_out_step(l, 0, B_F2, O_F2)
                dve.wait_ge(S["par_loaded"], l * 16 + 16)
                dve.wait_ge(S["mem_r"], l1)
                for k in range(KB):
                    STT(mem32[:, k, :], mem32[:, k, :], par[:, C_MEM + k:C_MEM + k + 1], memr,
                        ALU.mult, ALU.mult).then_inc(S["memh_ready"], 1)

                def mem_low():
                    for c in range(4):
                        dve.wait_ge(S["memhi_ready"], l * 4 + (c + 1))
                        TT(m_lo2[c], mem32[:, 2 * c:2 * c + 2, :], f(m_hi2[c]), ALU.subtract)\
                            .then_inc(S["memlo_ready"], 1)

                ffn_out_step(l, 1, B_F2, O_F2, between=mem_low)
                for k in range(8):
                    lo(lb, B_MEM + k)
                    if k == 1:
                        dve.wait_ge(S["rms_ready"], l * 3 + 2)
                        for kb in range(4):
                            STT(hf[:, kb, :], x[:, kb, :], par[:, C_MIX + kb:C_MIX + kb + 1], xr, ALU.mult, ALU.mult)\
                                .then_inc(S["hf_ready"], 1)
                    if k == 2:
                        for kb in range(4, 8):
                            STT(hf[:, kb, :], x[:, kb, :], par[:, C_MIX + kb:C_MIX + kb + 1], xr, ALU.mult, ALU.mult)\
                                .then_inc(S["hf_ready"], 1)
                    if k in (4, 6):
                        for kb in range(2 * k - 8, 2 * k - 4):
                            dve.wait_ge(S["hhi_ready"], l * (3 * KB) + (KB + kb + 1))
                            TT(hlo[:, kb, :], hf[:, kb, :], f(hhi[:, kb, :]), ALU.subtract).then_inc(S["hlo_ready"], 1)
                V.memset(ypad[:, :, 0:PAD], 0.0).then_inc(S["pad_zeroed"], 1)
                TS(qtab[:, :], ropeQ[:, :], par[:, C_MQR:C_MQR + 1], None, ALU.mult).then_inc(S["qtab_ready"], 1)
                for k in range(4):
                    lo(lb, B_LAT + k)
                    if k == 2:
                        head_norm(memk[:, :, :], C_EK, memkr, "memk_r", l1, "memk_normed")
                for c in range(2):
                    for k in range(4):
                        lo(lb, B_CONV + 4 * c + k)
                        if c == 0 and k == 3:
                            dve.wait_ge(S["lat_r"], l1)
                            for kb in range(4):
                                STT(lat32[:, kb, :], lat32[:, kb, :], par[:, C_QLAT + kb:C_QLAT + kb + 1],
                                    latr[:, (kb // 2) * T:(kb // 2 + 1) * T], ALU.mult, ALU.mult)\
                                    .then_inc(S["lat_normed"], 1)
                        if c == 1 and k == 1:
                            dve.wait_ge(S["lathi_ready"], l1)
                            TT(latlo[:, :, :], lat32, f(lathi[:, :, :]), ALU.subtract).then_inc(S["latlo_ready"], 1)
                            dve.wait_ge(lo_ready[B_UP % RING], lb + (B_UP // RING + 1))
                            V.tensor_copy(wide(actlo), runs(f(wlo[:, B_UP % RING, :]))).then_inc(S["widelo_ready"], 1)
                    for o in (O_CONV + 2 * c, O_CONV + 2 * c + 1):
                        dve.wait_ge(read[o % 2], read_value(o, lh))
                    y = ypad[:, 2 * c:2 * c + 2, PAD:PAD + T]
                    TT(y, y, glu[c], ALU.mult).then_inc(S["glu_ready"], 1)
                lo(lb, B_UP)
                dve.wait_ge(S["krsq_ready"], l1)
                TS(krg, PS[:, BANK_NORM, 0:T], par[:, C_MKR:C_MKR + 1], None, ALU.mult).then_inc(S["krg_ready"], 1)
                lo(lb, B_UP + 1)
                lo(lb, B_UP + 2)
                dve.wait_ge(S["kr_permuted"], l1)
                TT(krt[:, 0, :], PS[:, BANK_NORM, 0:T], cosT[:, :], ALU.mult).then_inc(S["krt_ready"], 1)
                TT(krt[:, 1, :], PS[:, BANK_NORM, T:2 * T], sinK[:, :], ALU.mult).then_inc(S["krt_ready"], 1)
                lo(lb, B_UP + 3)
                dve.wait_ge(S["krt_ready"], l * 2 + 2)
                TT(krot[:, :], krt[:, 0, :], krt[:, 1, :], ALU.add).then_inc(S["krot_ready"], 1)
                for c, b in enumerate([B_SBQ, B_SBQ + 2, B_SBQ + 4, B_SBQ + 6, B_MEMQ, B_MEMQ + 2, B_SBV, B_SBV + 2]):
                    lo(lb, b)
                    lo(lb, b + 1)
                    if c == 2:
                        qr = mlaqk[:, 1, :, :]
                        dve.wait_ge(S["mq_sq"], l * 2 + 2)
                        dve.wait_ge(S["qtab_ready"], l1)
                        TT(qr, qr, each_of(qtab[:, :], HEADS), ALU.mult).then_inc(S["mq_tabled"], 1)
                        head_norm(mlaqk[:, 0, :, :], C_MQN, mqR, "mq_r", l1, "mq_normed")
                        dve.wait_ge(S["mq_tabled"], l1)
                        TT(qr, qr, mqR, ALU.mult).then_inc(S["mq_normed"], 1)
                    if c == 3:
                        head_norm(mlaqk[:, 2, :, :], C_MKN, mkR, "mk_r", l1, "mk_normed")
                        dve.wait_ge(S["krot_ready"], l1)
                        TT(mlaqk[:, 3, :, :], each_of(krot[:, :], HEADS), mkR, ALU.mult).then_inc(S["mk_normed"], 1)
                    if c == 5:
                        head_norm(hf[:, 0:4, :], C_SBQ, sbqR, "sbq_r", l1, "sbq_normed")
                    if c == 6:
                        head_norm(hf[:, 4:8, :], C_SBK, sbkR, "sbk_r", l1, "sbk_normed")
                    if c == 7:
                        head_norm(memq[:, :, :], C_EQ, eqR, "eq_r", l1, "eq_normed")
                dve.wait_ge(S["eq_normed"], l1)
                dve.wait_ge(S["glu_ready"], l * 2 + 2)
                dve.sem_inc(S["dve_waited"], 1)
                with dve.Fori(0, HEADS) as i:
                    n1 = dve.snap(l * HEADS + i + 1)
                    base = dve.snap(l * TURNS + i * 2)
                    taps = dve.snap((l * HEADS + i) * 32)
                    wcol = dve.snap(i * CONVW)

                    def conv(k0, k1):
                        for k in range(k0, k1):
                            w = par[:, bass.ds(wcol + (C_CONV + min(k, 30)), 1)]
                            y = ypad[:, bass.ds(i, 1), min(k, 30):min(k, 30) + T].rearrange("p a n -> p (a n)")
                            dve.wait_ge(S["conv_tap"], taps + (1 if k < 2 else k if k < 30 else k + 1))
                            if k == 0:
                                bias = par[:, bass.ds(wcol + (C_CONV + TAPS), 1)]
                                ins = TS(acc[0], y, w, bias, ALU.mult, ALU.add)
                            elif k == 1:
                                ins = TS(acc[1], y, w, None, ALU.mult)
                            elif k < 30:
                                ins = STT(acc[k % 2], y, w, acc[k % 2], ALU.mult, ALU.add)
                            elif k == 30:
                                ins = TT(acc[0], acc[0], acc[1], ALU.add)
                            else:
                                ins = STT(y, y, w, acc[0], ALU.mult, ALU.add)
                            ins.then_inc(S["conv_tap"], 1)

                    conv(0, 4)
                    lo(base, B_GATE + 1)
                    conv(4, 8)
                    lo(base, B_GATE + 2)
                    dve.wait_ge(S["mla_s"], n1)
                    V.memset(rows(PS[0:CHUNK, BANK_MLA, :], 2)[:, :, CHUNK:P], -1e30).then_inc(S["mla_masked"], 1)
                    dve.wait_ge(S["mla_masked"], n1)
                    V.reduce_max(stat[:, 0:1], PS[:, BANK_MLA, 0:P], axis=AX.X).then_inc(S["mla_max"], 1)
                    V.reduce_max(stat[:, 1:2], PS[:, BANK_MLA, P:384], axis=AX.X).then_inc(S["mla_max"], 1)
                    dve.wait_ge(S["e_s"], n1)
                    V.reduce_max(stat[:, 8:10], rows(PS[:, BANK_MEM, :], 2), axis=AX.X).then_inc(S["e_max"], 1)
                    dve.wait_ge(S["mla_max"], n1 * 2)
                    TS(stat[:, 2:4], stat[:, 0:2], -MLA_SCALE, None, ALU.mult).then_inc(S["mla_neg"], 1)
                    dve.wait_ge(S["e_max"], n1)
                    TS(stat[:, 10:12], stat[:, 8:10], -SB_SCALE, None, ALU.mult).then_inc(S["e_neg"], 1)
                    dve.wait_ge(S["sb_relu"], n1)
                    dve.wait_ge(S["sb_L"], n1)
                    STT(lk, relu, -1.0, sbL, ALU.mult, ALU.subtract).then_inc(S["sb_lk"], 1)
                    lo(base, B_GATE + 3)
                    dve.wait_ge(S["sb_lk"], n1)
                    STT(lw, PS[:, BANK_SB, 0:384], SB_SCALE, lk, ALU.mult, ALU.add).then_inc(S["sb_a"], 1)
                    dve.wait_ge(S["sb_a"], n1)
                    TT(diag2(lk), diag2(lk), strict2, ALU.mult).then_inc(S["sb_lkm"], 1)
                    conv(8, 12)
                    dve.wait_ge(S["mla_p"], n1 * 2)
                    V.reciprocal(stat[:, 6:8], stat[:, 4:6]).then_inc(S["mla_rec"], 1)
                    dve.wait_ge(S["e_p"], n1 * 2)
                    V.reciprocal(stat[:, 14:16], stat[:, 12:14]).then_inc(S["e_rec"], 1)
                    dve.wait_ge(S["mla_rec"], n1)
                    TS(mP[:, 0:P], mP[:, 0:P], stat[:, 6:7], None, ALU.mult).then_inc(S["mla_pn"], 1)
                    TS(mP[:, P:384], mP[:, P:384], stat[:, 7:8], None, ALU.mult).then_inc(S["mla_pn"], 1)
                    dve.wait_ge(S["e_rec"], n1)
                    for j in range(2):
                        p = eP[:, j * T:(j + 1) * T]
                        TS(p, p, stat[:, 14 + j:15 + j], None, ALU.mult).then_inc(S["e_pn"], 1)
                    conv(12, 16)
                    lo(base, B_GATE + 5)
                    conv(16, 22)
                    dve.wait_ge(S["sb_later"], n1)
                    TT(lw, PS[:, BANK_SB, 0:384], lw, ALU.add).then_inc(S["sb_logw"], 1)
                    lo(base, B_GATE + 6)
                    conv(22, 26)
                    dve.wait_ge(S["sb_expw"], n1)
                    TT(diag2(lw), diag2(lw), strict2, ALU.mult).then_inc(S["sb_w"], 1)
                    lo(base, B_GATE + 7)
                    conv(26, 28)
                    for s, bank, dhi, dlo in (("mla", BANK_MLA, b2hi, b2lo), ("e", BANK_MEM, b3hi, b3lo),
                                              ("sb", BANK_SB, b1hi, b1lo)):
                        dve.wait_ge(S[s + "_hi"], n1)
                        TT(dlo[:, i, :], PS[:, bank, 0:T], f(dhi[:, i, :]), ALU.subtract).then_inc(S[s + "_lo"], 1)
                    conv(28, 32)
                for u in range(2):
                    for c in range(4):
                        if u or c % 2:
                            lo(lb, B_BRANCH + 8 * u + 2 * c)
                        lo(lb, B_BRANCH + 8 * u + 2 * c + 1)
                        if u == 0 and c == 0:
                            dve.wait_ge(S["ln_mean"], l1)
                            STT(yc, each_of(PS[:, BANK_NORM, 0:T], 4), -1.0 / CONV_CH, ypad[:, :, PAD:PAD + T],
                                ALU.mult, ALU.add).then_inc(S["ln_c"], 1)
                        if u == 0 and c == 1:
                            dve.wait_ge(S["ln_r"], l1)
                            TT(yc, yc, each_of(yr, 4), ALU.mult).then_inc(S["ln_n"], 1)
                        n = 4 * u + c
                        o = O_BRANCH + n
                        q = group(o, lb, B_BRANCH + 2 * n + 1)
                        j0 = 2 - 2 * u
                        g = [gates[:, j0 + s, 2 * c:2 * c + 2, :] for s in range(2)]
                        m, p = hf[:, 2 * c:2 * c + 2, :], prod[c % 2]
                        dve.wait_ge(S["gate_sig"], l * 16 + (2 * n + 2))
                        if n >= 2:
                            dve.wait_ge(S["merged_ready"], l * 8 + (n - 1))
                        first = m if u == 0 else p[0]
                        TT(first, PS[:, q:q + 2, 0:T], g[0], ALU.mult).then_inc(S["first_ready"], 1)
                        TT(p[1], PS[:, q:q + 2, T:2 * T], g[1], ALU.mult).then_inc(read[o % 2], 1)

                        def low(e):
                            dve.wait_ge(S["mergedhi_ready"], l * 4 + (e + 1))
                            TT(m_lo2[e], hf[:, 2 * e:2 * e + 2, :], f(m_hi2[e]), ALU.subtract)\
                                .then_inc(S["mergedlo_ready"], 1)

                        if u == 0 and c == 2:
                            dve.wait_ge(S["b0hi_ready"], l1)
                            TT(b0lo[:, :, :], y32, f(b0hi[:, :, :]), ALU.subtract).then_inc(S["b0lo_ready"], 1)
                        if u == 1 and c:
                            low(c - 1)
                        if n == 7:
                            dve.wait_ge(S["first_ready"], l * 8 + 8)
                            TT(m, m, p[0], ALU.add).then_inc(S["prod_added"], 1)
                            dve.wait_ge(read[o % 2], read_value(o, lh))
                            dve.wait_ge(S["prod_added"], l * 4 + 4)
                            TT(m, m, p[1], ALU.add).then_inc(S["merged_ready"], 1)
                            low(3)
                for c in range(4):
                    lo(lb, B_OUT + 2 * c)
                    update(O_OUT + c, lb, B_OUT + 2 * c + 1, slice(2 * c, 2 * c + 2), 1.0)
                    dve.wait_ge(read[(O_OUT + c) % 2], read_value(O_OUT + c, lh))
                    x_low(l * (3 * KB) + 2 * KB, 0, 2 * c, C_FFN2)
                    lo(lb, B_OUT + 2 * c + 1)
                ffn_in(l, B_G1, O_G1, 8, l * 3 + 3)
                with dve.Fori(0, 2) as it:
                    ffn_out_step(l, it, B_G2, O_G2, C_NEXT)

        @block.tensor
        def _(pe):
            MM = nc.tensor.matmul

            def split(out, whi_, wlo_, xhi, xlo, start, stop):
                MM(out, whi_, xhi, start=start, stop=False)
                MM(out, whi_, xlo, start=False, stop=False)
                return MM(out, wlo_, xhi, start=False, stop=stop)

            def turn(o, hb):
                pe.wait_ge(read[o % 2], hb + (o // 2 + 1))
                return 2 * (o % 2)

            def arrived(base, b):
                pe.wait_ge(lo_ready[b % RING], base + (b // RING + 1))

            def feature_block(base, b, out, xhi, xlo, first=True, last=True, each=None):
                arrived(base, b)
                s = b % RING
                for k in range(KB):
                    if each:
                        each(k)
                    w = slice(k * P, (k + 1) * P)
                    ins = split(out, whi[:, s, w], wlo[:, s, w], xhi[k], xlo[k], first and k == 0, last and k == KB - 1)
                ins.then_inc(S["block_done"], 1)

            def feature_pair(base, b, o, hb, xhi=h_hi, xlo=h_lo, each=None):
                q = turn(o, hb)
                for m in range(2):
                    feature_block(base, b + m, PS[:, q + m, 0:T], xhi, xlo, each=each if m == 0 else None)

            def token_pair(base, b, o, hb, xhi, xlo):
                q = turn(o, hb)
                for half in range(2):
                    arrived(base, b + half)
                    s = (b + half) % RING
                    for k in range(4):
                        kb, w = 4 * half + k, slice(k * 2 * P, (k + 1) * 2 * P)
                        for t in range(2):
                            tt = slice(t * P, (t + 1) * P)
                            out = PS[:, q + t, 0:T]
                            MM(out, xhi[kb][:, tt], whi[:, s, w], start=kb == 0, stop=False)
                            MM(out, xhi[kb][:, tt], wlo[:, s, w], start=False, stop=False)
                            ins = MM(out, xlo[kb][:, tt], whi[:, s, w], start=False, stop=kb == KB - 1)
                    ins.then_inc(S["block_done"], 1)

            def total(bank, value, s_sum):
                pe.wait_ge(S["const_loaded"], 16)
                pe.wait_ge(S["sq_added"], value)
                MM(PS[:, bank, 0:T], ones, hf[:, 0, :], start=True, stop=True).then_inc(S[s_sum], 1)

            def head_sums(bank, squares, s_sum):
                for half in range(2):
                    ins = MM(PS[:, bank + half, :], ones, flat(squares)[:, half * 512:(half + 1) * 512],
                             start=True, stop=True)
                ins.then_inc(S[s_sum], 1)

            def split_sums(bank, place, n, l, s_sum):
                pe.wait_ge(S["sq_low"], l * 5 + n)
                for half in range(2):
                    for m in range(2):
                        ins = MM(PS[:, bank + half, :], ones_r, flat(place[m])[:, half * 512:(half + 1) * 512],
                                 start=m == 0, stop=m == 1)
                ins.then_inc(S[s_sum], 1)

            def ffn_in_step(l, it, b0, o0, m, value=None):
                base, hb = pe.snap(l * TURNS + it * 2), pe.snap(l * HALF_OUT + it * 2)
                for j in range(4):
                    first = value is not None and j == 0
                    feature_pair(base, b0 + 2 * j, o0 + j, hb, each=normed(l, m) if first else None)
                    if first:
                        total(BANK_NORM, value, "ssq_ready")

            def ffn_in(l, b0, o0, m, value):
                ffn_in_step(l, 0, b0, o0, m, value)
                with pe.Fori(1, 4) as it:
                    ffn_in_step(l, it, b0, o0, m)

            def ffn_out(l, b0, o0, f0):
                with pe.Fori(0, 2) as it:
                    base, hb = pe.snap(l * TURNS + it * 2), pe.snap(l * HALF_OUT + it)
                    for j in range(2):
                        q = turn(o0 + j, hb)
                        for half in range(2):
                            pe.wait_ge(S["actlo_ready"], l * 16 + (f0 + 4 * half + 6))
                            hs = slice(8 * half, 8 * half + 8)
                            for m in range(2):
                                feature_block(base, b0 + 4 * j + 2 * half + m, PS[:, q + m, 0:T],
                                              act_hi[hs], act_lo[hs],
                                              first=half == 0, last=half == 1)

            def normed(l, m):
                return lambda k: pe.wait_ge(S["hlo_ready"], l * (3 * KB) + (m * KB + k + 1))

            pe.sem_inc(S["block_done"], RING)
            with pe.Fori(0, DEPTH) as l:
                lb, lh = pe.snap(l * TURNS), pe.snap(l * HALF_OUT)
                l1 = pe.snap(l + 1)
                ffn_in(l, B_F1, O_F1, 0, l * 16 + 5)
                total(BANK_MEM, l * 16 + 9, "mem_ssq")
                ffn_out(l, B_F2, O_F2, 0)
                pe.wait_ge(S["memlo_ready"], l * 4 + 4)
                for c in range(2):
                    feature_pair(lb, B_MEM + 2 * c, O_MEM + c, lh, m_hi, m_lo)
                    if c == 0:
                        total(BANK_NORM, l * 16 + 13, "ssq_ready")
                pe.wait_ge(S["rounded_ready"], 2)
                for c in range(2, 4):
                    token_pair(lb, B_MEM + 2 * c, O_MEM + c, lh, m_hi, m_lo)
                    if c == 3:
                        split_sums(4, sq_place[0], 1, l, "memk_ssq")
                for c in range(2):
                    feature_pair(lb, B_LAT + 2 * c, O_LAT + c, lh, each=normed(l, 1) if c == 0 else None)
                for c in range(4):
                    feature_pair(lb, B_CONV + 2 * c, O_CONV + c, lh)
                    if c == 0:
                        pe.wait_ge(S["lat_sq_all"], l1)
                        MM(PS[:, BANK_MLA, :], ones, latsq[:, 0:3:2, :], start=True, stop=True)\
                            .then_inc(S["lat_ssq"], 1)
                arrived(lb, B_UP)
                pe.wait_ge(S["widehi_ready"], l1)
                pe.wait_ge(S["widelo_ready"], l1)

                def twice(w, run):
                    return w[:, :, :].rearrange("p k n -> p (k n)")[:, run * P:(run + 1) * P]

                for kb in range(KB):
                    ins = split(PS[:, BANK_NORM, 0:T], twice(acthi, kb), twice(actlo, kb),
                                h_hi[kb], h_lo[kb], kb == 0, kb == KB - 1)
                ins.then_inc(S["kr_ready"], 1)
                pe.wait_ge(S["latlo_ready"], l1)
                for c in range(3):
                    q = turn(O_UP + c, lh)
                    if c:
                        arrived(lb, B_UP + c)
                    s, lat0 = (B_UP + c) % RING, 0 if c < 2 else 2
                    for h in range(HEADS):
                        for kb in range(2):
                            place = (h * 2 + kb) * P
                            if c == 0:
                                w = [twice(t, KB + h * 2 + kb) for t in (acthi, actlo)]
                            else:
                                w = [t[:, s, place:place + P] for t in (whi, wlo)]
                            ins = split(PS[:, q + h // 2, (h % 2) * T:(h % 2 + 1) * T], w[0], w[1],
                                        lathi[:, lat0 + kb, :], latlo[:, lat0 + kb, :], kb == 0, kb == 1)
                    ins.then_inc(S["block_done"], 1)
                    if c == 1:
                        pe.wait_ge(S["krg_ready"], l1)
                        MM(PS[:, BANK_NORM, 0:T], permA, krg, start=True, stop=True)
                        MM(PS[:, BANK_NORM, T:2 * T], permB, krg, start=True, stop=True).then_inc(S["kr_permuted"], 1)
                q = turn(O_UP + 3, lh)
                arrived(lb, B_UP + 3)
                s = (B_UP + 3) % RING
                for t in range(2):
                    tt = slice(t * P, (t + 1) * P)
                    for kb in range(2):
                        w = slice(kb * 512, (kb + 1) * 512)
                        out = PS[:, q + t, :]
                        MM(out, lathi[:, 2 + kb, tt], whi[:, s, w], start=kb == 0, stop=False)
                        MM(out, lathi[:, 2 + kb, tt], wlo[:, s, w], start=False, stop=False)
                        ins = MM(out, latlo[:, 2 + kb, tt], whi[:, s, w], start=False, stop=kb == 1)
                ins.then_inc(S["block_done"], 1)
                for c in range(4):
                    feature_pair(lb, B_SBQ + 2 * c, O_SBQ + c, lh)
                    if c == 1:
                        split_sums(4, sq_place[0], 2, l, "mq_ssq")
                    if c == 2:
                        pe.wait_ge(S["krt_ready"], l * 2 + 2)
                        split_sums(6, sq_place[1], 3, l, "mk_ssq")
                for c in range(2):
                    feature_pair(lb, B_MEMQ + 2 * c, O_MEMQ + c, lh)
                    if c == 0:
                        split_sums(4, sq_place[0], 4, l, "sbq_ssq")
                    else:
                        split_sums(6, sq_place[1], 5, l, "sbk_ssq")
                for c in range(2):
                    token_pair(lb, B_SBV + 2 * c, O_SBV + c, lh, h_hi, h_lo)
                    if c == 0:
                        pe.wait_ge(S["eq_sq"], l1)
                        head_sums(4, eqsq, "eq_ssq")
                with pe.Fori(0, HEADS) as i:
                    n1 = pe.snap(l * HEADS + i + 1)
                    base, hb = pe.snap(l * TURNS + i * 2), pe.snap(l * HALF_OUT + i * 2)

                    def weighted(bank, v0, w):
                        MM(PS[:, bank, 0:T], vh[:, v0, :], w[:, 0:T], start=True, stop=False)
                        return MM(PS[:, bank, P:T], vh[:, v0 + 1, :], w[:, T:384], start=False, stop=True)

                    feature_pair(base, B_GATE, O_GATE, hb)
                    for s in ("sbq_normed", "sbk_normed", "eq_normed", "memk_normed"):
                        pe.wait_ge(S[s], l1)
                    pe.wait_ge(S["mk_normed"], l * 2 + 2)
                    pe.wait_ge(S["fixed_ready"], n1 * 4)
                    pe.wait_ge(S["sb_lo"], n1)
                    pe.wait_ge(S["mla_lo"], n1)
                    pe.wait_ge(S["e_lo"], n1)
                    MM(PS[:, BANK_SB, 0:T], sbk[:, 0:P], hf[:, i, :], start=True, stop=True)
                    MM(PS[:, BANK_SB, T:384], sbk[:, P:T], hf[:, i, P:T], start=True, stop=True).then_inc(S["sb_z"], 1)
                    MM(PS[:, BANK_MLA, 0:P], mq[:, 0:P], mlaqk[:, 2, i, 0:P], start=True, stop=False)
                    MM(PS[:, BANK_MLA, 0:P], mqr[:, 0:P], mlaqk[:, 3, i, 0:P], start=False, stop=True)
                    MM(PS[:, BANK_MLA, P:384], mq[:, P:T], mlaqk[:, 2, i, :], start=True, stop=False)
                    MM(PS[:, BANK_MLA, P:384], mqr[:, P:T], mlaqk[:, 3, i, :], start=False, stop=True)\
                        .then_inc(S["mla_s"], 1)
                    for t in range(2):
                        ins = MM(PS[:, BANK_MEM, t * T:(t + 1) * T], eq[:, t * P:(t + 1) * P], memk[:, i, :],
                                 start=True, stop=True)
                    ins.then_inc(S["e_s"], 1)
                    feature_pair(base, B_GATE + 2, O_GATE + 1, hb)
                    feature_pair(base, B_GATE + 4, O_GATE + 2, hb)
                    pe.wait_ge(S["sb_lkl"], n1)
                    MM(PS[:, BANK_SB, 0:384], later_r, lkh, start=True, stop=False)
                    MM(PS[:, BANK_SB, 0:384], later_r, lkl, start=False, stop=False)
                    MM(PS[:, BANK_SB, P:T], ones_r, lkh[:, T:384], start=False, stop=False)
                    MM(PS[:, BANK_SB, P:T], ones_r, lkl[:, T:384], start=False, stop=True).then_inc(S["sb_later"], 1)
                    pe.wait_ge(S["mla_pn"], n1 * 2)
                    for k in range(3):
                        ins = nc.tensor.transpose(PS[:, BANK_MLA, k * P:(k + 1) * P], mP[:, k * P:(k + 1) * P], ident)
                    ins.then_inc(S["mla_transposed"], 1)
                    pe.wait_ge(S["e_pn"], n1 * 2)
                    for k in range(2):
                        for t in range(2):
                            ins = nc.tensor.transpose(PS[:, BANK_MEM, (2 * k + t) * P:(2 * k + t + 1) * P],
                                                      eP[:, (2 * t + k) * P:(2 * t + k + 1) * P], ident)
                    ins.then_inc(S["e_transposed"], 1)
                    feature_pair(base, B_GATE + 6, O_GATE + 3, hb)
                    pe.wait_ge(S["vh_ready"], n1)
                    pe.wait_ge(S["mla_PT"], n1)
                    weighted(BANK_MLA, 2, mPT).then_inc(S["mla_pv"], 1)
                    pe.wait_ge(S["e_PT"], n1)
                    MM(PS[:, BANK_MEM, 0:T], vh[:, 4, :], ePT[:, 0:T], start=True, stop=False)
                    MM(PS[:, BANK_MEM, 0:T], vh[:, 5, :], ePT[:, T:2 * T], start=False, stop=True)\
                        .then_inc(S["e_pv"], 1)
                    pe.wait_ge(S["sb_w"], n1)
                    weighted(BANK_SB, 0, lw).then_inc(S["sb_pv"], 1)
                for u in range(2):
                    j0 = 2 - 2 * u
                    if u == 1:
                        pe.wait_ge(S["sb_lo"], l * 4 + 5)
                        pe.wait_ge(S["b0lo_ready"], l1)
                    for c in range(4):
                        o = O_BRANCH + 4 * u + c
                        q = turn(o, lh)
                        for m in range(2):
                            b = B_BRANCH + 8 * u + 2 * c + m
                            arrived(lb, b)
                            for s in range(2):
                                for kb in range(4):
                                    if u == c == m == 0 and kb == 3:
                                        pe.wait_ge(S[("mla_lo", "e_lo")[s]], l * 4 + 5)
                                    w = slice((4 * s + kb) * P, (4 * s + kb + 1) * P)
                                    ins = split(PS[:, q + m, s * T:(s + 1) * T],
                                                whi[:, b % RING, w], wlo[:, b % RING, w],
                                                bhi[j0 + s][:, kb, :], blo[j0 + s][:, kb, :], kb == 0, kb == 3)
                            ins.then_inc(S["block_done"], 1)
                        if u == 0 and c == 0:
                            pe.wait_ge(S["y_paired"], l1)
                            for k in range(2):
                                ins = MM(PS[:, BANK_NORM, 0:T], ones, ysum[:, k, :], start=k == 0, stop=k == 1)
                            ins.then_inc(S["ln_mean"], 1)
                        if u == 0 and c == 1:
                            pe.wait_ge(S["ysq_paired"], l1)
                            for k in range(2):
                                ins = MM(PS[:, BANK_NORM, 0:T], ones, ysum[:, k, :], start=k == 0, stop=k == 1)
                            ins.then_inc(S["ln_var"], 1)
                q = turn(O_OUT, lh)
                for ks in (range(6), range(6, 8)):
                    for m in range(2):
                        arrived(lb, B_OUT + m)
                        for k in ks:
                            pe.wait_ge(S["mergedlo_ready"], l * 4 + (k // 2 + 1))
                            w = slice(k * P, (k + 1) * P)
                            ins = split(PS[:, q + m, 0:T],
                                        whi[:, (B_OUT + m) % RING, w], wlo[:, (B_OUT + m) % RING, w],
                                        m_hi[k], m_lo[k], k == 0, k == KB - 1)
                        if k == KB - 1:
                            ins.then_inc(S["block_done"], 1)
                for c in range(1, 4):
                    feature_pair(lb, B_OUT + 2 * c, O_OUT + c, lh, m_hi, m_lo)
                ffn_in(l, B_G1, O_G1, 2, l * 16 + 17)
                ffn_out(l, B_G2, O_G2, 8)


def _features(w, cols):
    return [w[:, c:c + P].reshape(-1, P, P).transpose(1, 0, 2).reshape(P, BLK) for c in cols]


def _tokens(w, cols):
    return [w[r:r + 512, c:c + 256].reshape(4, P, 256).transpose(1, 0, 2).reshape(P, BLK)
            for c in cols for r in (0, 512)]


def _ffn(w_in, w_out):
    cols = [half + c + m for c in range(0, FFN, 256) for half in (0, FFN) for m in (0, P)]
    out = _features(w_in, cols)
    for c in range(0, D_MODEL, 256):
        for rows in (0, 1024):
            out += _features(w_out[rows:rows + 1024], (c, c + P))
    return out


def _small(w, picks):
    blocks = w.reshape(-1, P, w.shape[1])
    return np.concatenate([b[:, c:c + n] for c, n in picks for b in blocks], axis=1)


def _layer_stream(l, a):
    w = a["w_in"][l]
    conv, sbq, sbv = 0, 1024, 1024 + 2 * 512
    qlat = 1024 + 3 * 512
    kr, memq = qlat + 2 * LORA, qlat + 2 * LORA + ROPE
    gate = memq + 512
    kv = a["mem_w_kv"][l]
    out = _ffn(a["ffn1_w_in"][l], a["ffn1_w_out"][l])
    out += _features(kv, range(0, 512, P)) + _tokens(kv, (512, 768))
    out += _features(w, range(qlat, qlat + 512, P))
    out += _features(w, [conv + c + part + m for c in (0, 256) for part in (0, CONV_CH) for m in (0, P)])
    uq, ukv, hd = a["mla_w_uq"][l], a["mla_w_ukv"][l], HEAD_DIM
    krw = w[:, kr:kr + ROPE].reshape(KB, P, ROPE).transpose(1, 0, 2).reshape(P, KB * ROPE)
    out.append(np.concatenate([krw, _small(uq, [(h * (hd + ROPE) + hd, ROPE) for h in range(HEADS)])], axis=1))
    out.append(_small(uq, [(h * (hd + ROPE), hd) for h in range(HEADS)]))
    out.append(_small(ukv, [(h * 2 * hd, hd) for h in range(HEADS)]))
    v = ukv.reshape(2, P, HEADS, 2, hd)[:, :, :, 1, :].reshape(2, P, HEADS * hd)
    out.append(v.transpose(1, 0, 2).reshape(P, BLK))
    out += _features(w, range(sbq, sbq + 1024, P)) + _features(w, range(memq, memq + 512, P))
    out += _tokens(w, (sbv, sbv + 256))
    out += _features(w, range(gate, gate + N_BRANCH * D_MODEL, P))
    wb = a["w_branch"][l].reshape(N_BRANCH * 512, D_MODEL)
    out += _features(wb[1024:], range(0, D_MODEL, P)) + _features(wb[:1024], range(0, D_MODEL, P))
    out += _features(a["w_out"][l], range(0, D_MODEL, P))
    return out + _ffn(a["ffn2_w_in"][l], a["ffn2_w_out"][l])


def _layer_params(l, a):
    def col(v):
        return v.reshape(-1, P).T

    def rope(v):
        return np.concatenate([v[HEAD_DIM:], v[HEAD_DIM:]]).reshape(1, P).T

    conv = [np.concatenate([a["conv_dw"][l][:, k * P:(k + 1) * P].T, a["conv_b"][l][k * P:(k + 1) * P, None]], axis=1)
            for k in range(4)]
    mq, mk = a["mla_q_hnorm"][l], a["mla_k_hnorm"][l]
    return np.concatenate(
        [col(a[n][l]) for n in ("ffn1_norm", "mix_norm", "ffn2_norm", "mem_norm")] + conv
        + [col(a[n][l]) for n in ("conv_ln_g", "conv_ln_b", "sb_q_hnorm", "sb_k_hnorm", "mla_q_norm", "mla_kv_norm")]
        + [col(mq[:HEAD_DIM]), rope(mq), col(mk[:HEAD_DIM]), rope(mk)]
        + [col(a[n][l]) for n in ("mem_q_hnorm", "mem_k_hnorm")] + [col(a["ffn1_norm"][(l + 1) % DEPTH])], axis=1)


def _constants():
    r = np.arange(P)
    quarter, j = r // 32, r % 32
    row_a, row_b = np.array([0, 1, 1, 0])[quarter] * 32 + j, np.array([1, 0, 0, 1])[quarter] * 32 + j
    freq = (ROPE_BASE ** (-np.arange(0, ROPE, 2) / ROPE)).astype(np.float32)
    cols = [np.array(c, np.float64)[quarter][:, None] for c in ([1, 1, 0, 0], [0, 0, 1, -1], [-1, 1, 1, -1])]
    return np.concatenate(
        [np.ones((P, P)), r[:, None] > r[None, :], np.eye(P), r[:, None] < r[None, :],
         r[:, None] == row_a[None, :], r[:, None] == row_b[None, :],
         np.full((P, 1), EPS), np.ones((P, 1)), freq[j][:, None]] + cols, axis=1).astype(np.float32)


def kernel(**inputs):
    import concourse.bacc as bacc
    from concourse.bass_utils import run_bass_kernel_spmd as run

    a = {n: np.asarray(v) for n, v in inputs.items()}
    blocks = [b for l in range(DEPTH) for b in _layer_stream(l, a)]
    arrays = {
        "stream": np.stack(blocks + blocks[:AHEAD]),
        "xT": np.ascontiguousarray(a["x"][0].T),
        "memT": np.ascontiguousarray(a["mem"][0].T),
        "positions": np.ascontiguousarray(a["positions"]),
        "params": np.stack([_layer_params(l, a) for l in range(DEPTH)]),
        "consts": _constants(),
    }
    nc = bacc.Bacc("TRN2", target_bir_lowering=False, num_devices=1)
    args = [nc.dram_tensor(n, v.shape, mybir.dt.from_np(v.dtype), kind="ExternalInput").ap() for n, v in arrays.items()]
    args.append(nc.dram_tensor("outT", (D_MODEL, SEQ), mybir.dt.float32, kind="ExternalOutput").ap())
    build(nc, *args)
    r = run(nc, [arrays], core_ids=[0])
    return np.ascontiguousarray(r.results[0]["outT"].T).reshape(1, SEQ, D_MODEL)
```
